# Optimizing a Trainium2 kernel written in Bass

```python
import math
import numpy as np
import jax
import jax.numpy as jnp
from jax import lax

D_MODEL = 1024
BATCH = 1
SEQ = 512
DEPTH = 1

CHUNK = 64
EPS = 1e-6
ADA_PARTS = 6

M_HEADS = 4
M_HEAD_DIM = 256
M_WIDTH = M_HEADS * M_HEAD_DIM
CONV_WIDTH = 4
F_BIAS_LO = 3.0
F_BIAS_HI = 6.0

D_HEADS = 4
D_QK_DIM = 128
D_V_DIM = 2 * D_QK_DIM
D_QK_WIDTH = D_HEADS * 2 * D_QK_DIM
D_V_WIDTH = D_HEADS * D_V_DIM
Q_BLOCK = 128

IN_WIDTH = 2 * M_WIDTH + M_WIDTH + M_WIDTH + 2 * M_HEADS + 2 * D_QK_WIDTH + D_V_WIDTH + 2 * D_MODEL

P_HEADS = 8
N_KEYS = 128
N_EXPERTS = N_KEYS * N_KEYS
P_TOPK = 16
P_QUERY_DIM = 256
P_HALF = P_QUERY_DIM // 2
P_TOKEN_BLOCK = 128

kernel_name = "hybrid_mlstm_diffattn_peer_block"

def rms_norm(x, gain):
    xf = x.astype(jnp.float32)
    y = xf * lax.rsqrt(jnp.mean(xf * xf, axis=-1, keepdims=True) + EPS)
    return (y * gain.astype(jnp.float32)).astype(x.dtype)

def lambda_init(layer):
    return 0.8 - 0.6 * math.exp(-0.3 * layer)

def causal_depthwise_conv(x, w, b):
    y = lax.conv_general_dilated(
        x, w[:, None, :].astype(x.dtype), window_strides=(1,),
        padding=[(CONV_WIDTH - 1, 0)], dimension_numbers=("NWC", "WIO", "NWC"),
        feature_group_count=x.shape[-1])
    return y + b.astype(x.dtype)

def mlstm_chunkwise(q, k, v, log_i, log_f):
    B, H, S, Dh = q.shape
    nc = S // CHUNK

    def to_chunks(t):
        return jnp.moveaxis(t.reshape(B, H, nc, CHUNK, *t.shape[3:]), 2, 0)

    causal = jnp.tril(jnp.ones((CHUNK, CHUNK), dtype=bool))

    def step(carry, inp):
        C, n, m = carry
        qb, kb, vb, lib, lfb = inp
        b = jnp.cumsum(lfb, axis=-1)
        a = b + m[..., None]
        d = jnp.where(causal, b[..., :, None] - b[..., None, :] + lib[..., None, :], -jnp.inf)
        m_t = jnp.maximum(a, jnp.max(d, axis=-1))
        w_inter = jnp.exp(a - m_t)
        s = jnp.einsum("bhtd,bhsd->bhts", qb, kb) * jnp.exp(d - m_t[..., None])
        num = jnp.einsum("bhts,bhsd->bhtd", s, vb) + w_inter[..., None] * jnp.einsum("bhvk,bhtk->bhtv", C, qb)
        den = jnp.sum(s, axis=-1) + w_inter * jnp.einsum("bhk,bhtk->bht", n, qb)
        h = num / jnp.maximum(jnp.abs(den), jnp.exp(-m_t))[..., None]
        m_new = m_t[..., -1]
        g_prev = jnp.exp(b[..., -1] + m - m_new)
        g_s = jnp.exp(b[..., -1:] - b + lib - m_new[..., None])
        C_new = g_prev[..., None, None] * C + jnp.einsum("bhs,bhsv,bhsk->bhvk", g_s, vb, kb)
        n_new = g_prev[..., None] * n + jnp.einsum("bhs,bhsk->bhk", g_s, kb)
        return (C_new, n_new, m_new), h

    init = (jnp.zeros((B, H, Dh, Dh), jnp.float32),
            jnp.zeros((B, H, Dh), jnp.float32),
            jnp.zeros((B, H), jnp.float32))
    xs = (to_chunks(q), to_chunks(k), to_chunks(v), to_chunks(log_i), to_chunks(log_f))
    _, hs = lax.scan(step, init, xs)
    return jnp.moveaxis(hs, 0, 2).reshape(B, H, S, Dh)

def diff_attention(q, k, v, lam):
    B, S, H, _, dqk = q.shape
    nqb = S // Q_BLOCK
    scale = dqk ** -0.5
    key_chunk = jnp.arange(S) // CHUNK
    q_blocks = jnp.moveaxis(q.reshape(B, nqb, Q_BLOCK, H, 2, dqk), 1, 0)

    def block(args):
        qb, blk = args
        q_chunk = (blk * Q_BLOCK + jnp.arange(Q_BLOCK)) // CHUNK
        mask = key_chunk[None, :] <= q_chunk[:, None]
        s = jnp.einsum("bqhcd,bkhcd->bhcqk", qb, k).astype(jnp.float32) * scale
        p = jax.nn.softmax(jnp.where(mask, s, -jnp.inf), axis=-1)
        a = p[:, :, 0] - lam * p[:, :, 1]
        return jnp.einsum("bhqk,bkhd->bqhd", a.astype(v.dtype), v)

    out = lax.map(block, (q_blocks, jnp.arange(nqb)))
    return jnp.moveaxis(out, 0, 1).reshape(B, S, H, v.shape[-1])

def hybrid_mixer(h, lam_init, w_in, b_if, conv_w, conv_b, m_head_gain, lam_q1, lam_k1, lam_q2, lam_k2,
                 d_head_gain, w_br_m, w_br_d, w_out):
    B, S, _ = h.shape
    proj = h @ w_in
    sizes = (2 * M_WIDTH, M_WIDTH, M_WIDTH, 2 * M_HEADS, D_QK_WIDTH, D_QK_WIDTH, D_V_WIDTH, D_MODEL, D_MODEL)
    m_qk, m_v, m_o, m_if, d_q, d_k, d_v, g_m, g_d = jnp.split(proj, np.cumsum(sizes)[:-1].tolist(), axis=-1)

    m_qk = jax.nn.silu(causal_depthwise_conv(m_qk, conv_w, conv_b))
    mq, mk = jnp.split(m_qk, 2, axis=-1)

    def heads(t):
        return t.reshape(B, S, M_HEADS, M_HEAD_DIM).transpose(0, 2, 1, 3).astype(jnp.float32)

    gate_pre = (m_if + b_if).astype(jnp.float32).transpose(0, 2, 1)
    log_i = gate_pre[:, :M_HEADS]
    log_f = jax.nn.log_sigmoid(gate_pre[:, M_HEADS:])
    cell = mlstm_chunkwise(heads(mq), heads(mk) * (M_HEAD_DIM ** -0.5), heads(m_v), log_i, log_f)
    cell = cell.transpose(0, 2, 1, 3).astype(h.dtype)
    y_m = rms_norm(cell, m_head_gain.reshape(M_HEADS, M_HEAD_DIM)).reshape(B, S, M_WIDTH) * jax.nn.sigmoid(m_o)

    f32 = jnp.float32
    lam = (jnp.exp(jnp.sum(lam_q1.astype(f32) * lam_k1.astype(f32)))
           - jnp.exp(jnp.sum(lam_q2.astype(f32) * lam_k2.astype(f32))) + lam_init)
    att = diff_attention(d_q.reshape(B, S, D_HEADS, 2, D_QK_DIM),
                         d_k.reshape(B, S, D_HEADS, 2, D_QK_DIM),
                         d_v.reshape(B, S, D_HEADS, D_V_DIM), lam)
    y_d = rms_norm(att, d_head_gain.reshape(D_HEADS, D_V_DIM)).reshape(B, S, D_V_WIDTH) * (1.0 - lam_init)

    merged = jax.nn.sigmoid(g_m) * (y_m @ w_br_m) + jax.nn.sigmoid(g_d) * (y_d @ w_br_d)
    return merged @ w_out

def peer_ffn(h, w_query, sub_keys, expert_u, expert_v):
    T, D = h.shape
    qry = (h @ w_query).reshape(T, P_HEADS, 2, P_HALF)
    scores = jnp.einsum("thcd,hcnd->thcn", qry, sub_keys).astype(jnp.float32)
    s_top, i_top = lax.top_k(scores, P_TOPK)
    cand_s = (s_top[:, :, 0, :, None] + s_top[:, :, 1, None, :]).reshape(T, P_HEADS, P_TOPK * P_TOPK)
    cand_i = (i_top[:, :, 0, :, None] * N_KEYS + i_top[:, :, 1, None, :]).reshape(T, P_HEADS, P_TOPK * P_TOPK)
    best_s, best_pos = lax.top_k(cand_s, P_TOPK)
    expert_idx = jnp.take_along_axis(cand_i, best_pos, axis=-1)
    gates = jax.nn.softmax(best_s, axis=-1).astype(h.dtype)
    nb = T // P_TOKEN_BLOCK

    def block(args):
        hb, eb, gb = args
        act = jax.nn.gelu(jnp.einsum("td,thkd->thk", hb, expert_u[eb]), approximate=False)
        return jnp.einsum("thk,thkd->td", act * gb, expert_v[eb])

    out = lax.map(block, (h.reshape(nb, P_TOKEN_BLOCK, D),
                          expert_idx.reshape(nb, P_TOKEN_BLOCK, P_HEADS, P_TOPK),
                          gates.reshape(nb, P_TOKEN_BLOCK, P_HEADS, P_TOPK)))
    return out.reshape(T, D)

def setup_inputs(seed: int = 0) -> dict:
    key = jax.random.key(seed)
    ks = jax.random.split(key, 26)
    f32 = jnp.float32

    def nrm(k, shape, scale):
        return jax.random.normal(k, shape, f32) * scale

    def gain(k, width):
        return 1.0 + nrm(k, (DEPTH, width), 0.05)

    f_bias = jnp.linspace(F_BIAS_LO, F_BIAS_HI, M_HEADS, dtype=f32)
    b_if = jnp.concatenate([nrm(ks[9], (DEPTH, M_HEADS), 0.1),
                            f_bias + nrm(ks[10], (DEPTH, M_HEADS), 0.1)], axis=-1)
    return {
        "x": nrm(ks[0], (BATCH, SEQ, D_MODEL), 1.0),
        "c": nrm(ks[1], (BATCH, D_MODEL), 1.0),
        "w_ada": nrm(ks[2], (DEPTH, D_MODEL, ADA_PARTS * D_MODEL), 0.5 * D_MODEL ** -0.5),
        "b_ada": nrm(ks[3], (DEPTH, ADA_PARTS * D_MODEL), 0.01),
        "g_pre_mix": gain(ks[4], D_MODEL),
        "g_post_mix": gain(ks[5], D_MODEL),
        "g_pre_ffn": gain(ks[6], D_MODEL),
        "g_post_ffn": gain(ks[7], D_MODEL),
        "w_in": nrm(ks[8], (DEPTH, D_MODEL, IN_WIDTH), D_MODEL ** -0.5),
        "b_if": b_if,
        "conv_w": nrm(ks[11], (DEPTH, CONV_WIDTH, 2 * M_WIDTH), CONV_WIDTH ** -0.5),
        "conv_b": nrm(ks[12], (DEPTH, 2 * M_WIDTH), 0.01),
        "m_head_gain": gain(ks[13], M_WIDTH),
        "lam_q1": nrm(ks[14], (DEPTH, D_QK_DIM), 0.1),
        "lam_k1": nrm(ks[15], (DEPTH, D_QK_DIM), 0.1),
        "lam_q2": nrm(ks[16], (DEPTH, D_QK_DIM), 0.1),
        "lam_k2": nrm(ks[17], (DEPTH, D_QK_DIM), 0.1),
        "d_head_gain": gain(ks[18], D_V_WIDTH),
        "w_br_m": nrm(ks[19], (DEPTH, M_WIDTH, D_MODEL), M_WIDTH ** -0.5),
        "w_br_d": nrm(ks[20], (DEPTH, D_V_WIDTH, D_MODEL), D_V_WIDTH ** -0.5),
        "w_out": nrm(ks[21], (DEPTH, D_MODEL, D_MODEL), D_MODEL ** -0.5),
        "w_query": nrm(ks[22], (DEPTH, D_MODEL, P_HEADS * P_QUERY_DIM), D_MODEL ** -0.5),
        "sub_keys": nrm(ks[23], (DEPTH, P_HEADS, 2, N_KEYS, P_HALF), P_HALF ** -0.5),
        "expert_u": nrm(ks[24], (DEPTH, N_EXPERTS, D_MODEL), D_MODEL ** -0.5),
        "expert_v": nrm(ks[25], (DEPTH, N_EXPERTS, D_MODEL), (P_HEADS * P_TOPK) ** -0.5),
    }

def reference(x, c, w_ada, b_ada, g_pre_mix, g_post_mix, g_pre_ffn, g_post_ffn, w_in, b_if, conv_w, conv_b,
              m_head_gain, lam_q1, lam_k1, lam_q2, lam_k2, d_head_gain, w_br_m, w_br_d, w_out,
              w_query, sub_keys, expert_u, expert_v):
    B, S, D = x.shape
    for l in range(DEPTH):
        ada = (jax.nn.silu(c) @ w_ada[l] + b_ada[l])[:, None, :]
        shift1, scale1, gate1, shift2, scale2, gate2 = jnp.split(ada, ADA_PARTS, axis=-1)
        h = rms_norm(x, g_pre_mix[l]) * (1.0 + scale1) + shift1
        y = hybrid_mixer(h, lambda_init(l), w_in[l], b_if[l], conv_w[l], conv_b[l], m_head_gain[l],
                         lam_q1[l], lam_k1[l], lam_q2[l], lam_k2[l], d_head_gain[l],
                         w_br_m[l], w_br_d[l], w_out[l])
        x = x + gate1 * rms_norm(y, g_post_mix[l])
        h = rms_norm(x, g_pre_ffn[l]) * (1.0 + scale2) + shift2
        y = peer_ffn(h.reshape(B * S, D), w_query[l], sub_keys[l], expert_u[l], expert_v[l]).reshape(B, S, D)
        x = x + gate2 * rms_norm(y, g_post_ffn[l])
    return x


_drawn_inputs = setup_inputs


def setup_inputs(seed=0):
    import zlib

    import numpy as np

    out = dict(_drawn_inputs(seed))
    spreads = {}
    factors = {'g_post_ffn': 4.135, 'conv_b': 7.845}
    for name, (base, spread) in spreads.items():
        noise = np.random.default_rng([zlib.crc32(name.encode()), seed]).standard_normal(out[name].shape)
        drawn = base * np.exp(spread * noise) if base else spread * noise
        out[name] = jnp.asarray(drawn.astype(out[name].dtype))
    for name, factor in factors.items():
        out[name] = (out[name] * factor).astype(out[name].dtype)
    return out
```

```python
import math
from contextlib import ExitStack

import numpy as np

import concourse.bass as bass
from concourse import mybir

F32 = mybir.dt.float32
F32R = mybir.dt.float32r
U32 = mybir.dt.uint32
ALU = mybir.AluOpType
ACT = mybir.ActivationFunctionType
AX_X = mybir.AxisListType.X

P = 128
D = 1024
T = 512
KD = D // P
NT = T // P
EPS = 1e-6
HEADS = 4
DH = 256
DQK = 128
CHUNK = 64
CONV = 4
PH = 8
NK = 128
TOPK = 16
HALVES = 2
GC = 256
LAM_INIT = 0.8 - 0.6 * math.exp(-0.3 * 0)
NEG = -3.0e38

C_QK, C_MV, C_MO, C_IF = 0, 2 * D, 3 * D, 4 * D
C_DQ = C_IF + 2 * HEADS
C_DV, C_GM, C_GD = C_DQ + 2 * D, C_DQ + 3 * D, C_DQ + 4 * D

R_BADA, R_GPREMIX, R_GPOSTMIX, R_GPREFFN, R_GPOSTFFN, R_CONVB, R_C, NROWS_A = 0, 48, 56, 64, 72, 80, 96, 104
R_CONVW, R_MGAIN, R_DGAIN, NROWS_B = 0, 64, 72, 80


def wait(eng, sem, value):
    if isinstance(value, int) and value <= 0:
        return
    eng.wait_ge(sem, value)


def pairs(eng, count, peel, peel_last=False):
    first, end = int(peel), count - int(peel_last)
    if peel:
        yield 0
    if end == first + 1:
        yield first
    elif end > first:
        with eng.Fori(first, end) as it:
            yield it
    if peel_last and count > first:
        yield count - 1


def settled(eng, value):
    return value if isinstance(value, int) else eng.snap(value)


class Alloc:
    sems = []

    def __init__(self, nc, tag):
        self.nc, self.tag, self.stack = nc, tag, ExitStack()

    def __enter__(self):
        self.stack.__enter__()
        return self

    def __exit__(self, *a):
        return self.stack.__exit__(*a)

    def sb(self, name, shape, dt=F32):
        return self.stack.enter_context(self.nc.sbuf_tensor(f"{self.tag}_{name}", shape, dt))

    def ps(self, name, shape, dt=F32):
        return self.stack.enter_context(self.nc.psum_tensor(f"{self.tag}_{name}", shape, dt))

    def sem(self, name):
        Alloc.sems.append(self.nc.alloc_semaphore(f"{self.tag}_{name}"))
        return Alloc.sems[-1]

    def block(self):
        return self.stack.enter_context(self.nc.Block())


def recycle_semaphores(nc):
    nc.clear_and_free_semaphores(Alloc.sems)
    nc.all_engine_barrier()
    Alloc.sems = []


def as_f32(ap):
    return ap.bitcast(F32)


def columns(w, k=KD):
    return w.rearrange("(k p) n -> p k n", p=P)


def adaln_block(nc, con, A):
    with Alloc(nc, "ada") as al:
        rows_a = al.sb("rows_a", [NROWS_A, P])
        rows_b = al.sb("rows_b", [NROWS_B, P])
        silu_c = al.sb("silu_c", [P, KD])
        sq = al.sb("sq", [P, 2])
        esum = al.sb("esum", [P, 2])
        ndma = 6 * D // GC
        raw = al.sb("raw", [P, 4, KD, GC])
        ps_t = al.ps("ps_t", [P, 512])
        ps_u = al.ps("ps_u", [P, 512])
        ps_ada = al.ps("ps_ada", [P, 512])
        ps_l = al.ps("ps_l", [P, 512])
        rows_in, consts, turned, cols_ready, silu_ready = map(
            al.sem, ("rows_in", "consts", "turned", "cols_ready", "silu_ready"))
        landed = [al.sem(f"landed{i}") for i in range(4)]
        used, ada_done, lam_in, lam_prod, lam_sum, lam_exp, chain = map(
            al.sem, ("used", "ada_done", "lam_in", "lam_prod", "lam_sum", "lam_exp", "chain"))
        w = columns(A["w_ada"][0])
        block = al.block()

        @block.sync
        def _(sp):
            def rows(dst, r, src, n):
                sp.dma_start(dst[r:r + n, :], src.rearrange("(r p) -> r p", p=P)).then_inc(rows_in, 16)

            rows(rows_a, R_BADA, A["b_ada"][0], 48)
            rows(rows_a, R_GPREMIX, A["g_pre_mix"][0], 8)
            rows(rows_a, R_GPOSTMIX, A["g_post_mix"][0], 8)
            rows(rows_a, R_GPREFFN, A["g_pre_ffn"][0], 8)
            rows(rows_a, R_GPOSTFFN, A["g_post_ffn"][0], 8)
            rows(rows_a, R_CONVB, A["conv_b"][0], 16)
            rows(rows_a, R_C, A["c"][0], 8)
            rows(rows_b, R_CONVW, A["conv_w"][0].rearrange("w c -> (w c)"), 64)
            rows(rows_b, R_MGAIN, A["m_head_gain"][0], 8)
            rows(rows_b, R_DGAIN, A["d_head_gain"][0], 8)
            for n, name in enumerate(("lam_q1", "lam_q2", "lam_k1", "lam_k2")):
                sp.dma_start(con.lam_cols[:, n:n + 1], A[name].rearrange("a p -> p a")).then_inc(lam_in, 16)
            for n in range(2):
                sp.dma_start(con.gate_bias[:, n:n + 1],
                             A["b_if"][:, n * HEADS:(n + 1) * HEADS].rearrange("a h -> h a")).then_inc(lam_in, 16)
            for it in pairs(sp, ndma // 4, True):
                for s in range(4):
                    col = settled(sp, (4 * it + s) * GC)
                    wait(sp, used, 4 * it + s - 3)
                    sp.dma_start(raw[:, s], w[:, :, bass.ds(col, GC)]).then_inc(landed[s], 16)

        @block.gpsimd
        def _(pool):
            pool.memset(con.ident[:], 0.0).then_inc(consts, 1)
            pool.memset(con.ones[:], 1.0).then_inc(consts, 1)
            pool.memset(con.pow_half[:], -0.5).then_inc(consts, 1)
            pool.memset(con.sel[:], 1.0).then_inc(consts, 1)
            pool.iota(con.iota[:], pattern=[[1, P]], base=0, channel_multiplier=0,
                      allow_small_or_imprecise_dtypes=True).then_inc(consts, 1)
            pool.wait_ge(consts, 5)
            pool.affine_select(out=con.ident[:], in_=con.ident[:], compare_op=ALU.not_equal, fill=1.0, base=0,
                               pattern=[[-1, P]], channel_multiplier=1).then_inc(consts, 1)
            pool.affine_select(out=con.sel[:], in_=con.sel[:], compare_op=ALU.is_equal, fill=0.0, base=0,
                               pattern=[[-1, HEADS], [0, P]], channel_multiplier=1).then_inc(consts, 1)

        @block.tensor
        def _(pe):
            pe.wait_ge(consts, 7)
            pe.wait_ge(rows_in, 160)
            pe.transpose(ps_t[:, 0:NROWS_A], rows_a[:], con.ident[0:NROWS_A, 0:NROWS_A])
            pe.transpose(ps_u[:, 0:NROWS_B], rows_b[:], con.ident[0:NROWS_B, 0:NROWS_B]).then_inc(turned, 1)
            pe.wait_ge(lam_prod, 1)
            pe.matmul(ps_l[:, 0:2], con.ones[:], sq[:], start=True, stop=True).then_inc(lam_sum, 1)
            pe.wait_ge(silu_ready, 1)
            for it in pairs(pe, ndma // 4, True):
                for s in range(4):
                    pe.wait_ge(landed[s], 16 * (it + 1))
                    for m in range(GC // P):
                        for k in range(KD):
                            mm = pe.matmul(ps_ada[:, bass.ds(2 * (4 * it + s) + m, 1)],
                                           raw[:, s, k, m * P:(m + 1) * P], silu_c[:, k:k + 1],
                                           start=(k == 0), stop=(k == KD - 1))
                    mm.then_inc(used, 1)

        @block.scalar
        def _(act):
            act.wait_ge(cols_ready, 1)
            act.activation(silu_c[:], con.cols_a[:, R_C:R_C + KD], ACT.Silu).then_inc(silu_ready, 1)
            act.wait_ge(lam_sum, 1)
            act.activation(esum[:], ps_l[:, 0:2], ACT.Exp).then_inc(lam_exp, 1)

        @block.vector
        def _(dve):
            n_chain = 0
            dve.wait_ge(turned, 1)
            dve.tensor_copy(con.cols_a[:], ps_t[:, 0:NROWS_A]).then_inc(cols_ready, 1)
            dve.tensor_copy(con.cols_b[:], ps_u[:, 0:NROWS_B]).then_inc(cols_ready, 1)
            dve.wait_ge(lam_in, 96)
            dve.tensor_tensor(sq[:], con.lam_cols[:, 0:2], con.lam_cols[:, 2:4], ALU.mult).then_inc(lam_prod, 1)
            dve.wait_ge(cols_ready, 2)
            dve.tensor_scalar(con.cols_b[:, R_DGAIN:R_DGAIN + KD], con.cols_b[:, R_DGAIN:R_DGAIN + KD],
                              1.0 - LAM_INIT, None, ALU.mult).then_inc(chain, 1)
            dve.wait_ge(lam_exp, 1)
            dve.scalar_tensor_tensor(out=con.lam[:], in0=esum[:, 0:1], scalar=LAM_INIT, in1=esum[:, 1:2],
                                     op0=ALU.add, op1=ALU.subtract).then_inc(chain, 1)
            dve.wait_ge(used, ndma)
            dve.tensor_tensor(con.ada[:], ps_ada[:, 0:48], con.cols_a[:, 0:48], ALU.add).then_inc(chain, 1)
            dve.wait_ge(chain, 3)
            for dst, gain, scale in ((con.scale_a, R_GPREMIX, 8), (con.scale_b, R_GPREFFN, 32)):
                dve.scalar_tensor_tensor(out=dst[:], in0=con.ada[:, scale:scale + 8], scalar=1.0,
                                         in1=con.cols_a[:, gain:gain + 8], op0=ALU.add,
                                         op1=ALU.mult).then_inc(chain, 1)
            for dst, gain, gate in ((con.gate_a, R_GPOSTMIX, 16), (con.gate_b, R_GPOSTFFN, 40)):
                dve.tensor_tensor(dst[:], con.ada[:, gate:gate + 8], con.cols_a[:, gain:gain + 8],
                                  ALU.mult).then_inc(chain, 1)


def modulate_block(nc, tag, con, x_src, hi, lo, scale, shift0):
    with Alloc(nc, tag) as al:
        in_dram = len(x_src.shape) == 2
        x = al.sb("x", [P, NT, D]) if in_dram else x_src
        xn = al.sb("xn", [P, NT, D])
        junk = al.sb("junk", [P, D])
        ss = al.sb("ss", [P, NT])
        ms = al.sb("ms", [P, NT])
        rstd = al.sb("rstd", [P, NT])
        h = al.sb("h", [P, 2, T])
        ps = [al.ps(f"ps{i}", [P, T]) for i in range(2)]
        x_in = [al.sem(f"x_in{i}") for i in range(NT)]
        summed, meaned, powed, normed, turned, modded, hi_done, lo_done = map(
            al.sem, ("summed", "meaned", "powed", "normed", "turned", "modded", "hi_done", "lo_done"))
        block = al.block()

        @block.sync
        def _(sp):
            if in_dram:
                for t in range(NT):
                    sp.dma_start(x[:, t], x_src[t * P:(t + 1) * P, :]).then_inc(x_in[t], 16)

        @block.scalar
        def _(act):
            for t in range(NT):
                if in_dram:
                    act.wait_ge(x_in[t], 16)
                if t:
                    act.wait_ge(summed, t)
                act.activation(junk[:], x[:, t], ACT.Square, accum_out=ss[:, t:t + 1]).then_inc(summed, 1)
            for k in range(KD):
                act.wait_ge(turned, k + 1)
                if k >= 2:
                    act.wait_ge(lo_done, k - 1)
                act.activation(h[:, k % 2], ps[k % 2][:], ACT.Identity, bias=con.ada[:, shift0 + k:shift0 + k + 1],
                               scale=scale[:, k:k + 1]).then_inc(modded, 1)

        @block.gpsimd
        def _(pool):
            pool.wait_ge(meaned, 1)
            pool.tensor_tensor(rstd[:], ms[:], con.pow_half[:, 0:NT], ALU.pow).then_inc(powed, 1)

        @block.vector
        def _(dve):
            dve.wait_ge(summed, NT)
            dve.tensor_scalar(ms[:], ss[:], 1.0 / D, EPS, ALU.mult, ALU.add).then_inc(meaned, 1)
            dve.wait_ge(powed, 1)
            for t in range(NT):
                dve.tensor_scalar(xn[:, t], x[:, t], rstd[:, t:t + 1], None, ALU.mult).then_inc(normed, 1)
            for k in range(KD):
                dve.wait_ge(modded, k + 1)
                dve.tensor_copy(hi[:, k], h[:, k % 2]).then_inc(hi_done, 1)
                dve.wait_ge(hi_done, k + 1)
                dve.tensor_tensor(lo[:, k], h[:, k % 2], as_f32(hi[:, k]), ALU.subtract).then_inc(lo_done, 1)

        @block.tensor
        def _(pe):
            pe.wait_ge(normed, NT)
            for k in range(KD):
                if k >= 2:
                    pe.wait_ge(modded, k - 1)
                for t in range(NT):
                    mm = pe.transpose(ps[k % 2][:, t * P:(t + 1) * P], xn[:, t, k * P:(k + 1) * P], con.ident[:])
                mm.then_inc(turned, 1)


def project_block(nc, tag, sections, make):
    with Alloc(nc, tag) as al:
        raw = [al.sb(f"raw{i}", [P, KD, GC]) for i in range(2)]
        whi = [al.sb(f"whi{i}", [P, KD, GC], F32R) for i in range(2)]
        wlo = [al.sb(f"wlo{i}", [P, KD, GC], F32R) for i in range(2)]
        bank = [al.ps(f"bank{i}", [P, 512]) for i in range(4)]
        landed = [al.sem(f"landed{i}") for i in range(2)]
        w_hi, w_lo, units = al.sem("w_hi"), al.sem("w_lo"), al.sem("units")
        freed = [al.sem(f"freed{i}") for i in range(4)]
        al.freed = freed
        empty_vector, empty_scalar = make(al)
        plan, g0, u0 = [], 0, 0
        for kind, groups, load, operand in sections:
            per = {"T": 2, "T1": 1, "N": 4}[kind]
            plan.append((kind, groups, load, operand, g0, u0, per))
            g0, u0 = g0 + groups, u0 + groups * per

        block = al.block()

        @block.sync
        def _(sp):
            for kind, groups, load, operand, gb, ub, per in plan:
                for it in range(groups // 2) if groups <= 8 else pairs(sp, groups // 2, gb == 0):
                    for s in range(2):
                        src = load(sp, it, s)
                        wait(sp, w_lo, gb + 2 * it + s - 1)
                        sp.dma_start(raw[s][:], src).then_inc(landed[s], 16)

        @block.gpsimd
        def _(pool):
            for kind, groups, load, operand, gb, ub, per in plan:
                for it in pairs(pool, groups // 2, False):
                    for s in range(2):
                        pool.wait_ge(w_hi, gb + 2 * it + s + 1)
                        pool.tensor_tensor(wlo[s][:], raw[s][:], as_f32(whi[s][:]), ALU.subtract).then_inc(w_lo, 1)

        @block.tensor
        def _(pe):
            for kind, groups, load, operand, gb, ub, per in plan:
                for it in pairs(pe, groups // 2, gb == 0):
                    for s in range(2):
                        pe.wait_ge(w_lo, gb + 2 * it + s + 1)
                        xh, xl = operand(s)
                        for c in range(per):
                            b = (s * per + c) % 4
                            use = (ub + s * per + c) // 4 + it * (2 * per // 4)
                            wait(pe, freed[b], use)
                            for k in range(KD):
                                if kind != "N":
                                    cs = slice(c * P, (c + 1) * P)
                                    ops = ((whi[s][:, k, cs], xh[:, k, :]), (whi[s][:, k, cs], xl[:, k, :]),
                                           (wlo[s][:, k, cs], xh[:, k, :]))
                                    out = bank[b][:]
                                else:
                                    ts = slice(c * P, (c + 1) * P)
                                    ops = ((xh[:, k, ts], whi[s][:, k, :]), (xh[:, k, ts], wlo[s][:, k, :]),
                                           (xl[:, k, ts], whi[s][:, k, :]))
                                    out = bank[b][:, 0:GC]
                                for n, (a, m) in enumerate(ops):
                                    mm = pe.matmul(out, a, m, start=(k == 0 and n == 0), stop=(k == KD - 1 and n == 2))
                            mm.then_inc(units, 1)

        def view(eng):
            for sec, (kind, groups, load, operand, gb, ub, per) in enumerate(plan):
                for it in pairs(eng, groups // 2, True, sec == len(plan) - 1):
                    for s in range(2):
                        first = ub + (2 * it + s) * per
                        last_group = isinstance(it, int) and gb + 2 * it + s + 1 == g0
                        if eng is nc.vector and not last_group:
                            o = 1 - s
                            eng.wait_ge(landed[o], 16 * (gb // 2 + it + s + 1))
                            wait(eng, units, first)
                            eng.tensor_copy(whi[o][:], raw[o][:]).then_inc(w_hi, 1)
                        for c in range(per):
                            b = (s * per + c) % 4
                            yield sec, it, s, c, first + c, bank[b], freed[b]

        @block.vector
        def _(dve):
            dve.wait_ge(landed[0], 16)
            dve.tensor_copy(whi[0][:], raw[0][:]).then_inc(w_hi, 1)
            empty_vector(dve, view(dve), units)

        @block.scalar
        def _(act):
            empty_scalar(act, view(act), units)


def w_group(w, col0, step=GC):
    v = columns(w)

    def load(sp, it, s):
        return v[:, :, bass.ds(settled(sp, col0 + it * 2 * GC + s * step), GC)]
    return load


def mlstm_inputs_block(nc, con, A, hT, qk, v, out_gate, gates):
    w = A["w_in"][0]

    def make(al):
        acc = [al.sb(f"acc{i}", [P, T]) for i in range(2)]
        conv, silu_done = al.sem("conv"), al.sem("silu_done")

        def vector(dve, units_of, units):
            for sec, it, s, c, u, bank, freed in units_of:
                if sec == 2:
                    continue
                dve.wait_ge(units, u + 1)
                if sec == 0:
                    ch = 4 * it + 2 * s + c
                    wait(dve, silu_done, ch - 1)
                    dve.tensor_scalar(acc[c][:], bank[:], con.cols_b[:, bass.ds(R_CONVW + 48 + ch, 1)],
                                      con.cols_a[:, bass.ds(R_CONVB + ch, 1)], ALU.mult, ALU.add).then_inc(conv, 1)
                    for j in range(1, CONV):
                        dve.wait_ge(conv, 3 * ch + j)
                        op = dve.scalar_tensor_tensor(
                            out=acc[c][:, j:], in0=bank[:, 0:T - j],
                            scalar=con.cols_b[:, bass.ds(R_CONVW + 16 * (3 - j) + ch, 1)],
                            in1=acc[c][:, j:], op0=ALU.mult, op1=ALU.add)
                        op.then_inc(conv if j < 3 else freed, 1)
                elif sec == 1:
                    dve.tensor_copy(v[:, c, bass.ds(2 * it + s, 1), 0:DH],
                                    bank[:, 0:DH].rearrange("p (a d) -> p a d", a=1)).then_inc(freed, 1)
                else:
                    dve.tensor_scalar(gates[:, s], bank[0:HEADS, :], con.gate_bias[:, s:s + 1], None,
                                      ALU.add).then_inc(freed, 1)

        def scalar(act, units_of, units):
            for sec, it, s, c, u, bank, freed in units_of:
                if sec == 0:
                    act.wait_ge(freed, it + 1)
                    act.activation(qk[:, bass.ds(4 * it + 2 * s + c, 1), :], acc[c][:].rearrange("p (a t) -> p a t", a=1),
                                   ACT.Silu).then_inc(silu_done, 1)
                elif sec == 2:
                    act.wait_ge(units, u + 1)
                    act.activation(out_gate[:, bass.ds(4 * it + 2 * s + c, 1), :],
                                   bank[:].rearrange("p (a t) -> p a t", a=1), ACT.Sigmoid).then_inc(freed, 1)
        return vector, scalar

    op = lambda s: hT
    project_block(nc, "proj_m", [("T", 8, w_group(w, C_QK), op), ("N", 4, w_group(w, C_MV), op),
                                 ("T", 4, w_group(w, C_MO), op), ("T1", 2, w_group(w, C_IF, HEADS), op)], make)


def mlstm_block(nc, con, qk, v, out_gate, gates, y_hi, y_lo):
    H = HEADS
    steps = [(h, i) for h in range(H) for i in range(NT)]
    with Alloc(nc, "mlstm") as al:
        absf, expf, logf, lf, fsum, a, g, nm, ones4 = [al.sb(n, [H, T]) for n in
                                                       ("absf", "expf", "logf", "lf", "fsum", "a", "g", "nm", "ones4")]
        a_col, floor = al.sb("a_col", [P, NT, H]), al.sb("floor", [P, NT, H])
        ex = [al.sb(f"ex{i}", [P, T]) for i in range(2)]
        ee = [al.sb(f"ee{i}", [P, T]) for i in range(2)]
        pt = [al.sb(f"pt{i}", [P, T]) for i in range(2)]
        pos, den, rden = al.sb("pos", [P, NT]), al.sb("den", [P, NT]), al.sb("rden", [P, NT])
        cell, y, junk = al.sb("cell", [P, NT, DH]), al.sb("y", [P, NT, DH]), al.sb("junk", [P, DH])
        ss, ms, rstd = al.sb("ss", [P, NT]), al.sb("ms", [P, NT]), al.sb("rstd", [P, NT])
        tmp = al.sb("tmp", [P, 2, T])
        ps_g, ps_t = al.ps("ps_g", [P, T]), al.ps("ps_t", [P, T])
        ps_s = [al.ps(f"ps_s{i}", [P, T]) for i in range(2)]
        ps_n = [al.ps(f"ps_n{i}", [P, T]) for i in range(NT)]
        (act_pre, dve_pre, ones_done, cols_t, col_done, floor_done, gb_done, ex_done, ee_done, mask_done, s_done,
         pt_done, pv_done, den_done, cell_done, ss_done, ms_done, pow_done, y_done, tr_done, tmp_done, hi_done,
         lo_done) = map(al.sem, (
             "act_pre", "dve_pre", "ones_done", "cols_t", "col_done", "floor_done", "gb_done", "ex_done", "ee_done",
             "mask_done", "s_done", "pt_done", "pv_done", "den_done", "cell_done", "ss_done", "ms_done", "pow_done",
             "y_done", "tr_done", "tmp_done", "hi_done", "lo_done"))
        block = al.block()

        @block.scalar
        def _(act):
            act.activation(absf[:], gates[:, 1], ACT.Abs).then_inc(act_pre, 1)
            act.wait_ge(act_pre, 1)
            act.activation(expf[:], absf[:], ACT.Exp, scale=-1.0).then_inc(act_pre, 1)
            act.wait_ge(act_pre, 2)
            act.activation(logf[:], expf[:], ACT.Ln, bias=1.0).then_inc(act_pre, 1)
            act.wait_ge(col_done, 1)
            act.activation(floor[:], ps_t[:, NT * H:2 * NT * H].rearrange("p (t h) -> p t h", h=H),
                           ACT.Exp).then_inc(floor_done, 1)
            for n, (h, i) in enumerate(steps):
                w = T - i * P
                act.wait_ge(ex_done, n + 1)
                if n >= 2:
                    act.wait_ge(pt_done, n - 1)
                act.activation(ee[n % 2][:, 0:w], ex[n % 2][:, 0:w], ACT.Exp, scale=-1.0).then_inc(ee_done, 1)
                if i == NT - 1:
                    for j in range(NT):
                        act.wait_ge(cell_done, NT * h + j + 1)
                        wait(act, ss_done, NT * h + j)
                        act.activation(junk[:], cell[:, j], ACT.Square, accum_out=ss[:, j:j + 1]).then_inc(ss_done, 1)
                    for c in range(2):
                        act.wait_ge(tmp_done, 2 * h + c + 1)
                        act.activation(y_hi[:, 2 * h + c], tmp[:, c], ACT.Copy).then_inc(hi_done, 1)

        @block.gpsimd
        def _(pool):
            pool.memset(ones4[:], 1.0).then_inc(ones_done, 1)
            pool.memset(v[:, :, :, DH:DH + 1], 1.0).then_inc(ones_done, 1)
            for n, (h, i) in enumerate(steps):
                pool.wait_ge(ee_done, n + 1)
                pool.affine_select(out=ee[n % 2][:, 0:P], in_=ee[n % 2][:, 0:P], compare_op=ALU.is_ge, fill=0.0,
                                   base=0, pattern=[[1, P]], channel_multiplier=-1).then_inc(mask_done, 1)
                if i == NT - 1:
                    pool.wait_ge(ms_done, h + 1)
                    pool.tensor_tensor(rstd[:], ms[:], con.pow_half[:, 0:NT], ALU.pow).then_inc(pow_done, 1)

        @block.tensor
        def _(pe):
            pe.wait_ge(dve_pre, 5)
            for t in range(NT):
                pe.transpose(ps_t[:, t * H:(t + 1) * H], a[:, t * P:(t + 1) * P], con.ident[0:H, 0:H])
            for t in range(NT):
                mm = pe.transpose(ps_t[:, (NT + t) * H:(NT + t + 1) * H], nm[:, t * P:(t + 1) * P],
                                  con.ident[0:H, 0:H])
            mm.then_inc(cols_t, 1)

            def scores(n):
                h, i = steps[n]
                if i == 0:
                    wait(pe, ex_done, n)
                    pe.matmul(ps_g[:], con.sel[:, h, :], g[:], start=True, stop=True).then_inc(gb_done, 1)
                wait(pe, pt_done, n - 1)
                for k in range(2):
                    mm = pe.matmul(ps_s[n % 2][:, 0:T - i * P], qk[:, 8 + 2 * h + k, i * P:(i + 1) * P],
                                   qk[:, 2 * h + k, i * P:T], start=(k == 0), stop=(k == 1))
                mm.then_inc(s_done, 1)

            scores(0)
            pe.wait_ge(ones_done, 2)
            for n, (h, i) in enumerate(steps):
                if n + 1 < len(steps):
                    scores(n + 1)
                pe.wait_ge(pt_done, n + 1)
                if i == 0:
                    wait(pe, cell_done, NT * h)
                for j in range(i, NT):
                    mm = pe.matmul(ps_n[j][:, 0:DH + 1], pt[n % 2][:, (j - i) * P:(j - i + 1) * P], v[:, i, h, :],
                                   start=(i == 0), stop=(i == j))
                mm.then_inc(pv_done, 1)
                if i == NT - 1:
                    pe.wait_ge(y_done, NT * (h + 1))
                    for c in range(2):
                        wait(pe, tmp_done, 2 * h + c)
                        if h == 0 and c == 0:
                            pe.wait_ge(col_done, 1)
                            pe.wait_ge(floor_done, 1)
                        for j in range(NT):
                            mm = pe.transpose(ps_t[:, j * P:(j + 1) * P], y[:, j, c * P:(c + 1) * P], con.ident[:])
                        mm.then_inc(tr_done, 1)

        @block.vector
        def _(dve):
            dve.wait_ge(act_pre, 3)
            dve.scalar_tensor_tensor(out=lf[:], in0=gates[:, 1], scalar=0.0, in1=logf[:], op0=ALU.min,
                                     op1=ALU.subtract).then_inc(dve_pre, 1)
            dve.wait_ge(ones_done, 1)
            dve.wait_ge(dve_pre, 1)
            dve.tensor_tensor_scan(fsum[:], ones4[:], lf[:], 0.0, ALU.mult, ALU.add).then_inc(dve_pre, 1)
            dve.wait_ge(dve_pre, 2)
            dve.tensor_tensor(a[:], gates[:, 0], fsum[:], ALU.subtract).then_inc(dve_pre, 1)
            dve.wait_ge(dve_pre, 3)
            dve.tensor_tensor_scan(g[:], a[:], a[:], 0.0, ALU.max, ALU.max).then_inc(dve_pre, 1)
            dve.wait_ge(dve_pre, 4)
            dve.scalar_tensor_tensor(out=nm[:], in0=fsum[:], scalar=-1.0, in1=g[:], op0=ALU.mult,
                                     op1=ALU.subtract).then_inc(dve_pre, 1)
            dve.wait_ge(cols_t, 1)
            dve.tensor_copy(a_col[:], ps_t[:, 0:NT * H].rearrange("p (t h) -> p t h", h=H)).then_inc(col_done, 1)
            dve.wait_ge(col_done, 1)

            def exponents(n):
                h, i = steps[n]
                w = T - i * P
                dve.wait_ge(gb_done, h + 1)
                wait(dve, ee_done, n - 1)
                dve.tensor_scalar(ex[n % 2][:, 0:w], ps_g[:, i * P:T], a_col[:, i, h:h + 1], 0.0, ALU.subtract,
                                  ALU.max).then_inc(ex_done, 1)

            exponents(0)
            for n, (h, i) in enumerate(steps):
                w = T - i * P
                if n + 1 < len(steps):
                    exponents(n + 1)
                dve.wait_ge(s_done, n + 1)
                dve.wait_ge(mask_done, n + 1)
                wait(dve, pv_done, n - 1)
                dve.scalar_tensor_tensor(out=pt[n % 2][:, 0:w], in0=ps_s[n % 2][:, 0:w], scalar=DH ** -0.5,
                                         in1=ee[n % 2][:, 0:w], op0=ALU.mult, op1=ALU.mult).then_inc(pt_done, 1)
                if i < NT - 1:
                    continue
                dve.wait_ge(floor_done, 1)
                dve.wait_ge(pv_done, n + 1)
                for j in range(NT):
                    dve.tensor_tensor(pos[:, j:j + 1], ps_n[j][:, DH:DH + 1], floor[:, j, h:h + 1],
                                      ALU.max).then_inc(den_done, 1)
                dve.wait_ge(den_done, 9 * h + 4)
                for j in range(NT):
                    dve.scalar_tensor_tensor(out=den[:, j:j + 1], in0=ps_n[j][:, DH:DH + 1], scalar=-1.0,
                                             in1=pos[:, j:j + 1], op0=ALU.mult, op1=ALU.max).then_inc(den_done, 1)
                dve.wait_ge(den_done, 9 * h + 8)
                dve.reciprocal(rden[:], den[:]).then_inc(den_done, 1)
                dve.wait_ge(den_done, 9 * h + 9)
                for j in range(NT):
                    wait(dve, y_done, NT * h)
                    dve.tensor_scalar(cell[:, j], ps_n[j][:, 0:DH], rden[:, j:j + 1], None,
                                      ALU.mult).then_inc(cell_done, 1)
                dve.wait_ge(ss_done, NT * (h + 1))
                dve.tensor_scalar(ms[:], ss[:], 1.0 / DH, EPS, ALU.mult, ALU.add).then_inc(ms_done, 1)
                dve.wait_ge(pow_done, h + 1)
                for j in range(NT):
                    dve.tensor_scalar(y[:, j], cell[:, j], rstd[:, j:j + 1], None, ALU.mult).then_inc(y_done, 1)
                for c in range(2):
                    dve.wait_ge(tr_done, 2 * h + c + 1)
                    wait(dve, lo_done, 2 * h)
                    dve.scalar_tensor_tensor(out=tmp[:, c], in0=ps_t[:],
                                             scalar=con.cols_b[:, R_MGAIN + 2 * h + c:R_MGAIN + 2 * h + c + 1],
                                             in1=out_gate[:, 2 * h + c], op0=ALU.mult, op1=ALU.mult).then_inc(tmp_done, 1)
                for c in range(2):
                    dve.wait_ge(hi_done, 2 * h + c + 1)
                    dve.tensor_tensor(y_lo[:, 2 * h + c], tmp[:, c], as_f32(y_hi[:, 2 * h + c]),
                                      ALU.subtract).then_inc(lo_done, 1)


def gated_branch_block(nc, tag, A, hT, y, gate_col, w_branch, merged, m_hl=None):
    branch, gates = columns(w_branch), columns(A["w_in"][0])

    def load(sp, it, s):
        return branch[:, :, bass.ds(it * GC, GC)] if s else gates[:, :, bass.ds(gate_col + it * GC, GC)]

    def make(al):
        freed_bank = lambda b: al.freed[b]
        sg = [al.sb(f"sg{i}", [P, T]) for i in range(2)]
        prod = [al.sb(f"prod{i}", [P, T]) for i in range(2)]
        added, m_hi_done = al.sem("added"), al.sem("m_hi_done")
        m_lo_done = al.sem("m_lo_done")
        freed_by = {}

        def vector(dve, units_of, units):
            for sec, it, s, c, u, bank, freed in units_of:
                freed_by[s, c] = freed
                if s == 0:
                    continue
                ch = 2 * it + c
                dve.wait_ge(units, u + 1)
                dve.wait_ge(freed_by[0, c], it + 1)
                out = merged[:, bass.ds(ch, 1), :]
                sg3 = sg[c][:].rearrange("p (a t) -> p a t", a=1)
                bank3 = bank[:].rearrange("p (a t) -> p a t", a=1)
                if m_hl is None:
                    dve.tensor_tensor(out, bank3, sg3, ALU.mult).then_inc(freed, 1)
                else:
                    p3 = prod[c][:].rearrange("p (a t) -> p a t", a=1)
                    wait(dve, m_lo_done, ch - 1)
                    dve.tensor_tensor(p3, bank3, sg3, ALU.mult).then_inc(freed, 1)
                    dve.wait_ge(freed, it + 1)
                    dve.tensor_tensor(p3, p3, out, ALU.add).then_inc(added, 1)
                    dve.wait_ge(added, ch + 1)
                    hi3, lo3 = m_hl[0][:, bass.ds(ch, 1), :], m_hl[1][:, bass.ds(ch, 1), :]
                    dve.tensor_copy(hi3, p3).then_inc(m_hi_done, 1)
                    dve.wait_ge(m_hi_done, ch + 1)
                    dve.tensor_tensor(lo3, p3, as_f32(hi3), ALU.subtract).then_inc(m_lo_done, 1)

        def scalar(act, units_of, units):
            seen = {}
            for sec, it, s, c, u, bank, freed in units_of:
                if s:
                    continue
                act.wait_ge(units, u + 1)
                wait(act, freed_bank(2 + c), it)
                act.activation(sg[c][:], bank[:], ACT.Sigmoid).then_inc(freed, 1)
        return vector, scalar

    project_block(nc, tag, [("T", 8, load, lambda s: y if s else hT)], make)


def attention_inputs_block(nc, A, hT, qk, v):
    w = A["w_in"][0]

    def make(al):
        def vector(dve, units_of, units):
            for sec, it, s, c, u, bank, freed in units_of:
                if sec == 1:
                    dve.wait_ge(units, u + 1)
                    dve.tensor_copy(v[:, c, bass.ds(2 * it + s, 1), 0:DH],
                                    bank[:, 0:DH].rearrange("p (a d) -> p a d", a=1)).then_inc(freed, 1)

        def scalar(act, units_of, units):
            for sec, it, s, c, u, bank, freed in units_of:
                if sec == 0:
                    act.wait_ge(units, u + 1)
                    act.activation(qk[:, bass.ds(4 * it + 2 * s + c, 1), :],
                                   bank[:].rearrange("p (a t) -> p a t", a=1), ACT.Copy).then_inc(freed, 1)
        return vector, scalar

    op = lambda s: hT
    project_block(nc, "proj_d", [("T", 8, w_group(w, C_DQ), op), ("N", 4, w_group(w, C_DV), op)], make)


def attention_block(nc, con, qk, v, y_hi, y_lo):
    scale = DQK ** -0.5
    steps = [(h, j) for h in range(HEADS) for j in range(NT)]
    with Alloc(nc, "attn") as al:
        p = [[al.sb(f"p{i}{c}", [P, T]) for c in range(2)] for i in range(2)]
        mx, nb, sm, rs = [[al.sb(f"{n}{i}", [P, 2]) for i in range(2)] for n in ("mx", "nb", "sm", "rs")]
        p1w, aw, awt = al.sb("p1w", [P, T]), al.sb("aw", [P, T]), al.sb("awt", [P, T])
        y, junk = al.sb("y", [P, NT, DH]), al.sb("junk", [P, DH])
        ss, ms, rstd = [[al.sb(f"{n}{i}", [P, 1]) for i in range(2)] for n in ("ss", "ms", "rstd")]
        tmp = al.sb("tmp", [P, 2, T])
        ps_s = [[al.ps(f"ps_s{i}{c}", [P, T]) for c in range(2)] for i in range(2)]
        ps_t, ps_y = al.ps("ps_t", [P, T]), al.ps("ps_y", [P, T])
        ps_o = [al.ps(f"ps_o{i}", [P, T]) for i in range(2)]
        (s_done, masked, max_done, nb_done, p_done, rs_done, w_done, p1_done, a_done, at_done, awt_done, o_done,
         ss_done, ms_done, pow_done, y_done, tr_done, tmp_done, hi_done, lo_done) = map(al.sem, (
             "s_done", "masked", "max_done", "nb_done", "p_done", "rs_done", "w_done", "p1_done", "a_done", "at_done",
             "awt_done", "o_done", "ss_done", "ms_done", "pow_done", "y_done", "tr_done", "tmp_done", "hi_done",
             "lo_done"))
        block = al.block()

        @block.tensor
        def _(pe):
            def scores(n):
                h, j = steps[n]
                wait(pe, p_done, 2 * (n - 1))
                for c in range(2):
                    pe.matmul(ps_s[n % 2][c][:, 0:(j + 1) * P], qk[:, 2 * h + c, j * P:(j + 1) * P],
                              qk[:, 8 + 2 * h + c, 0:(j + 1) * P], start=True, stop=True).then_inc(s_done, 1)

            scores(0)
            for n, (h, j) in enumerate(steps):
                if n + 1 < len(steps):
                    scores(n + 1)
                pe.wait_ge(a_done, n + 1)
                wait(pe, awt_done, n)
                for i in range(j + 1):
                    mm = pe.transpose(ps_t[:, i * P:(i + 1) * P], aw[:, i * P:(i + 1) * P], con.ident[:])
                mm.then_inc(at_done, 1)
                pe.wait_ge(awt_done, n + 1)
                wait(pe, y_done, n - 1)
                for i in range(j + 1):
                    mm = pe.matmul(ps_o[n % 2][:, 0:DH], awt[:, i * P:(i + 1) * P], v[:, i, h, 0:DH],
                                   start=(i == 0), stop=(i == j))
                mm.then_inc(o_done, 1)
                if j == NT - 1:
                    pe.wait_ge(y_done, n + 1)
                    for c in range(2):
                        wait(pe, tmp_done, 2 * h + c)
                        for t in range(NT):
                            mm = pe.transpose(ps_y[:, t * P:(t + 1) * P], y[:, t, c * P:(c + 1) * P], con.ident[:])
                        mm.then_inc(tr_done, 1)

        @block.scalar
        def _(act):
            def tail(n):
                w = (steps[n][1] + 1) * P
                act.wait_ge(at_done, n + 1)
                wait(act, o_done, n)
                act.activation(awt[:, 0:w], ps_t[:, 0:w], ACT.Copy).then_inc(awt_done, 1)
                act.wait_ge(o_done, n + 1)
                wait(act, ss_done, n)
                wait(act, ms_done, n - 1)
                act.activation(junk[:], ps_o[n % 2][:, 0:DH], ACT.Square, accum_out=ss[n % 2][:]).then_inc(ss_done, 1)

            for n, (h, j) in enumerate(steps):
                w = (j + 1) * P
                act.wait_ge(nb_done, n + 1)
                wait(act, a_done, n - 1)
                for c in range(2):
                    act.activation(p[n % 2][c][:, 0:w], ps_s[n % 2][c][:, 0:w], ACT.Exp, bias=nb[n % 2][:, c:c + 1],
                                   scale=scale, accum_out=sm[n % 2][:, c:c + 1]).then_inc(p_done, 1)
                tail(n)
                if j == NT - 1:
                    for c in range(2):
                        act.wait_ge(tmp_done, 2 * h + c + 1)
                        act.activation(y_hi[:, 2 * h + c], tmp[:, c], ACT.Copy).then_inc(hi_done, 1)

        @block.gpsimd
        def _(pool):
            for n in range(len(steps)):
                pool.wait_ge(ms_done, n + 1)
                wait(pool, y_done, n - 1)
                pool.tensor_tensor(rstd[n % 2][:], ms[n % 2][:], con.pow_half[:, 0:1], ALU.pow).then_inc(pow_done, 1)

        @block.vector
        def _(dve):
            def maxima(n):
                w = (steps[n][1] + 1) * P
                dve.wait_ge(s_done, 2 * n + 2)
                for c in range(2):
                    dve.memset(ps_s[n % 2][c][0:CHUNK, w - CHUNK:w], NEG).then_inc(masked, 1)
                dve.wait_ge(masked, 2 * n + 2)
                for c in range(2):
                    dve.tensor_reduce(mx[n % 2][:, c:c + 1], ps_s[n % 2][c][:, 0:w], AX_X, ALU.max).then_inc(max_done, 1)
                dve.wait_ge(max_done, 2 * n + 2)
                wait(dve, p_done, 2 * (n - 1))
                dve.tensor_scalar(nb[n % 2][:], mx[n % 2][:], -scale, None, ALU.mult).then_inc(nb_done, 1)

            maxima(0)
            for n, (h, j) in enumerate(steps):
                w = (j + 1) * P
                if n + 1 < len(steps):
                    maxima(n + 1)
                dve.wait_ge(p_done, 2 * n + 2)
                dve.reciprocal(rs[n % 2][:], sm[n % 2][:]).then_inc(rs_done, 1)
                dve.wait_ge(rs_done, n + 1)
                dve.tensor_tensor(rs[n % 2][:, 1:2], rs[n % 2][:, 1:2], con.lam[:], ALU.mult).then_inc(w_done, 1)
                dve.wait_ge(w_done, n + 1)
                dve.tensor_scalar(p1w[:, 0:w], p[n % 2][1][:, 0:w], rs[n % 2][:, 1:2], None, ALU.mult).then_inc(p1_done, 1)
                dve.wait_ge(p1_done, n + 1)
                wait(dve, at_done, n)
                dve.scalar_tensor_tensor(out=aw[:, 0:w], in0=p[n % 2][0][:, 0:w], scalar=rs[n % 2][:, 0:1],
                                         in1=p1w[:, 0:w], op0=ALU.mult, op1=ALU.subtract).then_inc(a_done, 1)
                dve.wait_ge(ss_done, n + 1)
                wait(dve, pow_done, n - 1)
                dve.tensor_scalar(ms[n % 2][:], ss[n % 2][:], 1.0 / DH, EPS, ALU.mult, ALU.add).then_inc(ms_done, 1)
                dve.wait_ge(pow_done, n + 1)
                wait(dve, tr_done, 2 * h)
                dve.tensor_scalar(y[:, j], ps_o[n % 2][:, 0:DH], rstd[n % 2][:], None, ALU.mult).then_inc(y_done, 1)
                if j < NT - 1:
                    continue
                for c in range(2):
                    dve.wait_ge(tr_done, 2 * h + c + 1)
                    wait(dve, lo_done, 2 * h)
                    dve.tensor_scalar(tmp[:, c], ps_y[:], con.cols_b[:, R_DGAIN + 2 * h + c:R_DGAIN + 2 * h + c + 1],
                                      None, ALU.mult).then_inc(tmp_done, 1)
                for c in range(2):
                    dve.wait_ge(hi_done, 2 * h + c + 1)
                    dve.tensor_tensor(y_lo[:, 2 * h + c], tmp[:, c], as_f32(y_hi[:, 2 * h + c]),
                                      ALU.subtract).then_inc(lo_done, 1)


def out_block(nc, A, m_hl, y):
    def make(al):
        def vector(dve, units_of, units):
            for sec, it, s, c, u, bank, freed in units_of:
                if c % 2 == 0:
                    dve.wait_ge(units, u + 1)
                    dve.tensor_copy(y[:, c, bass.ds((2 * it + s) * GC, GC)], bank[:, 0:GC]).then_inc(freed, 1)

        def scalar(act, units_of, units):
            for sec, it, s, c, u, bank, freed in units_of:
                if c % 2:
                    act.wait_ge(units, u + 1)
                    act.activation(y[:, c, bass.ds((2 * it + s) * GC, GC)], bank[:, 0:GC], ACT.Copy).then_inc(freed, 1)
        return vector, scalar

    project_block(nc, "proj_o", [("N", 4, w_group(A["w_out"][0], 0), lambda s: m_hl)], make)


def residual_block(nc, tag, con, x_src, y, gate_cols, dst):
    with Alloc(nc, tag) as al:
        x = al.sb("x", [P, NT, D])
        row = al.sb("row", [P, D])
        diag = [al.sb(f"diag{i}", [P, P]) for i in range(2)]
        junk, ss, ms, rstd = al.sb("junk", [P, D]), al.sb("ss", [P, NT]), al.sb("ms", [P, NT]), al.sb("rstd", [P, NT])
        yg = [al.sb(f"yg{i}", [P, D]) for i in range(2)]
        ps = [al.ps(f"ps{i}", [P, P]) for i in range(2)]
        x_in = [al.sem(f"x_in{i}") for i in range(NT)]
        diag_done, spread, row_done, ss_done, ms_done, pow_done, yg_done, sum_done, stored = map(al.sem, (
            "diag_done", "spread", "row_done", "ss_done", "ms_done", "pow_done", "yg_done", "sum_done", "stored"))
        block = al.block()

        @block.sync
        def _(sp):
            for t in range(NT):
                sp.dma_start(x[:, t], x_src[t * P:(t + 1) * P, :]).then_inc(x_in[t], 16)
            for t in range(NT):
                sp.wait_ge(sum_done, t + 1)
                sp.dma_start(dst[t * P:(t + 1) * P, :], x[:, t]).then_inc(stored, 16)
            sp.wait_ge(stored, 16 * NT)

        @block.scalar
        def _(act):
            for t in range(NT):
                wait(act, ss_done, t)
                act.activation(junk[:], y[:, t], ACT.Square, accum_out=ss[:, t:t + 1]).then_inc(ss_done, 1)
            for k in range(KD):
                act.wait_ge(spread, k + 1)
                act.activation(row[:, k * P:(k + 1) * P], ps[k % 2][:], ACT.Copy).then_inc(row_done, 1)

        @block.gpsimd
        def _(pool):
            pool.wait_ge(ms_done, 1)
            pool.tensor_tensor(rstd[:], ms[:], con.pow_half[:, 0:NT], ALU.pow).then_inc(pow_done, 1)

        @block.tensor
        def _(pe):
            for k in range(KD):
                pe.wait_ge(diag_done, k + 1)
                wait(pe, row_done, k - 1)
                pe.matmul(ps[k % 2][:], con.ones[:], diag[k % 2][:], start=True, stop=True).then_inc(spread, 1)

        @block.vector
        def _(dve):
            for k in range(KD):
                wait(dve, spread, k - 1)
                dve.tensor_scalar(diag[k % 2][:], con.ident[:], gate_cols[:, k:k + 1], None,
                                  ALU.mult).then_inc(diag_done, 1)
            dve.wait_ge(ss_done, NT)
            dve.tensor_scalar(ms[:], ss[:], 1.0 / D, EPS, ALU.mult, ALU.add).then_inc(ms_done, 1)
            dve.wait_ge(pow_done, 1)
            dve.wait_ge(row_done, KD)
            for t in range(NT):
                dve.wait_ge(x_in[t], 16)
                wait(dve, sum_done, t - 1)
                dve.scalar_tensor_tensor(out=yg[t % 2][:], in0=y[:, t], scalar=rstd[:, t:t + 1], in1=row[:],
                                         op0=ALU.mult, op1=ALU.mult).then_inc(yg_done, 1)
                dve.wait_ge(yg_done, t + 1)
                dve.tensor_tensor(x[:, t], x[:, t], yg[t % 2][:], ALU.add).then_inc(sum_done, 1)


class Consts:

    def __init__(self, al):
        self.ident, self.ones = al.sb("ident", [P, P]), al.sb("ones", [P, P])
        self.iota, self.pow_half = al.sb("iota", [P, P]), al.sb("pow_half", [P, 8])
        self.sel = al.sb("sel", [HEADS, HEADS, P])
        self.cols_a, self.cols_b = al.sb("cols_a", [P, NROWS_A]), al.sb("cols_b", [P, NROWS_B])
        self.ada = al.sb("ada", [P, 48])
        self.lam_cols, self.lam = al.sb("lam_cols", [P, 4]), al.sb("lam", [P, 1])
        self.gate_bias = al.sb("gate_bias", [HEADS, 2])
        self.scale_a, self.scale_b = al.sb("scale_a", [P, KD]), al.sb("scale_b", [P, KD])
        self.gate_a, self.gate_b = al.sb("gate_a", [P, KD]), al.sb("gate_b", [P, KD])


def mixer(nc, con, A, hT, x1):
    x = A["x"].rearrange("b s d -> (b s) d")
    modulate_block(nc, "mod_a", con, x, hT[0], hT[1], con.scale_a, 0)
    with Alloc(nc, "mix") as al:
        merged = al.sb("merged", [P, KD, T])
        y_hl = al.sb("y_hi", [P, KD, T], F32R), al.sb("y_lo", [P, KD, T], F32R)
        with Alloc(nc, "in") as ai:
            qk, v = ai.sb("qk", [P, 2 * KD, T]), ai.sb("v", [P, NT, HEADS, DH + 1])
            with Alloc(nc, "gate") as ag:
                out_gate, gates = ag.sb("out_gate", [P, KD, T]), ag.sb("gates", [HEADS, 2, T])
                mlstm_inputs_block(nc, con, A, hT, qk, v, out_gate, gates)
                mlstm_block(nc, con, qk, v, out_gate, gates, *y_hl)
            gated_branch_block(nc, "branch_m", A, hT, y_hl, C_GM, A["w_br_m"][0], merged)
            attention_inputs_block(nc, A, hT, qk, v)
            attention_block(nc, con, qk, v, *y_hl)
        with Alloc(nc, "mhl") as am:
            m_hl = am.sb("m_hi", [P, KD, T], F32R), am.sb("m_lo", [P, KD, T], F32R)
            gated_branch_block(nc, "branch_d", A, hT, y_hl, C_GD, A["w_br_d"][0], merged, m_hl)
            y = am.sb("y", [P, NT, D])
            out_block(nc, A, m_hl, y)
            residual_block(nc, "res_a", con, x, y, con.gate_a, x1)


U_RING, R_STEPS, G_STEPS, G_TOK = 4, 12, 16, 8
NEXP = NK


def query_block(nc, A, hT, qry):
    def make(al):
        def vector(dve, units_of, units):
            for sec, it, s, c, u, bank, freed in units_of:
                pass

        def scalar(act, units_of, units):
            for sec, it, s, c, u, bank, freed in units_of:
                act.wait_ge(units, u + 1)
                act.activation(qry[:, bass.ds(4 * it + 2 * s + c, 1), :],
                               bank[:].rearrange("p (a t) -> p a t", a=1), ACT.Copy).then_inc(freed, 1)
        return vector, scalar

    project_block(nc, "query", [("T", 8, w_group(A["w_query"][0], 0), lambda s: hT)], make)


def scores_block(nc, con, A, qry, scores):
    HC = PH * HALVES
    with Alloc(nc, "scores") as al:
        keys, keys_t = al.sb("keys", [P, HC, P]), al.sb("keys_t", [P, HC, NK])
        sc = [al.sb(f"sc{i}", [P, HC, NK]) for i in range(2)]
        ps = [al.ps(f"ps{i}", [P, 4, P]) for i in range(4)]
        keys_in, turned, kept, scored, copied = map(al.sem, ("keys_in", "turned", "kept", "scored", "copied"))
        stored = [al.sem(f"stored{i}") for i in range(2)]
        block = al.block()

        @block.sync
        def _(sp):
            sp.dma_start(keys[:], A["sub_keys"][0].rearrange("h c n d -> n (h c) d")).then_inc(keys_in, 16)
            for t in range(NT):
                sp.wait_ge(copied, 4 * (t + 1))
                sp.dma_start(scores[t * P:(t + 1) * P, :], sc[t % 2][:].rearrange("p a n -> p (a n)")).then_inc(
                    stored[t % 2], 16)
            for i in range(2):
                sp.wait_ge(stored[i], 16 * NT // 2)

        @block.tensor
        def _(pe):
            pe.wait_ge(keys_in, 16)
            for q in range(4):
                for m in range(4):
                    mm = pe.transpose(ps[q][:, m, :], keys[:, 4 * q + m, :], con.ident[:])
                mm.then_inc(turned, 1)
            for t in range(NT):
                for q in range(4):
                    pe.wait_ge(kept, 4)
                    wait(pe, copied, 4 * (t - 1) + q + 1)
                    for m in range(4):
                        mm = pe.matmul(ps[q][:, m, :], qry[:, 4 * q + m, t * P:(t + 1) * P], keys_t[:, 4 * q + m, :],
                                       start=True, stop=True)
                    mm.then_inc(scored, 1)

        @block.vector
        def _(dve):
            for q in range(4):
                dve.wait_ge(turned, q + 1)
                dve.tensor_copy(keys_t[:, 4 * q:4 * q + 4, :], ps[q][:]).then_inc(kept, 1)

        @block.scalar
        def _(act):
            for t in range(NT):
                wait(act, stored[t % 2], 16 * (t // 2))
                for q in range(4):
                    act.wait_ge(scored, 4 * t + q + 1)
                    act.activation(sc[t % 2][:, 4 * q:4 * q + 4, :], ps[q][:], ACT.Copy).then_inc(copied, 1)


def experts_in_block(nc, con, A, hT, scores, acts, gmat):
    HC = PH * HALVES
    u = A["expert_u"][0]
    with Alloc(nc, "xin") as al:
        raw = [al.sb(f"u{i}", [P, D]) for i in range(U_RING)]
        uhi = [al.sb(f"uhi{i}", [P, KD, P], F32R) for i in range(2)]
        ulo = [al.sb(f"ulo{i}", [P, KD, P], F32R) for i in range(2)]
        act_t = [al.sb(f"act{i}", [P, T]) for i in range(4)]
        sc, sc2 = al.sb("sc", [P, HC, NK]), al.sb("sc2", [P, HC, NK])
        top, ix, ixf = al.sb("top", [P, HC, TOPK]), al.sb("ix", [P, HC, TOPK], U32), al.sb("ixf", [P, HC, TOPK])
        best, bpos = al.sb("best", [P, PH, TOPK]), al.sb("bpos", [P, PH, TOPK], U32)
        au, bu = al.sb("au", [P, PH, TOPK], U32), al.sb("bu", [P, PH, TOPK], U32)
        rank = [al.sb(f"rank{c}", [P, PH, TOPK]) for c in range(2)]
        pick = [al.sb(f"pick{c}", [P, PH * TOPK, TOPK]) for c in range(2)]
        key = [al.sb(f"key{c}", [P, PH * TOPK]) for c in range(2)]
        eg, ge, gate = [al.sb(n, [P, PH, TOPK]) for n in ("eg", "ge", "gate")]
        gsum, ginv = al.sb("gsum", [P, PH]), al.sb("ginv", [P, PH])
        slot = [al.sb(f"slot{n}", [P, T]) for n in range(3)]
        hot_j = [al.sb(f"hot_j{i}", [P, G_TOK, NK]) for i in range(2)]
        hot_i = [al.sb(f"hot_i{i}", [P, G_TOK, NK]) for i in range(2)]
        stage = [al.sb(f"stage{i}", [P, NK, 8 * G_TOK]) for i in range(2)]
        ps_t = [al.ps(f"ps_t{i}", [P, KD, P]) for i in range(2)]
        ps_u = [al.ps(f"ps_u{i}", [P, T]) for i in range(2)]
        ps_g = [al.ps(f"ps_g{i}", [P, 4, NK]) for i in range(2)]
        landed = [al.sem(f"landed{i}") for i in range(U_RING)]
        kept = [al.sem(f"kept{i}") for i in range(4)]
        flushed = [al.sem(f"flushed{i}") for i in range(2)]
        (t_done, hi_done, lo_done, u_done, gelu_done, sc_in, chosen, exp_done, sub_done, pool_step, keys_done,
         slots_t, slots_done, hot_done, g_done, staged, sum_inv, is_rank) = map(al.sem, (
             "t_done", "hi_done", "lo_done", "u_done", "gelu_done", "sc_in", "chosen", "exp_done", "sub_done",
             "pool_step", "keys_done", "slots_t", "slots_done", "hot_done", "g_done", "staged", "sum_inv", "is_rank"))
        block = al.block()
        n_r = NT * R_STEPS
        n_g = T // G_TOK
        n_tail = NEXP - n_r - n_g
        assert n_tail > 0 and n_tail % 4 == 0
        cand = sc[:].rearrange("p (h c) k -> p h (c k)", c=2)
        cand2 = sc2[:].rearrange("p (h c) k -> p h (c k)", c=2)
        STAGES = 16

        def steps(eng, route, gates, every):
            for tt in pairs(eng, NT, True):
                for s in range(R_STEPS):
                    every(R_STEPS * tt + s, s, route, (tt, s))
            for gi in pairs(eng, n_g // G_STEPS, False):
                for q in range(G_STEPS):
                    every(n_r + G_STEPS * gi + q, q, gates, (gi, q))
            for it in pairs(eng, n_tail // 4, False, True):
                for s in range(4):
                    every(n_r + n_g + 4 * it + s, s, None, None)

        @block.sync
        def _(sp):
            def every(n, s, more, args):
                row = settled(sp, n * P)
                arow = settled(sp, (n - 4) * P) if not (isinstance(n, int) and n < 4) else 0
                wait(sp, t_done, n - 3)
                sp.dma_start(raw[s % U_RING][:], u[bass.ds(row, P), :]).then_inc(landed[s % U_RING], 16)
                if not (isinstance(n, int) and n < 4):
                    sp.wait_ge(gelu_done, n - 3)
                    sp.dma_start(acts[bass.ds(arow, P), :], act_t[s % 4][:]).then_inc(kept[s % 4], 16)
                if more:
                    more(*args)

            def route(tt, s):
                if s == 0:
                    trow = settled(sp, tt * P)
                    wait(sp, chosen, STAGES * (tt - 1) + 13)
                    sp.dma_start(sc[:].rearrange("p a k -> p (a k)"), scores[bass.ds(trow, P), :]).then_inc(sc_in, 16)

            def gates(gi, q):
                if q == 12:
                    flush(gi, 0)
                if q == 4 and not (isinstance(gi, int) and gi == 0):
                    flush(gi - 1, 1)

            def flush(gi, h):
                tok = settled(sp, gi * (G_STEPS * G_TOK) + h * 8 * G_TOK)
                sp.wait_ge(staged, 2 * (G_STEPS * gi + 8 * h + 8))
                sp.dma_start(gmat.rearrange("(i j) t -> j i t", j=NK)[:, :, bass.ds(tok, 8 * G_TOK)],
                             stage[h][:]).then_inc(flushed[h], 16)

            def route_or(tt, s):
                route(tt, s)

            for tt in pairs(sp, NT, True):
                for s in range(R_STEPS):
                    every(R_STEPS * tt + s, s, route_or, (tt, s))
            for gi in pairs(sp, n_g // G_STEPS, True):
                for q in range(G_STEPS):
                    every(n_r + G_STEPS * gi + q, q, gates, (gi, q))
            for it in pairs(sp, n_tail // 4, True):
                for s in range(4):
                    every(n_r + n_g + 4 * it + s, s, None, None)
                if isinstance(it, int) and it == 0:
                    flush(n_g // G_STEPS - 1, 1)
            for n in range(NEXP, NEXP + 4):
                sp.wait_ge(gelu_done, n - 3)
                sp.dma_start(acts[(n - 4) * P:(n - 3) * P, :], act_t[n % 4][:]).then_inc(kept[n % 4], 16)
            for i in range(4):
                sp.wait_ge(kept[i], 16 * NEXP // 4)
            for h in range(2):
                sp.wait_ge(flushed[h], 16 * (n_g // G_STEPS))

        @block.tensor
        def _(pe):
            def turn(n, s):
                pe.wait_ge(landed[s % U_RING], 16 * (n // U_RING + 1) if isinstance(n, int) else lap(n, s))
                wait(pe, lo_done, n - 1)
                for k in range(KD):
                    mm = pe.transpose(ps_t[s % 2][:, k, :], raw[s % U_RING][:, k * P:(k + 1) * P], con.ident[:])
                mm.then_inc(t_done, 1)

            laps = {}

            def lap(n, s):
                return laps["value"]

            def every(n, s, more, args, last=False, base=None, it=None, per=None):
                if not last:
                    if base is not None:
                        laps["value"] = 16 * ((base + s + 1) // U_RING + 1) + 16 * (per // U_RING) * it
                    turn(n + 1, s + 1)
                pe.wait_ge(lo_done, n + 1)
                wait(pe, gelu_done, n - 1)
                i = 0
                for k in range(KD):
                    for a, m in ((uhi, hT[0]), (uhi, hT[1]), (ulo, hT[0])):
                        mm = pe.matmul(ps_u[s % 2][:], a[s % 2][:, k, :], m[:, k, :], start=(i == 0),
                                       stop=(i == 3 * KD - 1))
                        i += 1
                mm.then_inc(u_done, 1)
                if more:
                    more(*args)

            def turn_slots(tt):
                pe.wait_ge(keys_done, 2 * tt + 2)
                pe.wait_ge(chosen, STAGES * (tt + 1))
                wait(pe, slots_done, tt)
                for i, src in enumerate((key[0][:], key[1][:], gate[:].rearrange("p h k -> p (h k)"))):
                    mm = pe.transpose(ps_g[0][:, i, :], src, con.ident[:])
                mm.then_inc(slots_t, 1)

            def route(tt, s):
                if s == 6 and not (isinstance(tt, int) and tt == 0):
                    turn_slots(tt - 1)

            def gates(gi, q):
                m = G_STEPS * gi + q
                pe.wait_ge(hot_done, m + 1)
                for b in range(2):
                    wait(pe, staged, 2 * m + b - 1)
                    for k in range(4):
                        mm = pe.matmul(ps_g[b][:, k, :], hot_j[q % 2][:, 4 * b + k, :], hot_i[q % 2][:, 4 * b + k, :],
                                       start=True, stop=True)
                    mm.then_inc(g_done, 1)

            pe.wait_ge(landed[0], 16)
            turn(0, 0)
            for tt in pairs(pe, NT, True):
                for s in range(R_STEPS):
                    every(R_STEPS * tt + s, s, route, (tt, s), base=0, it=tt, per=R_STEPS)
            turn_slots(NT - 1)
            pe.wait_ge(slots_done, NT)
            for gi in pairs(pe, n_g // G_STEPS, True):
                for q in range(G_STEPS):
                    every(n_r + G_STEPS * gi + q, q, gates, (gi, q), base=n_r, it=gi, per=G_STEPS)
            for it in pairs(pe, n_tail // 4, False, True):
                for s in range(4):
                    n = n_r + n_g + 4 * it + s
                    every(n, s, None, None, last=isinstance(n, int) and n == NEXP - 1, base=n_r + n_g, it=it, per=4)

        @block.scalar
        def _(act):
            def cut(n, s):
                act.wait_ge(t_done, n + 1)
                wait(act, u_done, n - 1)
                act.activation(uhi[s % 2][:], ps_t[s % 2][:], ACT.Copy).then_inc(hi_done, 1)

            def every(n, s, more, args, last=False, laps=None):
                if not last:
                    cut(n + 1, s + 1)
                act.wait_ge(u_done, n + 1)
                if laps is None or not (isinstance(laps, int) and laps <= 0):
                    wait(act, kept[s % 4], laps)
                act.activation(act_t[s % 4][:], ps_u[s % 2][:], ACT.Gelu).then_inc(gelu_done, 1)
                if more:
                    more(*args)

            def route(tt, s):
                if s == R_STEPS - 1:
                    act.wait_ge(sub_done, tt + 1)
                    act.activation(ge[:], eg[:], ACT.Exp).then_inc(exp_done, 1)

            def gates(gi, q):
                m = G_STEPS * gi + q
                for b in range(2):
                    act.wait_ge(g_done, 2 * m + b + 1)
                    if q % 8 == 0 and b == 0 and not (isinstance(gi, int) and gi == 0):
                        act.wait_ge(flushed[q // 8], 16 * gi)
                    t0 = (q % 8) * G_TOK + 4 * b
                    act.activation(stage[q // 8][:, :, t0:t0 + 4], ps_g[b][:].rearrange("p t i -> p i t"),
                                   ACT.Copy).then_inc(staged, 1)

            cut(0, 0)
            for tt in pairs(act, NT, True):
                for s in range(R_STEPS):
                    every(R_STEPS * tt + s, s, route, (tt, s), laps=16 * (s // 4) + 16 * (R_STEPS // 4) * tt)
            for gi in pairs(act, n_g // G_STEPS, True):
                for q in range(G_STEPS):
                    every(n_r + G_STEPS * gi + q, q, gates, (gi, q), laps=16 * ((n_r + q) // 4) + 16 * (G_STEPS // 4) * gi)
            for it in pairs(act, n_tail // 4, False, True):
                for s in range(4):
                    n = n_r + n_g + 4 * it + s
                    every(n, s, None, None, last=isinstance(n, int) and n == NEXP - 1,
                          laps=16 * ((n_r + n_g) // 4) + 16 * it)

        @block.gpsimd
        def _(pool):
            step = [0]

            def chain(op):
                op.then_inc(pool_step, 1)
                step[0] += 1
                return step[0]

            per_tile = 2 * 4
            for tt in pairs(pool, NT, True):
                step[0] = 0
                wait(pool, slots_t, tt)
                for c in range(HALVES):
                    base = per_tile * tt
                    pool.wait_ge(is_rank, 2 * tt + c + 1)
                    p4 = pick[c][:].rearrange("p (h k) a -> p h k a", h=PH)
                    nums = ixf[:].rearrange("p (h c) k -> p h c k", c=2)[:, :, c, :].unsqueeze(2).to_broadcast(
                        [P, PH, TOPK, TOPK])
                    chain(pool.tensor_tensor(p4, p4, nums, ALU.mult))
                    for w in (8, 4, 2):
                        pool.wait_ge(pool_step, base + step[0])
                        chain(pool.tensor_tensor(pick[c][:, :, 0:w], pick[c][:, :, 0:w], pick[c][:, :, w:2 * w],
                                                 ALU.add))
                    pool.wait_ge(pool_step, base + step[0])
                    pool.tensor_tensor(key[c][:].unsqueeze(2), pick[c][:, :, 0:1], pick[c][:, :, 1:2],
                                       ALU.add).then_inc(keys_done, 1)

        @block.vector
        def _(dve):
            def cut(n, s):
                dve.wait_ge(hi_done, n + 1)
                dve.tensor_tensor(ulo[s % 2][:], ps_t[s % 2][:], as_f32(uhi[s % 2][:]), ALU.subtract).then_inc(lo_done, 1)

            def every(n, s, more, args, last=False):
                if not last:
                    cut(n + 1, s + 1)
                if more:
                    more(*args)

            def at(tt, k):
                dve.wait_ge(chosen, STAGES * tt + k)

            def top8(out, src, tt, k, count):
                for x in range(count):
                    op = dve.max(out=out(x), in_=src(x))
                op.then_inc(chosen, 1)
                at(tt, k)

            def where(out, vals, src, tt, k, count):
                for x in range(count):
                    op = dve.max_index(out=out(x), in_max=vals(x), in_values=src(x))
                op.then_inc(chosen, 1)
                at(tt, k)

            def strike(out, vals, src, tt, k, count):
                for x in range(count):
                    op = dve.match_replace(out=out(x), in_to_replace=vals(x), in_values=src(x), imm_value=NEG)
                op.then_inc(chosen, 1)
                at(tt, k)

            lo8, hi8 = slice(0, 8), slice(8, 16)
            s_of, s2_of = (lambda x: sc[:, x, :]), (lambda x: sc2[:, x, :])
            c_of, c2_of = (lambda x: cand[:, x, :]), (lambda x: cand2[:, x, :])

            def route(tt, s):
                first = isinstance(tt, int) and tt == 0
                if s == 0:
                    if not first:
                        dve.wait_ge(keys_done, 2 * tt)
                        dve.wait_ge(exp_done, tt)
                    dve.wait_ge(sc_in, 16 * (tt + 1))
                    dve.memset(gsum[:], 0.0)
                    top8(lambda x: top[:, x, lo8], s_of, tt, 1, HC)
                elif s == 1:
                    where(lambda x: ix[:, x, lo8], lambda x: top[:, x, lo8], s_of, tt, 2, HC)
                elif s == 2:
                    strike(s2_of, lambda x: top[:, x, lo8], s_of, tt, 3, HC)
                elif s == 3:
                    top8(lambda x: top[:, x, hi8], s2_of, tt, 4, HC)
                elif s == 4:
                    where(lambda x: ix[:, x, hi8], lambda x: top[:, x, hi8], s2_of, tt, 5, HC)
                elif s == 5:
                    dve.tensor_copy(ixf[:], ix[:]).then_inc(chosen, 1)
                    at(tt, 6)
                    t4 = top[:].rearrange("p (h c) k -> p h c k", c=2)
                    shape = [P, PH, TOPK, TOPK]
                    dve.tensor_tensor(cand.rearrange("p h (a b) -> p h a b", b=TOPK),
                                      t4[:, :, 0, :].unsqueeze(3).to_broadcast(shape),
                                      t4[:, :, 1, :].unsqueeze(2).to_broadcast(shape), ALU.add).then_inc(chosen, 1)
                    at(tt, 7)
                elif s == 6:
                    if not first:
                        copy_slots(tt - 1)
                    top8(lambda x: best[:, x, lo8], c_of, tt, 8, PH)
                elif s == 7:
                    where(lambda x: bpos[:, x, lo8], lambda x: best[:, x, lo8], c_of, tt, 9, PH)
                elif s == 8:
                    strike(c2_of, lambda x: best[:, x, lo8], c_of, tt, 10, PH)
                elif s == 9:
                    top8(lambda x: best[:, x, hi8], c2_of, tt, 11, PH)
                elif s == 10:
                    where(lambda x: bpos[:, x, hi8], lambda x: best[:, x, hi8], c2_of, tt, 12, PH)
                    dve.tensor_single_scalar(au[:], bpos[:], 4, ALU.logical_shift_right)
                    dve.tensor_single_scalar(bu[:], bpos[:], 15, ALU.bitwise_and).then_inc(chosen, 1)
                    at(tt, 13)
                    dve.tensor_copy(rank[0][:], au[:])
                    dve.tensor_copy(rank[1][:], bu[:]).then_inc(chosen, 1)
                else:
                    opts = con.iota[:, 0:TOPK].unsqueeze(1).to_broadcast([P, PH * TOPK, TOPK])
                    dve.tensor_tensor(eg[:], best[:], best[:, :, 0:1].to_broadcast([P, PH, TOPK]),
                                      ALU.subtract).then_inc(sub_done, 1)
                    at(tt, 14)
                    for c in range(HALVES):
                        mine = rank[c][:].rearrange("p h k -> p (h k)").unsqueeze(2).to_broadcast(
                            [P, PH * TOPK, TOPK])
                        dve.tensor_tensor(pick[c][:], mine, opts, ALU.is_equal).then_inc(is_rank, 1)
                    dve.wait_ge(exp_done, tt + 1)
                    dve.tensor_reduce(gsum[:], ge[:], AX_X, ALU.add).then_inc(chosen, 1)
                    at(tt, 15)
                    dve.reciprocal(ginv[:], gsum[:]).then_inc(sum_inv, 1)
                    dve.wait_ge(sum_inv, tt + 1)
                    dve.tensor_tensor(gate[:], ge[:], ginv[:].unsqueeze(2).to_broadcast([P, PH, TOPK]),
                                      ALU.mult).then_inc(chosen, 1)

            def copy_slots(tt):
                dve.wait_ge(slots_t, tt + 1)
                for i in range(3):
                    op = dve.tensor_copy(slot[i][:, bass.ds(tt * P, P)], ps_g[0][:, i, :])
                op.then_inc(slots_done, 1)

            def gates(gi, q):
                m = G_STEPS * gi + q
                wait(dve, g_done, 2 * (m - 1))
                for k in range(G_TOK):
                    tok = gi * (G_STEPS * G_TOK) + q * G_TOK + k
                    i_s, j_s, g_s = [slot[x][:, bass.ds(tok, 1)] for x in range(3)]
                    dve.tensor_scalar(hot_j[q % 2][:, k, :], con.iota[:], j_s, None, ALU.is_equal)
                    op = dve.tensor_scalar(hot_i[q % 2][:, k, :], con.iota[:], i_s, g_s, ALU.is_equal, ALU.mult)
                op.then_inc(hot_done, 1)

            cut(0, 0)
            for tt in pairs(dve, NT, True):
                for s in range(R_STEPS):
                    every(R_STEPS * tt + s, s, route, (tt, s))
            copy_slots(NT - 1)
            dve.wait_ge(slots_done, NT)
            for gi in pairs(dve, n_g // G_STEPS, True):
                for q in range(G_STEPS):
                    every(n_r + G_STEPS * gi + q, q, gates, (gi, q))
            for it in pairs(dve, n_tail // 4, False, True):
                for s in range(4):
                    n = n_r + n_g + 4 * it + s
                    every(n, s, None, None, last=isinstance(n, int) and n == NEXP - 1)


def experts_out_block(nc, A, acts, gmat, y):
    vexp = A["expert_v"][0]
    RING = 4
    with Alloc(nc, "xout") as al:
        v = [al.sb(f"v{i}", [P, D]) for i in range(RING)]
        a = [al.sb(f"a{i}", [P, T]) for i in range(RING)]
        g = [al.sb(f"g{i}", [P, T]) for i in range(RING)]
        vhi, vlo = [[al.sb(f"{n}{i}", [P, D], F32R) for i in range(2)] for n in ("vhi", "vlo")]
        wt = [al.sb(f"wt{i}", [P, T]) for i in range(2)]
        whi, wlo = [[al.sb(f"{n}{i}", [P, T], F32R) for i in range(2)] for n in ("whi", "wlo")]
        out = [[al.ps(f"out{t}{h}", [P, T]) for h in range(2)] for t in range(NT)]
        v_in, ag_in = [al.sem(f"v_in{i}") for i in range(RING)], [al.sem(f"ag_in{i}") for i in range(RING)]
        vhi_done, vlo_done, wt_done, whi_done, wlo_done, used, y_done = map(
            al.sem, ("vhi_done", "vlo_done", "wt_done", "whi_done", "wlo_done", "used", "y_done"))
        block = al.block()

        def steps(eng):
            for it in pairs(eng, NEXP // RING, True, True):
                for s in range(RING):
                    yield RING * it + s, s, it

        @block.sync
        def _(sp):
            for n, s, it in steps(sp):
                row = settled(sp, n * P)
                wait(sp, vlo_done, n - 3)
                sp.dma_start(v[s][:], vexp[bass.ds(row, P), :]).then_inc(v_in[s], 16)
                wait(sp, wt_done, n - 3)
                sp.dma_start(a[s][:], acts[bass.ds(row, P), :]).then_inc(ag_in[s], 16)
                sp.dma_start(g[s][:], gmat[bass.ds(row, P), :]).then_inc(ag_in[s], 16)

        @block.scalar
        def _(act):
            for n, s, it in steps(act):
                act.wait_ge(v_in[s], 16 * (it + 1))
                wait(act, used, n - 1)
                act.activation(vhi[s % 2][:], v[s][:], ACT.Copy).then_inc(vhi_done, 1)
                act.wait_ge(wt_done, n + 1)
                act.activation(whi[s % 2][:], wt[s % 2][:], ACT.Copy).then_inc(whi_done, 1)

        @block.gpsimd
        def _(pool):
            for n, s, it in steps(pool):
                pool.wait_ge(vhi_done, n + 1)
                pool.tensor_tensor(vlo[s % 2][:], v[s][:], as_f32(vhi[s % 2][:]), ALU.subtract).then_inc(vlo_done, 1)

        @block.vector
        def _(dve):
            for n, s, it in steps(dve):
                dve.wait_ge(ag_in[s], 32 * (it + 1))
                wait(dve, wlo_done, n - 1)
                dve.tensor_tensor(wt[s % 2][:], a[s][:], g[s][:], ALU.mult).then_inc(wt_done, 1)
                dve.wait_ge(whi_done, n + 1)
                dve.tensor_tensor(wlo[s % 2][:], wt[s % 2][:], as_f32(whi[s % 2][:]), ALU.subtract).then_inc(wlo_done, 1)
            dve.wait_ge(used, NEXP)
            for t in range(NT):
                dve.tensor_copy(y[:, t, 0:T], out[t][0][:]).then_inc(y_done, 1)
                dve.tensor_copy(y[:, t, T:D], out[t][1][:]).then_inc(y_done, 1)

        @block.tensor
        def _(pe):
            for n, s, it in steps(pe):
                first, last = isinstance(n, int) and n == 0, isinstance(n, int) and n == NEXP - 1
                pe.wait_ge(vlo_done, n + 1)
                pe.wait_ge(wlo_done, n + 1)
                for t in range(NT):
                    ts = slice(t * P, (t + 1) * P)
                    for i, (w, m) in enumerate(((whi, vhi), (whi, vlo), (wlo, vhi))):
                        for h in range(2):
                            mm = pe.matmul(out[t][h][:], w[s % 2][:, ts], m[s % 2][:, h * T:(h + 1) * T],
                                           start=(first and i == 0), stop=(last and i == 2))
                mm.then_inc(used, 1)


def peer(nc, con, A, hT, x1, scores, acts, gmat, out):
    modulate_block(nc, "mod_b", con, x1, hT[0], hT[1], con.scale_b, 24)
    with Alloc(nc, "qry") as al:
        qry = al.sb("qry", [P, PH * HALVES, T])
        query_block(nc, A, hT, qry)
        scores_block(nc, con, A, qry, scores)
    experts_in_block(nc, con, A, hT, scores, acts, gmat)
    with Alloc(nc, "y") as al:
        y = al.sb("y", [P, NT, D])
        experts_out_block(nc, A, acts, gmat, y)
        residual_block(nc, "res_b", con, x1, y, con.gate_b, out)


def build_program(nc, A, out):
    Alloc.sems = []
    x1 = nc.dram_tensor("x1_scratch", (T, D), F32, kind="Internal").ap()
    scores = nc.dram_tensor("scores_scratch", (T, PH * HALVES * NK), F32, kind="Internal").ap()
    acts = nc.dram_tensor("act_scratch", (NK * NK, T), F32, kind="Internal").ap()
    gmat = nc.dram_tensor("gate_scratch", (NK * NK, T), F32, kind="Internal").ap()
    with Alloc(nc, "con") as al:
        con = Consts(al)
        hT = al.sb("h_hi", [P, KD, T], F32R), al.sb("h_lo", [P, KD, T], F32R)
        adaln_block(nc, con, A)
        mixer(nc, con, A, hT, x1)
        recycle_semaphores(nc)
        peer(nc, con, A, hT, x1, scores, acts, gmat, out.rearrange("b s d -> (b s) d"))


NAMES = ["x", "c", "w_ada", "b_ada", "g_pre_mix", "g_post_mix", "g_pre_ffn", "g_post_ffn", "w_in", "b_if", "conv_w",
         "conv_b", "m_head_gain", "lam_q1", "lam_k1", "lam_q2", "lam_k2", "d_head_gain", "w_br_m", "w_br_d", "w_out",
         "w_query", "sub_keys", "expert_u", "expert_v"]


def kernel(**inputs):
    import concourse.bacc as bacc
    from concourse.bass_utils import run_bass_kernel_spmd

    nc = bacc.Bacc("TRN2", target_bir_lowering=False, num_devices=1)
    arrays, views = {}, {}
    for name in NAMES:
        a = np.ascontiguousarray(inputs[name])
        arrays[f"in_{name}"] = a
        views[name] = nc.dram_tensor(f"in_{name}", a.shape, mybir.dt.from_np(a.dtype), kind="ExternalInput").ap()
    out = nc.dram_tensor("out", inputs["x"].shape, F32, kind="ExternalOutput").ap()
    build_program(nc, views, out)
    result = run_bass_kernel_spmd(nc, [arrays], core_ids=[0])
    return result.results[0]["out"]
```

```python
import math
from contextlib import ExitStack

import numpy as np

import concourse.bass as bass
from concourse import mybir

F32 = mybir.dt.float32
F32R = mybir.dt.float32r
U32 = mybir.dt.uint32
ALU = mybir.AluOpType
ACT = mybir.ActivationFunctionType
AX_X = mybir.AxisListType.X

P = 128
D = 1024
T = 512
KD = D // P
NT = T // P
EPS = 1e-6
HEADS = 4
DH = 256
DQK = 128
CHUNK = 64
CONV = 4
PH = 8
NK = 128
TOPK = 16
HALVES = 2
GC = 256
LAM_INIT = 0.8 - 0.6 * math.exp(-0.3 * 0)
NEG = -3.0e38

C_QK, C_MV, C_MO, C_IF = 0, 2 * D, 3 * D, 4 * D
C_DQ = C_IF + 2 * HEADS
C_DV, C_GM, C_GD = C_DQ + 2 * D, C_DQ + 3 * D, C_DQ + 4 * D

R_BADA, R_GPREMIX, R_GPOSTMIX, R_GPREFFN, R_GPOSTFFN, R_CONVB, R_C, NROWS_A = 0, 48, 56, 64, 72, 80, 96, 104
R_CONVW, R_MGAIN, R_DGAIN, NROWS_B = 0, 64, 72, 80


def wait(eng, sem, value):
    if isinstance(value, int) and value <= 0:
        return
    eng.wait_ge(sem, value)


def pairs(eng, count, peel, peel_last=False):
    first, end = int(peel), count - int(peel_last)
    if peel:
        yield 0
    if end == first + 1:
        yield first
    elif end > first:
        with eng.Fori(first, end) as it:
            yield it
    if peel_last and count > first:
        yield count - 1


def settled(eng, value):
    return value if isinstance(value, int) else eng.snap(value)


class Alloc:
    sems = []

    def __init__(self, nc, tag):
        self.nc, self.tag, self.stack = nc, tag, ExitStack()

    def __enter__(self):
        self.stack.__enter__()
        return self

    def __exit__(self, *a):
        return self.stack.__exit__(*a)

    def sb(self, name, shape, dt=F32):
        return self.stack.enter_context(self.nc.sbuf_tensor(f"{self.tag}_{name}", shape, dt))

    def ps(self, name, shape, dt=F32):
        return self.stack.enter_context(self.nc.psum_tensor(f"{self.tag}_{name}", shape, dt))

    def sem(self, name):
        Alloc.sems.append(self.nc.alloc_semaphore(f"{self.tag}_{name}"))
        return Alloc.sems[-1]

    def block(self):
        return self.stack.enter_context(self.nc.Block())


def recycle_semaphores(nc, keep):
    nc.clear_and_free_semaphores([sem for sem in Alloc.sems if sem not in keep])
    nc.all_engine_barrier()
    Alloc.sems = []


def as_f32(ap):
    return ap.bitcast(F32)


def columns(w, k=KD):
    return w.rearrange("(k p) n -> p k n", p=P)


def ada_columns(eng_sum, w_cols, silu_c, acc, step_done, count0):
    for k in range(KD):
        if k == 0:
            op = eng_sum.tensor_scalar(acc, w_cols[:, 0], silu_c[:, 0:1], None, ALU.mult)
        else:
            eng_sum.wait_ge(step_done, count0 + k)
            op = eng_sum.scalar_tensor_tensor(out=acc, in0=w_cols[:, k], scalar=silu_c[:, k:k + 1], in1=acc,
                                              op0=ALU.mult, op1=ALU.add)
        op.then_inc(step_done, 1)


def head_block(nc, con, slots, A, x_src, hi, lo):
    with Alloc(nc, "head") as al:
        rows_a = al.sb("rows_a", [NROWS_A, P])
        rows_b = al.sb("rows_b", [NROWS_B, P])
        sq = al.sb("sq", [P, 2])
        esum = al.sb("esum", [P, 2])
        groups = 2 * D // GC
        raw = al.sb("raw", [P, groups, KD, GC])
        acc = [al.sb(f"acc{i}", [P, GC]) for i in range(2)]
        x = al.sb("x", [P, NT, D])
        junk = al.sb("junk", [P, D])
        ss, ms, rstd = al.sb("ss", [P, NT]), al.sb("ms", [P, NT]), al.sb("rstd", [P, NT])
        h = al.sb("h", [P, 2, T])
        ps_t = al.ps("ps_t", [P, 512])
        ps_u = al.ps("ps_u", [P, 512])
        ps_ada = al.ps("ps_ada", [P, 512])
        ps_l = al.ps("ps_l", [P, 512])
        ps = [al.ps(f"ps{i}", [P, T]) for i in range(4)]
        rows_in, rows_b_in, consts, cols_ready, silu_ready = map(
            al.sem, ("rows_in", "rows_b_in", "consts", "cols_ready", "silu_ready"))
        a_turned, b_turned = al.sem("a_turned"), al.sem("b_turned")
        landed = [al.sem(f"landed{i}") for i in range(groups)]
        x_in = [al.sem(f"x_in{i}") for i in range(NT)]
        acc_step, summed_up, ada_done, scale_done, lam_in, lam_prod, lam_sum, lam_exp, lam_done = map(
            al.sem, ("acc_step", "summed_up", "ada_done", "scale_done", "lam_in", "lam_prod", "lam_sum", "lam_exp",
                     "lam_done"))
        summed, meaned, powed, normed, turned, modded, hi_done, lo_done = map(
            al.sem, ("summed", "meaned", "powed", "normed", "turned", "modded", "hi_done", "lo_done"))
        w = columns(A["w_ada"][0])
        block = al.block()

        @block.sync
        def _(sp):
            def rows(dst, r, src, n, sem):
                sp.dma_start(dst[r:r + n, :], src.rearrange("(r p) -> r p", p=P)).then_inc(sem, 16)

            rows(rows_a, R_BADA, A["b_ada"][0], 48, rows_in)
            rows(rows_a, R_GPREMIX, A["g_pre_mix"][0], 8, rows_in)
            rows(rows_a, R_GPOSTMIX, A["g_post_mix"][0], 8, rows_in)
            rows(rows_a, R_GPREFFN, A["g_pre_ffn"][0], 8, rows_in)
            rows(rows_a, R_GPOSTFFN, A["g_post_ffn"][0], 8, rows_in)
            rows(rows_a, R_CONVB, A["conv_b"][0], 16, rows_in)
            rows(rows_a, R_C, A["c"][0], 8, rows_in)
            for g in range(groups):
                sp.dma_start(raw[:, g], w[:, :, g * GC:(g + 1) * GC]).then_inc(landed[g], 16)
                if g < NT:
                    sp.dma_start(x[:, g], x_src[g * P:(g + 1) * P, :]).then_inc(x_in[g], 16)
            rows(rows_b, R_CONVW, A["conv_w"][0].rearrange("w c -> (w c)"), 64, rows_b_in)
            rows(rows_b, R_MGAIN, A["m_head_gain"][0], 8, rows_b_in)
            rows(rows_b, R_DGAIN, A["d_head_gain"][0], 8, rows_b_in)
            for n, name in enumerate(("lam_q1", "lam_q2", "lam_k1", "lam_k2")):
                sp.dma_start(con.lam_cols[:, n:n + 1], A[name].rearrange("a p -> p a")).then_inc(lam_in, 16)
            for n in range(2):
                sp.dma_start(con.gate_bias[:, n:n + 1],
                             A["b_if"][:, n * HEADS:(n + 1) * HEADS].rearrange("a h -> h a")).then_inc(lam_in, 16)
            slots.load_ahead(sp, w_group(A["w_in"][0], C_QK))

        @block.gpsimd
        def _(pool):
            pool.memset(con.ident[:], 0.0).then_inc(consts, 1)
            pool.memset(con.ones[:], 1.0).then_inc(consts, 1)
            pool.memset(con.pow_half[:], -0.5).then_inc(consts, 1)
            pool.memset(con.sel[:], 1.0).then_inc(consts, 1)
            pool.iota(con.iota[:], pattern=[[1, P]], base=0, channel_multiplier=0,
                      allow_small_or_imprecise_dtypes=True).then_inc(consts, 1)
            pool.wait_ge(consts, 5)
            pool.affine_select(out=con.ident[:], in_=con.ident[:], compare_op=ALU.not_equal, fill=1.0, base=0,
                               pattern=[[-1, P]], channel_multiplier=1).then_inc(consts, 1)
            pool.affine_select(out=con.sel[:], in_=con.sel[:], compare_op=ALU.is_equal, fill=0.0, base=0,
                               pattern=[[-1, HEADS], [0, P]], channel_multiplier=1).then_inc(consts, 1)
            pool.wait_ge(meaned, 1)
            pool.tensor_tensor(rstd[:], ms[:], con.pow_half[:, 0:NT], ALU.pow).then_inc(powed, 1)

        @block.tensor
        def _(pe):
            pe.wait_ge(consts, 7)
            pe.wait_ge(rows_in, 112)
            pe.transpose(ps_t[:, 0:NROWS_A], rows_a[:], con.ident[0:NROWS_A, 0:NROWS_A]).then_inc(a_turned, 1)

            def sum_columns(g):
                pe.wait_ge(acc_step, KD * (g + 1))
                for m in range(GC // P):
                    c = g * GC // P + m
                    mm = pe.matmul(ps_ada[:, c:c + 1], acc[g % 2][:, m * P:(m + 1) * P], con.ones[:, 0:1],
                                   start=True, stop=True)
                mm.then_inc(summed_up, 1)

            def turn(k):
                for t in range(NT):
                    mm = pe.transpose(ps[k % 4][:, t * P:(t + 1) * P], x[:, t, k * P:(k + 1) * P], con.ident[:])
                mm.then_inc(turned, 1)

            for g in range(groups - 1):
                sum_columns(g)
            pe.wait_ge(normed, NT)
            for k in range(4):
                turn(k)
            sum_columns(groups - 1)
            for k in range(4, KD):
                pe.wait_ge(modded, k - 3)
                turn(k)
            pe.wait_ge(rows_b_in, 48)
            pe.transpose(ps_u[:, 0:NROWS_B], rows_b[:], con.ident[0:NROWS_B, 0:NROWS_B]).then_inc(b_turned, 1)
            pe.wait_ge(lam_prod, 1)
            pe.matmul(ps_l[:, 0:2], con.ones[:], sq[:], start=True, stop=True).then_inc(lam_sum, 1)

        @block.scalar
        def _(act):
            act.wait_ge(cols_ready, 1)
            act.activation(con.silu_c[:], con.cols_a[:, R_C:R_C + KD], ACT.Silu).then_inc(silu_ready, 1)
            for t in range(NT):
                act.wait_ge(x_in[t], 16)
                if t:
                    act.wait_ge(summed, t)
                act.activation(junk[:], x[:, t], ACT.Square, accum_out=ss[:, t:t + 1]).then_inc(summed, 1)
            act.wait_ge(scale_done, 1)
            for k in range(KD):
                act.wait_ge(turned, k + 1)
                if k >= 2:
                    act.wait_ge(lo_done, k - 1)
                act.activation(h[:, k % 2], ps[k % 4][:], ACT.Identity, bias=con.ada[:, k:k + 1],
                               scale=con.scale_a[:, k:k + 1]).then_inc(modded, 1)
            act.wait_ge(lam_sum, 1)
            act.activation(esum[:], ps_l[:, 0:2], ACT.Exp).then_inc(lam_exp, 1)

        @block.vector
        def _(dve):
            dve.wait_ge(a_turned, 1)
            dve.tensor_copy(con.cols_a[:], ps_t[:, 0:NROWS_A]).then_inc(cols_ready, 1)
            dve.wait_ge(silu_ready, 1)
            for g in range(groups):
                dve.wait_ge(landed[g], 16)
                wait(dve, summed_up, g - 1)
                ada_columns(dve, raw[:, g], con.silu_c, acc[g % 2][:], acc_step, KD * g)
                if g == NT:
                    dve.wait_ge(summed, NT)
                    dve.tensor_scalar(ms[:], ss[:], 1.0 / D, EPS, ALU.mult, ALU.add).then_inc(meaned, 1)
                if g == NT + 1:
                    dve.wait_ge(powed, 1)
                    for t in range(NT):
                        dve.tensor_scalar(x[:, t], x[:, t], rstd[:, t:t + 1], None, ALU.mult).then_inc(normed, 1)
            dve.wait_ge(summed_up, groups)
            dve.tensor_tensor(con.ada[:, 0:16], ps_ada[:, 0:16], con.cols_a[:, 0:16], ALU.add).then_inc(ada_done, 1)
            dve.wait_ge(ada_done, 1)
            dve.scalar_tensor_tensor(out=con.scale_a[:], in0=con.ada[:, 8:16], scalar=1.0,
                                     in1=con.cols_a[:, R_GPREMIX:R_GPREMIX + 8], op0=ALU.add,
                                     op1=ALU.mult).then_inc(scale_done, 1)
            for k in range(KD):
                dve.wait_ge(modded, k + 1)
                dve.tensor_copy(hi[:, k], h[:, k % 2]).then_inc(hi_done, 1)
                dve.wait_ge(hi_done, k + 1)
                dve.tensor_tensor(lo[:, k], h[:, k % 2], as_f32(hi[:, k]), ALU.subtract).then_inc(lo_done, 1)
            dve.wait_ge(b_turned, 1)
            dve.tensor_copy(con.cols_b[:], ps_u[:, 0:NROWS_B]).then_inc(cols_ready, 1)
            dve.wait_ge(lam_in, 96)
            dve.tensor_tensor(sq[:], con.lam_cols[:, 0:2], con.lam_cols[:, 2:4], ALU.mult).then_inc(lam_prod, 1)
            dve.wait_ge(cols_ready, 2)
            dve.tensor_scalar(con.cols_b[:, R_DGAIN:R_DGAIN + KD], con.cols_b[:, R_DGAIN:R_DGAIN + KD],
                              1.0 - LAM_INIT, None, ALU.mult).then_inc(lam_done, 1)
            dve.wait_ge(lam_exp, 1)
            dve.scalar_tensor_tensor(out=con.lam[:], in0=esum[:, 0:1], scalar=LAM_INIT, in1=esum[:, 1:2],
                                     op0=ALU.add, op1=ALU.subtract).then_inc(lam_done, 1)


def modulate_block(nc, con, x, stored, hi, lo, scale, shift0, slots, following):
    with Alloc(nc, "mod") as al:
        xn = al.sb("xn", [P, NT, D])
        junk = al.sb("junk", [P, D])
        ss = al.sb("ss", [P, NT])
        ms = al.sb("ms", [P, NT])
        rstd = al.sb("rstd", [P, NT])
        h = al.sb("h", [P, 2, T])
        ps = [al.ps(f"ps{i}", [P, T]) for i in range(2)]
        summed, meaned, powed, normed, turned, modded, hi_done, lo_done = map(
            al.sem, ("summed", "meaned", "powed", "normed", "turned", "modded", "hi_done", "lo_done"))
        block = al.block()

        @block.sync
        def _(sp):
            slots.load_ahead(sp, following)
            sp.wait_ge(stored, 16 * NT)

        @block.scalar
        def _(act):
            for t in range(NT):
                if t:
                    act.wait_ge(summed, t)
                act.activation(junk[:], x[:, t], ACT.Square, accum_out=ss[:, t:t + 1]).then_inc(summed, 1)
            for k in range(KD):
                act.wait_ge(turned, k + 1)
                if k >= 2:
                    act.wait_ge(lo_done, k - 1)
                act.activation(h[:, k % 2], ps[k % 2][:], ACT.Identity, bias=con.ada[:, shift0 + k:shift0 + k + 1],
                               scale=scale[:, k:k + 1]).then_inc(modded, 1)

        @block.gpsimd
        def _(pool):
            pool.wait_ge(meaned, 1)
            pool.tensor_tensor(rstd[:], ms[:], con.pow_half[:, 0:NT], ALU.pow).then_inc(powed, 1)

        @block.vector
        def _(dve):
            dve.wait_ge(summed, NT)
            dve.tensor_scalar(ms[:], ss[:], 1.0 / D, EPS, ALU.mult, ALU.add).then_inc(meaned, 1)
            dve.wait_ge(powed, 1)
            for t in range(NT):
                dve.tensor_scalar(xn[:, t], x[:, t], rstd[:, t:t + 1], None, ALU.mult).then_inc(normed, 1)
            for k in range(KD):
                dve.wait_ge(modded, k + 1)
                dve.tensor_copy(hi[:, k], h[:, k % 2]).then_inc(hi_done, 1)
                dve.wait_ge(hi_done, k + 1)
                dve.tensor_tensor(lo[:, k], h[:, k % 2], as_f32(hi[:, k]), ALU.subtract).then_inc(lo_done, 1)

        @block.tensor
        def _(pe):
            pe.wait_ge(normed, NT)
            for k in range(KD):
                if k >= 2:
                    pe.wait_ge(modded, k - 1)
                for t in range(NT):
                    mm = pe.transpose(ps[k % 2][:, t * P:(t + 1) * P], xn[:, t, k * P:(k + 1) * P], con.ident[:])
                mm.then_inc(turned, 1)


class Slots:

    def __init__(self, al):
        self.raw = [al.sb(f"raw{i}", [P, KD, GC]) for i in range(2)]
        self.landed = [al.sem(f"landed{i}") for i in range(2)]
        self.loads = 0

    def load_ahead(self, sp, load):
        for s in range(2):
            sp.dma_start(self.raw[s][:], load(sp, 0, s)).then_inc(self.landed[s], 16)


def project_block(nc, tag, slots, sections, make, ada=None, following=None):
    with Alloc(nc, tag) as al:
        raw, landed, base = slots.raw, slots.landed, 16 * slots.loads
        whi = [al.sb(f"whi{i}", [P, KD, GC], F32R) for i in range(2)]
        wlo = [al.sb(f"wlo{i}", [P, KD, GC], F32R) for i in range(2)]
        bank = [al.ps(f"bank{i}", [P, 512]) for i in range(4)]
        half_hi, half_lo = al.sem("half_hi"), al.sem("half_lo")
        w_hi, w_lo, units = al.sem("w_hi"), al.sem("w_lo"), al.sem("units")
        freed = [al.sem(f"freed{i}") for i in range(4)]
        al.freed = freed
        empty_vector, empty_scalar = make(al)
        if ada:
            con, A, ada0 = ada
            w_ada = columns(A["w_ada"][0])
            ada_w, acc = al.sb("ada_w", [P, KD, GC]), [al.sb(f"acc{i}", [P, GC]) for i in range(2)]
            ps_ada = al.ps("ps_ada", [P, 512])
            ada_in, acc_step, summed_up, ada_done = map(al.sem, ("ada_in", "acc_step", "summed_up", "ada_done"))
        plan, g0, u0 = [], 0, 0
        for kind, groups, load, operand in sections:
            per = {"T": 2, "T1": 1, "N": 4}[kind]
            plan.append((kind, groups, load, operand, g0, u0, per))
            g0, u0 = g0 + groups, u0 + groups * per
        slots.loads += g0 // 2
        lower, upper = slice(0, KD // 2), slice(KD // 2, KD)

        block = al.block()

        @block.sync
        def _(sp):
            for kind, groups, load, operand, gb, ub, per in plan:
                for it in range(groups // 2):
                    for s in range(2):
                        if not (isinstance(it, int) and gb + it == 0):
                            src = load(sp, it, s)
                            if isinstance(it, int) and gb + 2 * it + s == 2:
                                sp.wait_ge(half_lo, 1)
                            wait(sp, w_lo, gb + 2 * it + s - 1)
                            sp.dma_start(raw[s][:], src).then_inc(landed[s], 16)
                        if ada and gb == 0:
                            wait(sp, acc_step, KD * (2 * it + s))
                            col = ada0 * P + (2 * it + s) * GC
                            sp.dma_start(ada_w[:], w_ada[:, :, col:col + GC]).then_inc(ada_in, 16)
            if following:
                sp.wait_ge(w_lo, g0)
                slots.load_ahead(sp, following)

        @block.gpsimd
        def _(pool):
            pool.wait_ge(half_hi, 1)
            pool.tensor_tensor(wlo[0][:, lower], raw[0][:, lower], as_f32(whi[0][:, lower]),
                               ALU.subtract).then_inc(w_lo, 1)
            for kind, groups, load, operand, gb, ub, per in plan:
                for it in pairs(pool, groups // 2, gb == 0):
                    for s in range(2):
                        if isinstance(it, int) and gb + 2 * it + s == 0:
                            continue
                        pool.wait_ge(w_hi, gb + 2 * it + s + 1)
                        pool.tensor_tensor(wlo[s][:], raw[s][:], as_f32(whi[s][:]), ALU.subtract).then_inc(w_lo, 1)

        @block.tensor
        def _(pe):
            for kind, groups, load, operand, gb, ub, per in plan:
                for it in pairs(pe, groups // 2, gb == 0):
                    for s in range(2):
                        if isinstance(it, int) and gb + 2 * it + s == 0:
                            pe.wait_ge(half_lo, 1)
                        pe.wait_ge(w_lo, gb + 2 * it + s + 1)
                        xh, xl = operand(s)
                        for c in range(per):
                            b = (s * per + c) % 4
                            use = (ub + s * per + c) // 4 + it * (2 * per // 4)
                            wait(pe, freed[b], use)
                            for k in range(KD):
                                if kind != "N":
                                    cs = slice(c * P, (c + 1) * P)
                                    ops = ((whi[s][:, k, cs], xh[:, k, :]), (whi[s][:, k, cs], xl[:, k, :]),
                                           (wlo[s][:, k, cs], xh[:, k, :]))
                                    out = bank[b][:]
                                else:
                                    ts = slice(c * P, (c + 1) * P)
                                    ops = ((xh[:, k, ts], whi[s][:, k, :]), (xh[:, k, ts], wlo[s][:, k, :]),
                                           (xl[:, k, ts], whi[s][:, k, :]))
                                    out = bank[b][:, 0:GC]
                                for n, (a, m) in enumerate(ops):
                                    mm = pe.matmul(out, a, m, start=(k == 0 and n == 0), stop=(k == KD - 1 and n == 2))
                            mm.then_inc(units, 1)
                        if ada and gb == 0:
                            pe.wait_ge(acc_step, KD * (2 * it + s + 1))
                            for m in range(2):
                                mm = pe.matmul(ps_ada[:, bass.ds(4 * it + 2 * s + m, 1)],
                                               acc[s][:, m * P:(m + 1) * P], con.ones[:, 0:1], start=True, stop=True)
                            mm.then_inc(summed_up, 1)

        def view(eng):
            for sec, (kind, groups, load, operand, gb, ub, per) in enumerate(plan):
                for it in pairs(eng, groups // 2, True, sec == len(plan) - 1):
                    for s in range(2):
                        first = ub + (2 * it + s) * per
                        last_group = isinstance(it, int) and gb + 2 * it + s + 1 == g0
                        if eng is nc.vector and not last_group:
                            o = 1 - s
                            eng.wait_ge(landed[o], base + 16 * (gb // 2 + it + s + 1))
                            wait(eng, units, first)
                            eng.tensor_copy(whi[o][:], raw[o][:]).then_inc(w_hi, 1)
                        if ada and gb == 0 and eng is nc.vector:
                            n = 2 * it + s
                            eng.wait_ge(ada_in, 16 * (n + 1))
                            wait(eng, summed_up, n - 1)
                            ada_columns(eng, ada_w, con.silu_c, acc[s][:], acc_step, KD * n)
                        for c in range(per):
                            b = (s * per + c) % 4
                            yield sec, it, s, c, first + c, bank[b], freed[b]

        @block.vector
        def _(dve):
            dve.wait_ge(landed[0], base + 16)
            dve.tensor_copy(whi[0][:, lower], raw[0][:, lower]).then_inc(half_hi, 1)
            dve.tensor_copy(whi[0][:, upper], raw[0][:, upper]).then_inc(w_hi, 1)
            dve.wait_ge(w_hi, 1)
            dve.tensor_tensor(wlo[0][:, upper], raw[0][:, upper], as_f32(whi[0][:, upper]),
                              ALU.subtract).then_inc(half_lo, 1)
            empty_vector(dve, view(dve), units)
            if ada:
                n = 2 * plan[0][1]
                dve.wait_ge(summed_up, plan[0][1])
                dve.tensor_tensor(con.ada[:, ada0:ada0 + n], ps_ada[:, 0:n], con.cols_a[:, ada0:ada0 + n],
                                  ALU.add).then_inc(ada_done, 1)
                if ada0 + n == 6 * KD:
                    dve.wait_ge(ada_done, 1)
                    dve.scalar_tensor_tensor(out=con.scale_b[:], in0=con.ada[:, 32:40], scalar=1.0,
                                             in1=con.cols_a[:, R_GPREFFN:R_GPREFFN + 8], op0=ALU.add, op1=ALU.mult)
                    for dst, gain, gate in ((con.gate_a, R_GPOSTMIX, 16), (con.gate_b, R_GPOSTFFN, 40)):
                        dve.tensor_tensor(dst[:], con.ada[:, gate:gate + 8], con.cols_a[:, gain:gain + 8], ALU.mult)

        @block.scalar
        def _(act):
            empty_scalar(act, view(act), units)


def w_group(w, col0, step=GC):
    v = columns(w)

    def load(sp, it, s):
        return v[:, :, bass.ds(settled(sp, col0 + it * 2 * GC + s * step), GC)]
    return load


def mlstm_inputs_block(nc, con, slots, A, hT, qk, v, out_gate, gates):
    w = A["w_in"][0]

    def make(al):
        acc = [al.sb(f"acc{i}", [P, T]) for i in range(2)]
        conv, silu_done = al.sem("conv"), al.sem("silu_done")

        def vector(dve, units_of, units):
            for sec, it, s, c, u, bank, freed in units_of:
                if sec == 2:
                    continue
                dve.wait_ge(units, u + 1)
                if sec == 0:
                    ch = 4 * it + 2 * s + c
                    wait(dve, silu_done, ch - 1)
                    dve.tensor_scalar(acc[c][:], bank[:], con.cols_b[:, bass.ds(R_CONVW + 48 + ch, 1)],
                                      con.cols_a[:, bass.ds(R_CONVB + ch, 1)], ALU.mult, ALU.add).then_inc(conv, 1)
                    for j in range(1, CONV):
                        dve.wait_ge(conv, 3 * ch + j)
                        op = dve.scalar_tensor_tensor(
                            out=acc[c][:, j:], in0=bank[:, 0:T - j],
                            scalar=con.cols_b[:, bass.ds(R_CONVW + 16 * (3 - j) + ch, 1)],
                            in1=acc[c][:, j:], op0=ALU.mult, op1=ALU.add)
                        op.then_inc(conv if j < 3 else freed, 1)
                elif sec == 1:
                    dve.tensor_copy(v[:, c, bass.ds(2 * it + s, 1), 0:DH],
                                    bank[:, 0:DH].rearrange("p (a d) -> p a d", a=1)).then_inc(freed, 1)
                else:
                    dve.tensor_scalar(gates[:, s], bank[0:HEADS, :], con.gate_bias[:, s:s + 1], None,
                                      ALU.add).then_inc(freed, 1)

        def scalar(act, units_of, units):
            for sec, it, s, c, u, bank, freed in units_of:
                if sec == 0:
                    act.wait_ge(freed, it + 1)
                    act.activation(qk[:, bass.ds(4 * it + 2 * s + c, 1), :], acc[c][:].rearrange("p (a t) -> p a t", a=1),
                                   ACT.Silu).then_inc(silu_done, 1)
                elif sec == 2:
                    act.wait_ge(units, u + 1)
                    act.activation(out_gate[:, bass.ds(4 * it + 2 * s + c, 1), :],
                                   bank[:].rearrange("p (a t) -> p a t", a=1), ACT.Sigmoid).then_inc(freed, 1)
        return vector, scalar

    op = lambda s: hT
    project_block(nc, "proj_m", slots, [("T", 8, w_group(w, C_QK), op), ("N", 4, w_group(w, C_MV), op),
                                 ("T", 4, w_group(w, C_MO), op), ("T1", 2, w_group(w, C_IF, HEADS), op)], make,
                  following=branch_load(A, C_GM, "w_br_m"))


def mlstm_block(nc, con, qk, v, out_gate, gates, y_hi, y_lo):
    H = HEADS
    steps = [(h, i) for h in range(H) for i in range(NT)]
    with Alloc(nc, "mlstm") as al:
        lf, fsum, a, g, ones4 = [al.sb(n, [H, T]) for n in ("lf", "fsum", "a", "g", "ones4")]
        absf = expf = logf = lf
        nm = fsum
        a_col, floor = al.sb("a_col", [P, NT, H]), al.sb("floor", [P, NT, H])
        ex = [al.sb(f"ex{i}", [P, T]) for i in range(2)]
        ee = [al.sb(f"ee{i}", [P, T]) for i in range(2)]
        pt = [al.sb(f"pt{i}", [P, T]) for i in range(2)]
        pos, den, rden = al.sb("pos", [P, NT]), al.sb("den", [P, NT]), al.sb("rden", [P, NT])
        cell, y, junk = al.sb("cell", [P, NT, DH]), al.sb("y", [P, NT, DH]), al.sb("junk", [P, DH])
        ss, ms, rstd = al.sb("ss", [P, NT]), al.sb("ms", [P, NT]), al.sb("rstd", [P, NT])
        tmp = al.sb("tmp", [P, 2, T])
        ps_g, ps_t = al.ps("ps_g", [P, T]), al.ps("ps_t", [P, T])
        ps_s = [al.ps(f"ps_s{i}", [P, T]) for i in range(2)]
        ps_n = [al.ps(f"ps_n{i}", [P, T]) for i in range(NT)]
        (act_pre, dve_pre, ones_done, cols_t, col_done, floor_done, gb_done, ex_done, ee_done, mask_done, s_done,
         pt_done, pv_done, den_done, cell_done, ss_done, ms_done, pow_done, y_done, tr_done, tmp_done, hi_done,
         lo_done) = map(al.sem, (
             "act_pre", "dve_pre", "ones_done", "cols_t", "col_done", "floor_done", "gb_done", "ex_done", "ee_done",
             "mask_done", "s_done", "pt_done", "pv_done", "den_done", "cell_done", "ss_done", "ms_done", "pow_done",
             "y_done", "tr_done", "tmp_done", "hi_done", "lo_done"))
        block = al.block()

        @block.scalar
        def _(act):
            act.activation(absf[:], gates[:, 1], ACT.Abs).then_inc(act_pre, 1)
            act.wait_ge(act_pre, 1)
            act.activation(expf[:], absf[:], ACT.Exp, scale=-1.0).then_inc(act_pre, 1)
            act.wait_ge(act_pre, 2)
            act.activation(logf[:], expf[:], ACT.Ln, bias=1.0).then_inc(act_pre, 1)
            act.wait_ge(col_done, 1)
            act.activation(floor[:], ps_t[:, NT * H:2 * NT * H].rearrange("p (t h) -> p t h", h=H),
                           ACT.Exp).then_inc(floor_done, 1)
            for n, (h, i) in enumerate(steps):
                w = T - i * P
                act.wait_ge(ex_done, n + 1)
                if n >= 2:
                    act.wait_ge(pt_done, n - 1)
                act.activation(ee[n % 2][:, 0:w], ex[n % 2][:, 0:w], ACT.Exp, scale=-1.0).then_inc(ee_done, 1)
                if i == NT - 1:
                    for j in range(NT):
                        act.wait_ge(cell_done, NT * h + j + 1)
                        wait(act, ss_done, NT * h + j)
                        act.activation(junk[:], cell[:, j], ACT.Square, accum_out=ss[:, j:j + 1]).then_inc(ss_done, 1)
                    for c in range(2):
                        act.wait_ge(tmp_done, 2 * h + c + 1)
                        act.activation(y_hi[:, 2 * h + c], tmp[:, c], ACT.Copy).then_inc(hi_done, 1)

        @block.gpsimd
        def _(pool):
            pool.memset(ones4[:], 1.0).then_inc(ones_done, 1)
            pool.memset(v[:, :, :, DH:DH + 1], 1.0).then_inc(ones_done, 1)
            for n, (h, i) in enumerate(steps):
                pool.wait_ge(ee_done, n + 1)
                pool.affine_select(out=ee[n % 2][:, 0:P], in_=ee[n % 2][:, 0:P], compare_op=ALU.is_ge, fill=0.0,
                                   base=0, pattern=[[1, P]], channel_multiplier=-1).then_inc(mask_done, 1)
                if i == NT - 1:
                    pool.wait_ge(ms_done, h + 1)
                    pool.tensor_tensor(rstd[:], ms[:], con.pow_half[:, 0:NT], ALU.pow).then_inc(pow_done, 1)

        @block.tensor
        def _(pe):
            pe.wait_ge(dve_pre, 5)
            for t in range(NT):
                pe.transpose(ps_t[:, t * H:(t + 1) * H], a[:, t * P:(t + 1) * P], con.ident[0:H, 0:H])
            for t in range(NT):
                mm = pe.transpose(ps_t[:, (NT + t) * H:(NT + t + 1) * H], nm[:, t * P:(t + 1) * P],
                                  con.ident[0:H, 0:H])
            mm.then_inc(cols_t, 1)

            def scores(n):
                h, i = steps[n]
                if i == 0:
                    wait(pe, ex_done, n)
                    pe.matmul(ps_g[:], con.sel[:, h, :], g[:], start=True, stop=True).then_inc(gb_done, 1)
                wait(pe, pt_done, n - 1)
                for k in range(2):
                    mm = pe.matmul(ps_s[n % 2][:, 0:T - i * P], qk[:, 8 + 2 * h + k, i * P:(i + 1) * P],
                                   qk[:, 2 * h + k, i * P:T], start=(k == 0), stop=(k == 1))
                mm.then_inc(s_done, 1)

            scores(0)
            pe.wait_ge(ones_done, 2)
            for n, (h, i) in enumerate(steps):
                if n + 1 < len(steps):
                    scores(n + 1)
                pe.wait_ge(pt_done, n + 1)
                if i == 0:
                    wait(pe, cell_done, NT * h)
                for j in range(i, NT):
                    mm = pe.matmul(ps_n[j][:, 0:DH + 1], pt[n % 2][:, (j - i) * P:(j - i + 1) * P], v[:, i, h, :],
                                   start=(i == 0), stop=(i == j))
                mm.then_inc(pv_done, 1)
                if i == NT - 1:
                    pe.wait_ge(y_done, NT * (h + 1))
                    for c in range(2):
                        wait(pe, tmp_done, 2 * h + c)
                        if h == 0 and c == 0:
                            pe.wait_ge(col_done, 1)
                            pe.wait_ge(floor_done, 1)
                        for j in range(NT):
                            mm = pe.transpose(ps_t[:, j * P:(j + 1) * P], y[:, j, c * P:(c + 1) * P], con.ident[:])
                        mm.then_inc(tr_done, 1)

        @block.vector
        def _(dve):
            dve.wait_ge(act_pre, 3)
            dve.scalar_tensor_tensor(out=lf[:], in0=gates[:, 1], scalar=0.0, in1=logf[:], op0=ALU.min,
                                     op1=ALU.subtract).then_inc(dve_pre, 1)
            dve.wait_ge(ones_done, 1)
            dve.wait_ge(dve_pre, 1)
            dve.tensor_tensor_scan(fsum[:], ones4[:], lf[:], 0.0, ALU.mult, ALU.add).then_inc(dve_pre, 1)
            dve.wait_ge(dve_pre, 2)
            dve.tensor_tensor(a[:], gates[:, 0], fsum[:], ALU.subtract).then_inc(dve_pre, 1)
            dve.wait_ge(dve_pre, 3)
            dve.tensor_tensor_scan(g[:], a[:], a[:], 0.0, ALU.max, ALU.max).then_inc(dve_pre, 1)
            dve.wait_ge(dve_pre, 4)
            dve.scalar_tensor_tensor(out=nm[:], in0=fsum[:], scalar=-1.0, in1=g[:], op0=ALU.mult,
                                     op1=ALU.subtract).then_inc(dve_pre, 1)
            dve.wait_ge(cols_t, 1)
            dve.tensor_copy(a_col[:], ps_t[:, 0:NT * H].rearrange("p (t h) -> p t h", h=H)).then_inc(col_done, 1)
            dve.wait_ge(col_done, 1)

            def exponents(n):
                h, i = steps[n]
                w = T - i * P
                dve.wait_ge(gb_done, h + 1)
                wait(dve, ee_done, n - 1)
                dve.tensor_scalar(ex[n % 2][:, 0:w], ps_g[:, i * P:T], a_col[:, i, h:h + 1], 0.0, ALU.subtract,
                                  ALU.max).then_inc(ex_done, 1)

            exponents(0)
            for n, (h, i) in enumerate(steps):
                w = T - i * P
                if n + 1 < len(steps):
                    exponents(n + 1)
                dve.wait_ge(s_done, n + 1)
                dve.wait_ge(mask_done, n + 1)
                wait(dve, pv_done, n - 1)
                dve.scalar_tensor_tensor(out=pt[n % 2][:, 0:w], in0=ps_s[n % 2][:, 0:w], scalar=DH ** -0.5,
                                         in1=ee[n % 2][:, 0:w], op0=ALU.mult, op1=ALU.mult).then_inc(pt_done, 1)
                if i < NT - 1:
                    continue
                dve.wait_ge(floor_done, 1)
                dve.wait_ge(pv_done, n + 1)
                for j in range(NT):
                    dve.tensor_tensor(pos[:, j:j + 1], ps_n[j][:, DH:DH + 1], floor[:, j, h:h + 1],
                                      ALU.max).then_inc(den_done, 1)
                dve.wait_ge(den_done, 9 * h + 4)
                for j in range(NT):
                    dve.scalar_tensor_tensor(out=den[:, j:j + 1], in0=ps_n[j][:, DH:DH + 1], scalar=-1.0,
                                             in1=pos[:, j:j + 1], op0=ALU.mult, op1=ALU.max).then_inc(den_done, 1)
                dve.wait_ge(den_done, 9 * h + 8)
                dve.reciprocal(rden[:], den[:]).then_inc(den_done, 1)
                dve.wait_ge(den_done, 9 * h + 9)
                for j in range(NT):
                    wait(dve, y_done, NT * h)
                    dve.tensor_scalar(cell[:, j], ps_n[j][:, 0:DH], rden[:, j:j + 1], None,
                                      ALU.mult).then_inc(cell_done, 1)
                dve.wait_ge(ss_done, NT * (h + 1))
                dve.tensor_scalar(ms[:], ss[:], 1.0 / DH, EPS, ALU.mult, ALU.add).then_inc(ms_done, 1)
                dve.wait_ge(pow_done, h + 1)
                for j in range(NT):
                    dve.tensor_scalar(y[:, j], cell[:, j], rstd[:, j:j + 1], None, ALU.mult).then_inc(y_done, 1)
                for c in range(2):
                    dve.wait_ge(tr_done, 2 * h + c + 1)
                    wait(dve, lo_done, 2 * h)
                    dve.scalar_tensor_tensor(out=tmp[:, c], in0=ps_t[:],
                                             scalar=con.cols_b[:, R_MGAIN + 2 * h + c:R_MGAIN + 2 * h + c + 1],
                                             in1=out_gate[:, 2 * h + c], op0=ALU.mult, op1=ALU.mult).then_inc(tmp_done, 1)
                for c in range(2):
                    dve.wait_ge(hi_done, 2 * h + c + 1)
                    dve.tensor_tensor(y_lo[:, 2 * h + c], tmp[:, c], as_f32(y_hi[:, 2 * h + c]),
                                      ALU.subtract).then_inc(lo_done, 1)


def branch_load(A, gate_col, name):
    branch, gates = columns(A[name][0]), columns(A["w_in"][0])

    def load(sp, it, s):
        return branch[:, :, bass.ds(it * GC, GC)] if s else gates[:, :, bass.ds(gate_col + it * GC, GC)]
    return load


def gated_branch_block(nc, tag, slots, load, hT, y, merged, following, m_hl=None, ada=None):
    def make(al):
        freed_bank = lambda b: al.freed[b]
        sg = [al.sb(f"sg{i}", [P, T]) for i in range(2)]
        prod = [al.sb(f"prod{i}", [P, T]) for i in range(2)]
        added, m_hi_done = al.sem("added"), al.sem("m_hi_done")
        m_lo_done = al.sem("m_lo_done")
        freed_by = {}

        def vector(dve, units_of, units):
            for sec, it, s, c, u, bank, freed in units_of:
                freed_by[s, c] = freed
                if s == 0:
                    continue
                ch = 2 * it + c
                dve.wait_ge(units, u + 1)
                dve.wait_ge(freed_by[0, c], it + 1)
                out = merged[:, bass.ds(ch, 1), :]
                sg3 = sg[c][:].rearrange("p (a t) -> p a t", a=1)
                bank3 = bank[:].rearrange("p (a t) -> p a t", a=1)
                if m_hl is None:
                    dve.tensor_tensor(out, bank3, sg3, ALU.mult).then_inc(freed, 1)
                else:
                    p3 = prod[c][:].rearrange("p (a t) -> p a t", a=1)
                    wait(dve, m_lo_done, ch - 1)
                    dve.tensor_tensor(p3, bank3, sg3, ALU.mult).then_inc(freed, 1)
                    dve.wait_ge(freed, it + 1)
                    dve.tensor_tensor(p3, p3, out, ALU.add).then_inc(added, 1)
                    dve.wait_ge(added, ch + 1)
                    hi3, lo3 = m_hl[0][:, bass.ds(ch, 1), :], m_hl[1][:, bass.ds(ch, 1), :]
                    dve.tensor_copy(hi3, p3).then_inc(m_hi_done, 1)
                    dve.wait_ge(m_hi_done, ch + 1)
                    dve.tensor_tensor(lo3, p3, as_f32(hi3), ALU.subtract).then_inc(m_lo_done, 1)

        def scalar(act, units_of, units):
            seen = {}
            for sec, it, s, c, u, bank, freed in units_of:
                if s:
                    continue
                act.wait_ge(units, u + 1)
                wait(act, freed_bank(2 + c), it)
                act.activation(sg[c][:], bank[:], ACT.Sigmoid).then_inc(freed, 1)
        return vector, scalar

    project_block(nc, tag, slots, [("T", 8, load, lambda s: y if s else hT)], make, ada, following)


def attention_inputs_block(nc, con, slots, A, hT, qk, v):
    w = A["w_in"][0]

    def make(al):
        def vector(dve, units_of, units):
            for sec, it, s, c, u, bank, freed in units_of:
                if sec == 1:
                    dve.wait_ge(units, u + 1)
                    dve.tensor_copy(v[:, c, bass.ds(2 * it + s, 1), 0:DH],
                                    bank[:, 0:DH].rearrange("p (a d) -> p a d", a=1)).then_inc(freed, 1)

        def scalar(act, units_of, units):
            for sec, it, s, c, u, bank, freed in units_of:
                if sec == 0:
                    act.wait_ge(units, u + 1)
                    act.activation(qk[:, bass.ds(4 * it + 2 * s + c, 1), :],
                                   bank[:].rearrange("p (a t) -> p a t", a=1), ACT.Copy).then_inc(freed, 1)
        return vector, scalar

    op = lambda s: hT
    project_block(nc, "proj_d", slots, [("T", 8, w_group(w, C_DQ), op), ("N", 4, w_group(w, C_DV), op)], make,
                  (con, A, 32), branch_load(A, C_GD, "w_br_d"))


def attention_block(nc, con, qk, v, y_hi, y_lo):
    scale = DQK ** -0.5
    steps = [(h, j) for h in range(HEADS) for j in range(NT)]
    N = len(steps)

    def ended(n):
        return [(steps[n - 1 - c][0], c) for c in range(2) if 0 <= n - 1 - c < N and steps[n - 1 - c][1] == NT - 1]

    with Alloc(nc, "attn") as al:
        p = [[al.sb(f"p{i}{c}", [P, T]) for c in range(2)] for i in range(2)]
        mx, nb, sm, rs = [[al.sb(f"{n}{i}", [P, 2]) for i in range(2)] for n in ("mx", "nb", "sm", "rs")]
        p1w, aw, awt = al.sb("p1w", [P, T]), al.sb("aw", [P, T]), al.sb("awt", [P, T])
        y = [al.sb(f"y{i}", [P, NT, DH]) for i in range(2)]
        junk = al.sb("junk", [P, DH])
        ss, ms, rstd = [[al.sb(f"{n}{i}", [P, 1]) for i in range(2)] for n in ("ss", "ms", "rstd")]
        ps_s = [[al.ps(f"ps_s{i}{c}", [P, T]) for c in range(2)] for i in range(2)]
        ps_t, ps_y = al.ps("ps_t", [P, T]), al.ps("ps_y", [P, T])
        ps_o = [al.ps(f"ps_o{i}", [P, T]) for i in range(2)]
        (s_done, masked, max_done, nb_done, p_done, rs_done, w_done, p1_done, a_done, at_done, awt_done, o_done,
         ss_done, ms_done, pow_done, y_done, tr_done, hi_done, lo_done) = map(al.sem, (
             "s_done", "masked", "max_done", "nb_done", "p_done", "rs_done", "w_done", "p1_done", "a_done", "at_done",
             "awt_done", "o_done", "ss_done", "ms_done", "pow_done", "y_done", "tr_done", "hi_done", "lo_done"))
        block = al.block()

        @block.tensor
        def _(pe):
            def scores(n):
                h, j = steps[n]
                wait(pe, p_done, 2 * (n - 1))
                for c in range(2):
                    pe.matmul(ps_s[n % 2][c][:, 0:(j + 1) * P], qk[:, 2 * h + c, j * P:(j + 1) * P],
                              qk[:, 8 + 2 * h + c, 0:(j + 1) * P], start=True, stop=True).then_inc(s_done, 1)

            def output(n):
                h, j = steps[n]
                pe.wait_ge(a_done, n + 1)
                wait(pe, awt_done, n)
                for i in range(j + 1):
                    mm = pe.transpose(ps_t[:, i * P:(i + 1) * P], aw[:, i * P:(i + 1) * P], con.ident[:])
                mm.then_inc(at_done, 1)
                wait(pe, y_done, n - 1)
                pe.wait_ge(awt_done, n + 1)
                for i in range(j + 1):
                    mm = pe.matmul(ps_o[n % 2][:, 0:DH], awt[:, i * P:(i + 1) * P], v[:, i, h, 0:DH],
                                   start=(i == 0), stop=(i == j))
                mm.then_inc(o_done, 1)

            scores(0)
            for n in range(N + 3):
                if n + 1 < N:
                    scores(n + 1)
                if 1 <= n <= N:
                    output(n - 1)
                for h, c in ended(n - 1):
                    pe.wait_ge(y_done, NT * (h + 1))
                    wait(pe, lo_done, 2 * h + c)
                    for t in range(NT):
                        mm = pe.transpose(ps_y[:, t * P:(t + 1) * P], y[h % 2][:, t, c * P:(c + 1) * P], con.ident[:])
                    mm.then_inc(tr_done, 1)

        @block.scalar
        def _(act):
            def norm(n):
                w = (steps[n][1] + 1) * P
                act.wait_ge(at_done, n + 1)
                wait(act, o_done, n)
                act.activation(awt[:, 0:w], ps_t[:, 0:w], ACT.Copy).then_inc(awt_done, 1)
                act.wait_ge(o_done, n + 1)
                wait(act, ss_done, n)
                wait(act, ms_done, n - 1)
                act.activation(junk[:], ps_o[n % 2][:, 0:DH], ACT.Square, accum_out=ss[n % 2][:]).then_inc(ss_done, 1)

            for n in range(N + 3):
                if n < N:
                    w = (steps[n][1] + 1) * P
                    act.wait_ge(nb_done, n + 1)
                    wait(act, a_done, n - 1)
                    for c in range(2):
                        act.activation(p[n % 2][c][:, 0:w], ps_s[n % 2][c][:, 0:w], ACT.Exp,
                                       bias=nb[n % 2][:, c:c + 1], scale=scale,
                                       accum_out=sm[n % 2][:, c:c + 1]).then_inc(p_done, 1)
                if 1 <= n <= N:
                    norm(n - 1)
                for h, c in ended(n - 1):
                    act.wait_ge(tr_done, 2 * h + c + 1)
                    gain = con.cols_b[:, R_DGAIN + 2 * h + c:R_DGAIN + 2 * h + c + 1]
                    act.activation(y_hi[:, 2 * h + c], ps_y[:], ACT.Copy, scale=gain).then_inc(hi_done, 1)

        @block.gpsimd
        def _(pool):
            for n in range(N):
                pool.wait_ge(ms_done, n + 1)
                wait(pool, y_done, n - 1)
                pool.tensor_tensor(rstd[n % 2][:], ms[n % 2][:], con.pow_half[:, 0:1], ALU.pow).then_inc(pow_done, 1)

        @block.vector
        def _(dve):
            def maxima(n):
                w = (steps[n][1] + 1) * P
                dve.wait_ge(s_done, 2 * n + 2)
                for c in range(2):
                    dve.memset(ps_s[n % 2][c][0:CHUNK, w - CHUNK:w], NEG).then_inc(masked, 1)
                dve.wait_ge(masked, 2 * n + 2)
                for c in range(2):
                    dve.tensor_reduce(mx[n % 2][:, c:c + 1], ps_s[n % 2][c][:, 0:w], AX_X, ALU.max).then_inc(max_done, 1)
                dve.wait_ge(max_done, 2 * n + 2)
                wait(dve, p_done, 2 * (n - 1))
                dve.tensor_scalar(nb[n % 2][:], mx[n % 2][:], -scale, None, ALU.mult).then_inc(nb_done, 1)

            def weights(n):
                w = (steps[n][1] + 1) * P
                dve.wait_ge(p_done, 2 * n + 2)
                dve.reciprocal(rs[n % 2][:], sm[n % 2][:]).then_inc(rs_done, 1)
                dve.wait_ge(rs_done, n + 1)
                dve.tensor_tensor(rs[n % 2][:, 1:2], rs[n % 2][:, 1:2], con.lam[:], ALU.mult).then_inc(w_done, 1)
                dve.wait_ge(w_done, n + 1)
                dve.tensor_scalar(p1w[:, 0:w], p[n % 2][1][:, 0:w], rs[n % 2][:, 1:2], None, ALU.mult).then_inc(p1_done, 1)
                dve.wait_ge(p1_done, n + 1)
                wait(dve, at_done, n)
                dve.scalar_tensor_tensor(out=aw[:, 0:w], in0=p[n % 2][0][:, 0:w], scalar=rs[n % 2][:, 0:1],
                                         in1=p1w[:, 0:w], op0=ALU.mult, op1=ALU.subtract).then_inc(a_done, 1)

            def norm(n):
                h, j = steps[n]
                dve.wait_ge(ss_done, n + 1)
                wait(dve, pow_done, n - 1)
                dve.tensor_scalar(ms[n % 2][:], ss[n % 2][:], 1.0 / DH, EPS, ALU.mult, ALU.add).then_inc(ms_done, 1)
                dve.wait_ge(pow_done, n + 1)
                wait(dve, tr_done, 2 * (h - 1))
                dve.tensor_scalar(y[h % 2][:, j], ps_o[n % 2][:, 0:DH], rstd[n % 2][:], None,
                                  ALU.mult).then_inc(y_done, 1)

            maxima(0)
            for n in range(N + 3):
                if n + 1 < N:
                    maxima(n + 1)
                if n < N:
                    weights(n)
                if 1 <= n <= N:
                    norm(n - 1)
                for h, c in ended(n - 1):
                    dve.wait_ge(hi_done, 2 * h + c + 1)
                    gain = con.cols_b[:, R_DGAIN + 2 * h + c:R_DGAIN + 2 * h + c + 1]
                    dve.scalar_tensor_tensor(out=y_lo[:, 2 * h + c], in0=ps_y[:], scalar=gain,
                                             in1=as_f32(y_hi[:, 2 * h + c]), op0=ALU.mult,
                                             op1=ALU.subtract).then_inc(lo_done, 1)


def out_block(nc, slots, A, m_hl, y):
    def make(al):
        def vector(dve, units_of, units):
            for sec, it, s, c, u, bank, freed in units_of:
                if c % 2 == 0:
                    dve.wait_ge(units, u + 1)
                    dve.tensor_copy(y[:, c, bass.ds((2 * it + s) * GC, GC)], bank[:, 0:GC]).then_inc(freed, 1)

        def scalar(act, units_of, units):
            for sec, it, s, c, u, bank, freed in units_of:
                if c % 2:
                    act.wait_ge(units, u + 1)
                    act.activation(y[:, c, bass.ds((2 * it + s) * GC, GC)], bank[:, 0:GC], ACT.Copy).then_inc(freed, 1)
        return vector, scalar

    project_block(nc, "proj_o", slots, [("N", 4, w_group(A["w_out"][0], 0), lambda s: m_hl)], make)


def residual_block(nc, tag, con, x_src, x, y, gate_cols, dst, stored, last):
    with Alloc(nc, tag) as al:
        row = al.sb("row", [P, D])
        diag = [al.sb(f"diag{i}", [P, P]) for i in range(2)]
        junk, ss, ms, rstd = al.sb("junk", [P, D]), al.sb("ss", [P, NT]), al.sb("ms", [P, NT]), al.sb("rstd", [P, NT])
        yg = [al.sb(f"yg{i}", [P, D]) for i in range(2)]
        ps = [al.ps(f"ps{i}", [P, P]) for i in range(2)]
        x_in = [al.sem(f"x_in{i}") for i in range(NT)]
        diag_done, spread, row_done, ss_done, ms_done, pow_done, yg_done, sum_done = map(al.sem, (
            "diag_done", "spread", "row_done", "ss_done", "ms_done", "pow_done", "yg_done", "sum_done"))
        block = al.block()

        @block.sync
        def _(sp):
            for t in range(NT):
                sp.dma_start(x[:, t], x_src[t * P:(t + 1) * P, :]).then_inc(x_in[t], 16)
            for t in range(NT):
                sp.wait_ge(sum_done, t + 1)
                sp.dma_start(dst[t * P:(t + 1) * P, :], x[:, t]).then_inc(stored, 16)
            if last:
                sp.wait_ge(stored, 16 * NT)

        @block.scalar
        def _(act):
            for t in range(NT):
                wait(act, ss_done, t)
                act.activation(junk[:], y[:, t], ACT.Square, accum_out=ss[:, t:t + 1]).then_inc(ss_done, 1)
            for k in range(KD):
                act.wait_ge(spread, k + 1)
                act.activation(row[:, k * P:(k + 1) * P], ps[k % 2][:], ACT.Copy).then_inc(row_done, 1)

        @block.gpsimd
        def _(pool):
            pool.wait_ge(ms_done, 1)
            pool.tensor_tensor(rstd[:], ms[:], con.pow_half[:, 0:NT], ALU.pow).then_inc(pow_done, 1)

        @block.tensor
        def _(pe):
            for k in range(KD):
                pe.wait_ge(diag_done, k + 1)
                wait(pe, row_done, k - 1)
                pe.matmul(ps[k % 2][:], con.ones[:], diag[k % 2][:], start=True, stop=True).then_inc(spread, 1)

        @block.vector
        def _(dve):
            for k in range(KD):
                wait(dve, spread, k - 1)
                dve.tensor_scalar(diag[k % 2][:], con.ident[:], gate_cols[:, k:k + 1], None,
                                  ALU.mult).then_inc(diag_done, 1)
            dve.wait_ge(ss_done, NT)
            dve.tensor_scalar(ms[:], ss[:], 1.0 / D, EPS, ALU.mult, ALU.add).then_inc(ms_done, 1)
            dve.wait_ge(pow_done, 1)
            dve.wait_ge(row_done, KD)
            for t in range(NT):
                dve.wait_ge(x_in[t], 16)
                wait(dve, sum_done, t - 1)
                dve.scalar_tensor_tensor(out=yg[t % 2][:], in0=y[:, t], scalar=rstd[:, t:t + 1], in1=row[:],
                                         op0=ALU.mult, op1=ALU.mult).then_inc(yg_done, 1)
                dve.wait_ge(yg_done, t + 1)
                dve.tensor_tensor(x[:, t], x[:, t], yg[t % 2][:], ALU.add).then_inc(sum_done, 1)


class Consts:

    def __init__(self, al):
        self.ident, self.ones = al.sb("ident", [P, P]), al.sb("ones", [P, P])
        self.iota, self.pow_half = al.sb("iota", [P, P]), al.sb("pow_half", [P, 8])
        self.sel = al.sb("sel", [HEADS, HEADS, P])
        self.cols_a, self.cols_b = al.sb("cols_a", [P, NROWS_A]), al.sb("cols_b", [P, NROWS_B])
        self.silu_c, self.ada = al.sb("silu_c", [P, KD]), al.sb("ada", [P, 48])
        self.lam_cols, self.lam = al.sb("lam_cols", [P, 4]), al.sb("lam", [P, 1])
        self.gate_bias = al.sb("gate_bias", [HEADS, 2])
        self.scale_a, self.scale_b = al.sb("scale_a", [P, KD]), al.sb("scale_b", [P, KD])
        self.gate_a, self.gate_b = al.sb("gate_a", [P, KD]), al.sb("gate_b", [P, KD])


def mixer(nc, con, slots, A, hT, x1):
    x = A["x"].rearrange("b s d -> (b s) d")
    with Alloc(nc, "mix") as al:
        merged = al.sb("merged", [P, KD, T])
        y_hl = al.sb("y_hi", [P, KD, T], F32R), al.sb("y_lo", [P, KD, T], F32R)
        with Alloc(nc, "in") as ai:
            qk, v = ai.sb("qk", [P, 2 * KD, T]), ai.sb("v", [P, NT, HEADS, DH + 1])
            with Alloc(nc, "gate") as ag:
                out_gate, gates = ag.sb("out_gate", [P, KD, T]), ag.sb("gates", [HEADS, 2, T])
                mlstm_inputs_block(nc, con, slots, A, hT, qk, v, out_gate, gates)
                mlstm_block(nc, con, qk, v, out_gate, gates, *y_hl)
            gated_branch_block(nc, "branch_m", slots, branch_load(A, C_GM, "w_br_m"), hT, y_hl, merged,
                               w_group(A["w_in"][0], C_DQ), ada=(con, A, 16))
            attention_inputs_block(nc, con, slots, A, hT, qk, v)
            attention_block(nc, con, qk, v, *y_hl)
        with Alloc(nc, "mhl") as am:
            m_hl = am.sb("m_hi", [P, KD, T], F32R), am.sb("m_lo", [P, KD, T], F32R)
            gated_branch_block(nc, "branch_d", slots, branch_load(A, C_GD, "w_br_d"), hT, y_hl, merged,
                               w_group(A["w_out"][0], 0), m_hl)
            y = am.sb("y", [P, NT, D])
            out_block(nc, slots, A, m_hl, y)
            recycle_semaphores(nc, slots.landed)
            with Alloc(nc, "x1") as ax:
                x1_sb, stored = ax.sb("rows", [P, NT, D]), ax.sem("stored")
                residual_block(nc, "res_a", con, x, x1_sb, y, con.gate_a, x1, stored, False)
                modulate_block(nc, con, x1_sb, stored, *hT, con.scale_b, 24, slots, w_group(A["w_query"][0], 0))


U_RING, R_STEPS, G_STEPS, G_TOK = 4, 12, 16, 8
NEXP = NK


def query_block(nc, slots, A, hT, qry):
    def make(al):
        def vector(dve, units_of, units):
            for sec, it, s, c, u, bank, freed in units_of:
                pass

        def scalar(act, units_of, units):
            for sec, it, s, c, u, bank, freed in units_of:
                act.wait_ge(units, u + 1)
                act.activation(qry[:, bass.ds(4 * it + 2 * s + c, 1), :],
                               bank[:].rearrange("p (a t) -> p a t", a=1), ACT.Copy).then_inc(freed, 1)
        return vector, scalar

    project_block(nc, "query", slots, [("T", 8, w_group(A["w_query"][0], 0), lambda s: hT)], make)


def scores_block(nc, con, A, qry, scores):
    HC = PH * HALVES
    with Alloc(nc, "scores") as al:
        keys, keys_t = al.sb("keys", [P, HC, P]), al.sb("keys_t", [P, HC, NK])
        sc = [al.sb(f"sc{i}", [P, HC, NK]) for i in range(2)]
        ps = [al.ps(f"ps{i}", [P, 4, P]) for i in range(4)]
        keys_in, turned, kept, scored, copied = map(al.sem, ("keys_in", "turned", "kept", "scored", "copied"))
        stored = [al.sem(f"stored{i}") for i in range(2)]
        block = al.block()

        @block.sync
        def _(sp):
            sp.dma_start(keys[:], A["sub_keys"][0].rearrange("h c n d -> n (h c) d")).then_inc(keys_in, 16)
            for t in range(NT):
                sp.wait_ge(copied, 4 * (t + 1))
                sp.dma_start(scores[t * P:(t + 1) * P, :], sc[t % 2][:].rearrange("p a n -> p (a n)")).then_inc(
                    stored[t % 2], 16)
            for i in range(2):
                sp.wait_ge(stored[i], 16 * NT // 2)

        @block.tensor
        def _(pe):
            pe.wait_ge(keys_in, 16)
            for q in range(4):
                for m in range(4):
                    mm = pe.transpose(ps[q][:, m, :], keys[:, 4 * q + m, :], con.ident[:])
                mm.then_inc(turned, 1)
            for t in range(NT):
                for q in range(4):
                    pe.wait_ge(kept, 4)
                    wait(pe, copied, 4 * (t - 1) + q + 1)
                    for m in range(4):
                        mm = pe.matmul(ps[q][:, m, :], qry[:, 4 * q + m, t * P:(t + 1) * P], keys_t[:, 4 * q + m, :],
                                       start=True, stop=True)
                    mm.then_inc(scored, 1)

        @block.vector
        def _(dve):
            for q in range(4):
                dve.wait_ge(turned, q + 1)
                dve.tensor_copy(keys_t[:, 4 * q:4 * q + 4, :], ps[q][:]).then_inc(kept, 1)

        @block.scalar
        def _(act):
            for t in range(NT):
                wait(act, stored[t % 2], 16 * (t // 2))
                for q in range(4):
                    act.wait_ge(scored, 4 * t + q + 1)
                    act.activation(sc[t % 2][:, 4 * q:4 * q + 4, :], ps[q][:], ACT.Copy).then_inc(copied, 1)


def experts_in_block(nc, con, A, hT, scores, acts, gmat):
    HC = PH * HALVES
    u = A["expert_u"][0]
    with Alloc(nc, "xin") as al:
        raw = [al.sb(f"u{i}", [P, D]) for i in range(U_RING)]
        uhi = [al.sb(f"uhi{i}", [P, KD, P], F32R) for i in range(2)]
        ulo = [al.sb(f"ulo{i}", [P, KD, P], F32R) for i in range(2)]
        act_t = [al.sb(f"act{i}", [P, T]) for i in range(4)]
        sc, sc2 = al.sb("sc", [P, HC, NK]), al.sb("sc2", [P, HC, NK])
        top, ix, ixf = al.sb("top", [P, HC, TOPK]), al.sb("ix", [P, HC, TOPK], U32), al.sb("ixf", [P, HC, TOPK])
        best, bpos = al.sb("best", [P, PH, TOPK]), al.sb("bpos", [P, PH, TOPK], U32)
        au, bu = al.sb("au", [P, PH, TOPK], U32), al.sb("bu", [P, PH, TOPK], U32)
        rank = [al.sb(f"rank{c}", [P, PH, TOPK]) for c in range(2)]
        pick = [al.sb(f"pick{c}", [P, PH * TOPK, TOPK]) for c in range(2)]
        key = [al.sb(f"key{c}", [P, PH * TOPK]) for c in range(2)]
        eg, ge, gate = [al.sb(n, [P, PH, TOPK]) for n in ("eg", "ge", "gate")]
        gsum, ginv = al.sb("gsum", [P, PH]), al.sb("ginv", [P, PH])
        slot = [al.sb(f"slot{n}", [P, T]) for n in range(3)]
        hot_j = [al.sb(f"hot_j{i}", [P, G_TOK, NK]) for i in range(2)]
        hot_i = [al.sb(f"hot_i{i}", [P, G_TOK, NK]) for i in range(2)]
        stage = [al.sb(f"stage{i}", [P, NK, 8 * G_TOK]) for i in range(2)]
        ps_t = [al.ps(f"ps_t{i}", [P, KD, P]) for i in range(2)]
        ps_u = [al.ps(f"ps_u{i}", [P, T]) for i in range(2)]
        ps_g = [al.ps(f"ps_g{i}", [P, 4, NK]) for i in range(2)]
        landed = [al.sem(f"landed{i}") for i in range(U_RING)]
        kept = [al.sem(f"kept{i}") for i in range(4)]
        flushed = [al.sem(f"flushed{i}") for i in range(2)]
        (t_done, hi_done, lo_done, u_done, gelu_done, sc_in, chosen, exp_done, sub_done, pool_step, keys_done,
         slots_t, slots_done, hot_done, g_done, staged, sum_inv, is_rank) = map(al.sem, (
             "t_done", "hi_done", "lo_done", "u_done", "gelu_done", "sc_in", "chosen", "exp_done", "sub_done",
             "pool_step", "keys_done", "slots_t", "slots_done", "hot_done", "g_done", "staged", "sum_inv", "is_rank"))
        block = al.block()
        n_r = NT * R_STEPS
        n_m = 4
        n_g = T // G_TOK
        n_g0 = n_r + n_m
        n_tail = NEXP - n_g0 - n_g
        assert n_tail > 0 and n_tail % 4 == 0
        cand = sc[:].rearrange("p (h c) k -> p h (c k)", c=2)
        cand2 = sc2[:].rearrange("p (h c) k -> p h (c k)", c=2)
        STAGES = 16

        @block.sync
        def _(sp):
            def every(n, s, more, args):
                row = settled(sp, n * P)
                arow = settled(sp, (n - 4) * P) if not (isinstance(n, int) and n < 4) else 0
                wait(sp, t_done, n - 3)
                sp.dma_start(raw[s % U_RING][:], u[bass.ds(row, P), :]).then_inc(landed[s % U_RING], 16)
                if not (isinstance(n, int) and n < 4):
                    sp.wait_ge(gelu_done, n - 3)
                    sp.dma_start(acts[bass.ds(arow, P), :], act_t[s % 4][:]).then_inc(kept[s % 4], 16)
                if more:
                    more(*args)

            def route(tt, s):
                if s == 0:
                    trow = settled(sp, tt * P)
                    wait(sp, chosen, STAGES * (tt - 1) + 13)
                    sp.dma_start(sc[:].rearrange("p a k -> p (a k)"), scores[bass.ds(trow, P), :]).then_inc(sc_in, 16)

            def gates(gi, q):
                if q >= 12:
                    flush(gi, 0, q - 12)
                if 4 <= q < 8 and not (isinstance(gi, int) and gi == 0):
                    flush(gi - 1, 1, q - 4)

            def flush(gi, h, part):
                tok = settled(sp, gi * (G_STEPS * G_TOK) + h * 8 * G_TOK)
                rows = slice(part * NK // 4, (part + 1) * NK // 4)
                sp.wait_ge(staged, 2 * (G_STEPS * gi + 8 * h + 8))
                sp.dma_start(gmat.rearrange("(i j) t -> j i t", j=NK)[:, rows, bass.ds(tok, 8 * G_TOK)],
                             stage[h][:, rows, :]).then_inc(flushed[h], 16)

            for tt in pairs(sp, NT, True):
                for s in range(R_STEPS):
                    every(R_STEPS * tt + s, s, route, (tt, s))
            for s in range(n_m):
                every(n_r + s, s, None, None)
            for gi in pairs(sp, n_g // G_STEPS, True):
                for q in range(G_STEPS):
                    every(n_g0 + G_STEPS * gi + q, q, gates, (gi, q))
            for it in range(n_tail // 4):
                for s in range(4):
                    every(n_g0 + n_g + 4 * it + s, s, None, None)
                    if it == 1:
                        flush(n_g // G_STEPS - 1, 1, s)
            for n in range(NEXP, NEXP + 4):
                sp.wait_ge(gelu_done, n - 3)
                sp.dma_start(acts[(n - 4) * P:(n - 3) * P, :], act_t[n % 4][:]).then_inc(kept[n % 4], 16)
            for i in range(4):
                sp.wait_ge(kept[i], 16 * NEXP // 4)
            for h in range(2):
                sp.wait_ge(flushed[h], 64 * (n_g // G_STEPS))

        @block.tensor
        def _(pe):
            def turn(n, s):
                pe.wait_ge(landed[s % U_RING], 16 * (n // U_RING + 1) if isinstance(n, int) else lap(n, s))
                wait(pe, lo_done, n - 1)
                for k in range(KD):
                    mm = pe.transpose(ps_t[s % 2][:, k, :], raw[s % U_RING][:, k * P:(k + 1) * P], con.ident[:])
                mm.then_inc(t_done, 1)

            laps = {}

            def lap(n, s):
                return laps["value"]

            def every(n, s, more, args, last=False, base=None, it=None, per=None):
                if not last:
                    if base is not None:
                        laps["value"] = 16 * ((base + s + 1) // U_RING + 1) + 16 * (per // U_RING) * it
                    turn(n + 1, s + 1)
                pe.wait_ge(lo_done, n + 1)
                wait(pe, gelu_done, n - 1)
                i = 0
                for k in range(KD):
                    for a, m in ((uhi, hT[0]), (uhi, hT[1]), (ulo, hT[0])):
                        mm = pe.matmul(ps_u[s % 2][:], a[s % 2][:, k, :], m[:, k, :], start=(i == 0),
                                       stop=(i == 3 * KD - 1))
                        i += 1
                mm.then_inc(u_done, 1)
                if more:
                    more(*args)

            def turn_slots(tt):
                pe.wait_ge(keys_done, 2 * tt + 2)
                pe.wait_ge(chosen, STAGES * (tt + 1))
                wait(pe, slots_done, tt)
                for i, src in enumerate((key[0][:], key[1][:], gate[:].rearrange("p h k -> p (h k)"))):
                    mm = pe.transpose(ps_g[0][:, i, :], src, con.ident[:])
                mm.then_inc(slots_t, 1)

            def route(tt, s):
                if s == 6 and not (isinstance(tt, int) and tt == 0):
                    turn_slots(tt - 1)

            def gates(gi, q):
                m = G_STEPS * gi + q
                pe.wait_ge(hot_done, m + 1)
                for b in range(2):
                    wait(pe, staged, 2 * m + b - 1)
                    for k in range(4):
                        mm = pe.matmul(ps_g[b][:, k, :], hot_j[q % 2][:, 4 * b + k, :], hot_i[q % 2][:, 4 * b + k, :],
                                       start=True, stop=True)
                    mm.then_inc(g_done, 1)

            pe.wait_ge(landed[0], 16)
            turn(0, 0)
            for tt in pairs(pe, NT, True):
                for s in range(R_STEPS):
                    every(R_STEPS * tt + s, s, route, (tt, s), base=0, it=tt, per=R_STEPS)
            for s in range(n_m):
                every(n_r + s, s, None, None)
            turn_slots(NT - 1)
            pe.wait_ge(slots_done, NT)
            for gi in pairs(pe, n_g // G_STEPS, True):
                for q in range(G_STEPS):
                    every(n_g0 + G_STEPS * gi + q, q, gates, (gi, q), base=n_g0, it=gi, per=G_STEPS)
            for it in pairs(pe, n_tail // 4, False, True):
                for s in range(4):
                    n = n_g0 + n_g + 4 * it + s
                    every(n, s, None, None, last=isinstance(n, int) and n == NEXP - 1, base=n_g0 + n_g, it=it, per=4)

        @block.scalar
        def _(act):
            def cut(n, s):
                act.wait_ge(t_done, n + 1)
                wait(act, u_done, n - 1)
                act.activation(uhi[s % 2][:], ps_t[s % 2][:], ACT.Copy).then_inc(hi_done, 1)

            def every(n, s, more, args, last=False, laps=None):
                if not last:
                    cut(n + 1, s + 1)
                act.wait_ge(u_done, n + 1)
                if laps is None or not (isinstance(laps, int) and laps <= 0):
                    wait(act, kept[s % 4], laps)
                act.activation(act_t[s % 4][:], ps_u[s % 2][:], ACT.Gelu).then_inc(gelu_done, 1)
                if more:
                    more(*args)

            def route(tt, s):
                if s == R_STEPS - 1:
                    act.wait_ge(sub_done, tt + 1)
                    act.activation(ge[:], eg[:], ACT.Exp).then_inc(exp_done, 1)

            def gates(gi, q):
                m = G_STEPS * gi + q
                for b in range(2):
                    act.wait_ge(g_done, 2 * m + b + 1)
                    if q % 8 == 0 and b == 0 and not (isinstance(gi, int) and gi == 0):
                        act.wait_ge(flushed[q // 8], 64 * gi)
                    t0 = (q % 8) * G_TOK + 4 * b
                    act.activation(stage[q // 8][:, :, t0:t0 + 4], ps_g[b][:].rearrange("p t i -> p i t"),
                                   ACT.Copy).then_inc(staged, 1)

            cut(0, 0)
            for tt in pairs(act, NT, True):
                for s in range(R_STEPS):
                    every(R_STEPS * tt + s, s, route, (tt, s), laps=16 * (s // 4) + 16 * (R_STEPS // 4) * tt)
            for s in range(n_m):
                every(n_r + s, s, None, None, laps=16 * ((n_r + s) // 4))
            for gi in pairs(act, n_g // G_STEPS, True):
                for q in range(G_STEPS):
                    every(n_g0 + G_STEPS * gi + q, q, gates, (gi, q), laps=16 * ((n_g0 + q) // 4) + 16 * (G_STEPS // 4) * gi)
            for it in pairs(act, n_tail // 4, False, True):
                for s in range(4):
                    n = n_g0 + n_g + 4 * it + s
                    every(n, s, None, None, last=isinstance(n, int) and n == NEXP - 1,
                          laps=16 * ((n_g0 + n_g) // 4) + 16 * it)

        @block.gpsimd
        def _(pool):
            step = [0]

            def chain(op):
                op.then_inc(pool_step, 1)
                step[0] += 1
                return step[0]

            per_tile = 2 * 4
            for tt in pairs(pool, NT, True):
                step[0] = 0
                wait(pool, slots_t, tt)
                for c in range(HALVES):
                    base = per_tile * tt
                    pool.wait_ge(is_rank, 2 * tt + c + 1)
                    p4 = pick[c][:].rearrange("p (h k) a -> p h k a", h=PH)
                    nums = ixf[:].rearrange("p (h c) k -> p h c k", c=2)[:, :, c, :].unsqueeze(2).to_broadcast(
                        [P, PH, TOPK, TOPK])
                    chain(pool.tensor_tensor(p4, p4, nums, ALU.mult))
                    for w in (8, 4, 2):
                        pool.wait_ge(pool_step, base + step[0])
                        chain(pool.tensor_tensor(pick[c][:, :, 0:w], pick[c][:, :, 0:w], pick[c][:, :, w:2 * w],
                                                 ALU.add))
                    pool.wait_ge(pool_step, base + step[0])
                    pool.tensor_tensor(key[c][:].unsqueeze(2), pick[c][:, :, 0:1], pick[c][:, :, 1:2],
                                       ALU.add).then_inc(keys_done, 1)

        @block.vector
        def _(dve):
            def cut(n, s):
                dve.wait_ge(hi_done, n + 1)
                dve.tensor_tensor(ulo[s % 2][:], ps_t[s % 2][:], as_f32(uhi[s % 2][:]), ALU.subtract).then_inc(lo_done, 1)

            def every(n, s, more, args, last=False):
                if more is gates:
                    more(*args)
                if not last:
                    cut(n + 1, s + 1)
                if more is route:
                    more(*args)

            def at(tt, k):
                dve.wait_ge(chosen, STAGES * tt + k)

            def top8(out, src, tt, k, count):
                for x in range(count):
                    op = dve.max(out=out(x), in_=src(x))
                op.then_inc(chosen, 1)
                at(tt, k)

            def where(out, vals, src, tt, k, count):
                for x in range(count):
                    op = dve.max_index(out=out(x), in_max=vals(x), in_values=src(x))
                op.then_inc(chosen, 1)
                at(tt, k)

            def strike(out, vals, src, tt, k, count):
                for x in range(count):
                    op = dve.match_replace(out=out(x), in_to_replace=vals(x), in_values=src(x), imm_value=NEG)
                op.then_inc(chosen, 1)
                at(tt, k)

            lo8, hi8 = slice(0, 8), slice(8, 16)
            s_of, s2_of = (lambda x: sc[:, x, :]), (lambda x: sc2[:, x, :])
            c_of, c2_of = (lambda x: cand[:, x, :]), (lambda x: cand2[:, x, :])

            def route(tt, s):
                first = isinstance(tt, int) and tt == 0
                if s == 0:
                    if not first:
                        dve.wait_ge(exp_done, tt)
                    dve.wait_ge(sc_in, 16 * (tt + 1))
                    dve.memset(gsum[:], 0.0)
                    top8(lambda x: top[:, x, lo8], s_of, tt, 1, HC)
                elif s == 1:
                    where(lambda x: ix[:, x, lo8], lambda x: top[:, x, lo8], s_of, tt, 2, HC)
                elif s == 2:
                    strike(s2_of, lambda x: top[:, x, lo8], s_of, tt, 3, HC)
                elif s == 3:
                    top8(lambda x: top[:, x, hi8], s2_of, tt, 4, HC)
                elif s == 4:
                    where(lambda x: ix[:, x, hi8], lambda x: top[:, x, hi8], s2_of, tt, 5, HC)
                elif s == 5:
                    if not first:
                        dve.wait_ge(keys_done, 2 * tt)
                    dve.tensor_copy(ixf[:], ix[:]).then_inc(chosen, 1)
                    at(tt, 6)
                    t4 = top[:].rearrange("p (h c) k -> p h c k", c=2)
                    shape = [P, PH, TOPK, TOPK]
                    dve.tensor_tensor(cand.rearrange("p h (a b) -> p h a b", b=TOPK),
                                      t4[:, :, 0, :].unsqueeze(3).to_broadcast(shape),
                                      t4[:, :, 1, :].unsqueeze(2).to_broadcast(shape), ALU.add).then_inc(chosen, 1)
                    at(tt, 7)
                elif s == 6:
                    if not first:
                        copy_slots(tt - 1)
                    top8(lambda x: best[:, x, lo8], c_of, tt, 8, PH)
                elif s == 7:
                    where(lambda x: bpos[:, x, lo8], lambda x: best[:, x, lo8], c_of, tt, 9, PH)
                elif s == 8:
                    strike(c2_of, lambda x: best[:, x, lo8], c_of, tt, 10, PH)
                elif s == 9:
                    top8(lambda x: best[:, x, hi8], c2_of, tt, 11, PH)
                elif s == 10:
                    where(lambda x: bpos[:, x, hi8], lambda x: best[:, x, hi8], c2_of, tt, 12, PH)
                    dve.tensor_single_scalar(au[:], bpos[:], 4, ALU.logical_shift_right)
                    dve.tensor_single_scalar(bu[:], bpos[:], 15, ALU.bitwise_and).then_inc(chosen, 1)
                    at(tt, 13)
                    dve.tensor_copy(rank[0][:], au[:])
                    dve.tensor_copy(rank[1][:], bu[:]).then_inc(chosen, 1)
                else:
                    opts = con.iota[:, 0:TOPK].unsqueeze(1).to_broadcast([P, PH * TOPK, TOPK])
                    dve.tensor_tensor(eg[:], best[:], best[:, :, 0:1].to_broadcast([P, PH, TOPK]),
                                      ALU.subtract).then_inc(sub_done, 1)
                    at(tt, 14)
                    for c in range(HALVES):
                        mine = rank[c][:].rearrange("p h k -> p (h k)").unsqueeze(2).to_broadcast(
                            [P, PH * TOPK, TOPK])
                        dve.tensor_tensor(pick[c][:], mine, opts, ALU.is_equal).then_inc(is_rank, 1)
                    dve.wait_ge(exp_done, tt + 1)
                    dve.tensor_reduce(gsum[:], ge[:], AX_X, ALU.add).then_inc(chosen, 1)
                    at(tt, 15)
                    dve.reciprocal(ginv[:], gsum[:]).then_inc(sum_inv, 1)
                    dve.wait_ge(sum_inv, tt + 1)
                    dve.tensor_tensor(gate[:], ge[:], ginv[:].unsqueeze(2).to_broadcast([P, PH, TOPK]),
                                      ALU.mult).then_inc(chosen, 1)

            def copy_slots(tt):
                dve.wait_ge(slots_t, tt + 1)
                for i in range(3):
                    op = dve.tensor_copy(slot[i][:, bass.ds(tt * P, P)], ps_g[0][:, i, :])
                op.then_inc(slots_done, 1)

            def gates(gi, q):
                m = G_STEPS * gi + q
                wait(dve, g_done, 2 * (m - 1))
                for k in range(G_TOK):
                    tok = gi * (G_STEPS * G_TOK) + q * G_TOK + k
                    i_s, j_s, g_s = [slot[x][:, bass.ds(tok, 1)] for x in range(3)]
                    dve.tensor_scalar(hot_j[q % 2][:, k, :], con.iota[:], j_s, None, ALU.is_equal)
                    op = dve.tensor_scalar(hot_i[q % 2][:, k, :], con.iota[:], i_s, g_s, ALU.is_equal, ALU.mult)
                op.then_inc(hot_done, 1)

            cut(0, 0)
            for tt in pairs(dve, NT, True):
                for s in range(R_STEPS):
                    every(R_STEPS * tt + s, s, route, (tt, s))
            for s in range(n_m):
                every(n_r + s, s, None, None)
            copy_slots(NT - 1)
            dve.wait_ge(slots_done, NT)
            for gi in pairs(dve, n_g // G_STEPS, True):
                for q in range(G_STEPS):
                    every(n_g0 + G_STEPS * gi + q, q, gates, (gi, q))
            for it in pairs(dve, n_tail // 4, False, True):
                for s in range(4):
                    n = n_g0 + n_g + 4 * it + s
                    every(n, s, None, None, last=isinstance(n, int) and n == NEXP - 1)


def experts_out_block(nc, A, acts, gmat, y):
    vexp = A["expert_v"][0]
    RING = 4
    with Alloc(nc, "xout") as al:
        v = [al.sb(f"v{i}", [P, D]) for i in range(RING)]
        a = [al.sb(f"a{i}", [P, T]) for i in range(RING)]
        g = [al.sb(f"g{i}", [P, T]) for i in range(RING)]
        vhi, vlo = [[al.sb(f"{n}{i}", [P, D], F32R) for i in range(2)] for n in ("vhi", "vlo")]
        wt = [al.sb(f"wt{i}", [P, T]) for i in range(2)]
        whi, wlo = [[al.sb(f"{n}{i}", [P, T], F32R) for i in range(2)] for n in ("whi", "wlo")]
        out = [[al.ps(f"out{t}{h}", [P, T]) for h in range(2)] for t in range(NT)]
        v_in, ag_in = [al.sem(f"v_in{i}") for i in range(RING)], [al.sem(f"ag_in{i}") for i in range(RING)]
        vhi_done, vlo_done, wt_done, whi_done, wlo_done, used, y_done = map(
            al.sem, ("vhi_done", "vlo_done", "wt_done", "whi_done", "wlo_done", "used", "y_done"))
        block = al.block()

        def steps(eng):
            for it in pairs(eng, NEXP // RING, True, True):
                for s in range(RING):
                    yield RING * it + s, s, it

        @block.sync
        def _(sp):
            for n, s, it in steps(sp):
                row = settled(sp, n * P)
                wait(sp, vlo_done, n - 3)
                sp.dma_start(v[s][:], vexp[bass.ds(row, P), :]).then_inc(v_in[s], 16)
                wait(sp, wt_done, n - 3)
                sp.dma_start(a[s][:], acts[bass.ds(row, P), :]).then_inc(ag_in[s], 16)
                sp.dma_start(g[s][:], gmat[bass.ds(row, P), :]).then_inc(ag_in[s], 16)

        @block.scalar
        def _(act):
            for n, s, it in steps(act):
                act.wait_ge(v_in[s], 16 * (it + 1))
                wait(act, used, n - 1)
                act.activation(vhi[s % 2][:], v[s][:], ACT.Copy).then_inc(vhi_done, 1)
                act.wait_ge(wt_done, n + 1)
                act.activation(whi[s % 2][:], wt[s % 2][:], ACT.Copy).then_inc(whi_done, 1)

        @block.gpsimd
        def _(pool):
            for n, s, it in steps(pool):
                pool.wait_ge(vhi_done, n + 1)
                pool.tensor_tensor(vlo[s % 2][:], v[s][:], as_f32(vhi[s % 2][:]), ALU.subtract).then_inc(vlo_done, 1)

        @block.vector
        def _(dve):
            for n, s, it in steps(dve):
                dve.wait_ge(ag_in[s], 32 * (it + 1))
                wait(dve, wlo_done, n - 1)
                dve.tensor_tensor(wt[s % 2][:], a[s][:], g[s][:], ALU.mult).then_inc(wt_done, 1)
                dve.wait_ge(whi_done, n + 1)
                dve.tensor_tensor(wlo[s % 2][:], wt[s % 2][:], as_f32(whi[s % 2][:]), ALU.subtract).then_inc(wlo_done, 1)
            dve.wait_ge(used, NEXP)
            for t in range(NT):
                dve.tensor_copy(y[:, t, 0:T], out[t][0][:]).then_inc(y_done, 1)
                dve.tensor_copy(y[:, t, T:D], out[t][1][:]).then_inc(y_done, 1)

        @block.tensor
        def _(pe):
            for n, s, it in steps(pe):
                first, last = isinstance(n, int) and n == 0, isinstance(n, int) and n == NEXP - 1
                pe.wait_ge(vlo_done, n + 1)
                pe.wait_ge(wlo_done, n + 1)
                for t in range(NT):
                    ts = slice(t * P, (t + 1) * P)
                    for i, (w, m) in enumerate(((whi, vhi), (whi, vlo), (wlo, vhi))):
                        for h in range(2):
                            mm = pe.matmul(out[t][h][:], w[s % 2][:, ts], m[s % 2][:, h * T:(h + 1) * T],
                                           start=(first and i == 0), stop=(last and i == 2))
                mm.then_inc(used, 1)


def experts(nc, con, A, hT, x1, scores, acts, gmat, out):
    experts_in_block(nc, con, A, hT, scores, acts, gmat)
    with Alloc(nc, "y") as al:
        y = al.sb("y", [P, NT, D])
        experts_out_block(nc, A, acts, gmat, y)
        x, stored = al.sb("x", [P, NT, D]), al.sem("stored")
        residual_block(nc, "res_b", con, x1, x, y, con.gate_b, out, stored, True)


def build_program(nc, A, out):
    Alloc.sems = []
    x1 = nc.dram_tensor("x1_scratch", (T, D), F32, kind="Internal").ap()
    scores = nc.dram_tensor("scores_scratch", (T, PH * HALVES * NK), F32, kind="Internal").ap()
    acts = nc.dram_tensor("act_scratch", (NK * NK, T), F32, kind="Internal").ap()
    gmat = nc.dram_tensor("gate_scratch", (NK * NK, T), F32, kind="Internal").ap()
    with Alloc(nc, "con") as al:
        con = Consts(al)
        hT = al.sb("h_hi", [P, KD, T], F32R), al.sb("h_lo", [P, KD, T], F32R)
        with Alloc(nc, "in_slots") as ai:
            slots = Slots(ai)
            head_block(nc, con, slots, A, A["x"].rearrange("b s d -> (b s) d"), *hT)
            mixer(nc, con, slots, A, hT, x1)
            with Alloc(nc, "qry") as aq:
                qry = aq.sb("qry", [P, PH * HALVES, T])
                query_block(nc, slots, A, hT, qry)
                scores_block(nc, con, A, qry, scores)
        experts(nc, con, A, hT, x1, scores, acts, gmat, out.rearrange("b s d -> (b s) d"))


NAMES = ["x", "c", "w_ada", "b_ada", "g_pre_mix", "g_post_mix", "g_pre_ffn", "g_post_ffn", "w_in", "b_if", "conv_w",
         "conv_b", "m_head_gain", "lam_q1", "lam_k1", "lam_q2", "lam_k2", "d_head_gain", "w_br_m", "w_br_d", "w_out",
         "w_query", "sub_keys", "expert_u", "expert_v"]


def kernel(**inputs):
    import concourse.bacc as bacc
    from concourse.bass_utils import run_bass_kernel_spmd

    nc = bacc.Bacc("TRN2", target_bir_lowering=False, num_devices=1)
    arrays, views = {}, {}
    for name in NAMES:
        a = np.ascontiguousarray(inputs[name])
        arrays[f"in_{name}"] = a
        views[name] = nc.dram_tensor(f"in_{name}", a.shape, mybir.dt.from_np(a.dtype), kind="ExternalInput").ap()
    out = nc.dram_tensor("out", inputs["x"].shape, F32, kind="ExternalOutput").ap()
    build_program(nc, views, out)
    result = run_bass_kernel_spmd(nc, [arrays], core_ids=[0])
    return result.results[0]["out"]
```

```python
import math
from contextlib import ExitStack

import numpy as np

import concourse.bass as bass
from concourse import mybir

F32 = mybir.dt.float32
F32R = mybir.dt.float32r
U32 = mybir.dt.uint32
ALU = mybir.AluOpType
ACT = mybir.ActivationFunctionType
AX_X = mybir.AxisListType.X

P = 128
D = 1024
T = 512
KD = D // P
NT = T // P
EPS = 1e-6
HEADS = 4
DH = 256
DQK = 128
CHUNK = 64
CONV = 4
PH = 8
NK = 128
TOPK = 16
HALVES = 2
GC = 256
LAM_INIT = 0.8 - 0.6 * math.exp(-0.3 * 0)
NEG = -3.0e38

C_QK, C_MV, C_MO, C_IF = 0, 2 * D, 3 * D, 4 * D
C_DQ = C_IF + 2 * HEADS
C_DV, C_GM, C_GD = C_DQ + 2 * D, C_DQ + 3 * D, C_DQ + 4 * D

R_BADA, R_GPREMIX, R_GPOSTMIX, R_GPREFFN, R_GPOSTFFN, R_CONVB, R_C, NROWS_A = 0, 48, 56, 64, 72, 80, 96, 104
R_CONVW, R_MGAIN, R_DGAIN, NROWS_B = 0, 64, 72, 80


def wait(eng, sem, value):
    if isinstance(value, int) and value <= 0:
        return
    eng.wait_ge(sem, value)


def pairs(eng, count, peel, peel_last=False):
    first, end = int(peel), count - int(peel_last)
    if peel:
        yield 0
    if end == first + 1:
        yield first
    elif end > first:
        with eng.Fori(first, end) as it:
            yield it
    if peel_last and count > first:
        yield count - 1


def settled(eng, value):
    return value if isinstance(value, int) else eng.snap(value)


HBUF = 4


class Alloc:
    sems = []

    def __init__(self, nc, tag):
        self.nc, self.tag, self.stack = nc, tag, ExitStack()

    def __enter__(self):
        self.stack.__enter__()
        return self

    def __exit__(self, *a):
        return self.stack.__exit__(*a)

    def sb(self, name, shape, dt=F32):
        return self.stack.enter_context(self.nc.sbuf_tensor(f"{self.tag}_{name}", shape, dt))

    def ps(self, name, shape, dt=F32):
        return self.stack.enter_context(self.nc.psum_tensor(f"{self.tag}_{name}", shape, dt))

    def sem(self, name):
        Alloc.sems.append(self.nc.alloc_semaphore(f"{self.tag}_{name}"))
        return Alloc.sems[-1]

    def block(self):
        return self.stack.enter_context(self.nc.Block())


def recycle_semaphores(nc, keep):
    nc.clear_and_free_semaphores([sem for sem in Alloc.sems if sem not in keep])
    nc.all_engine_barrier()
    Alloc.sems = []


def as_f32(ap):
    return ap.bitcast(F32)


def columns(w, k=KD):
    return w.rearrange("(k p) n -> p k n", p=P)


def ada_columns(eng_sum, w_cols, silu_c, acc, step_done, count0):
    for k in range(KD):
        if k == 0:
            op = eng_sum.tensor_scalar(acc, w_cols[:, 0], silu_c[:, 0:1], None, ALU.mult)
        else:
            eng_sum.wait_ge(step_done, count0 + k)
            op = eng_sum.scalar_tensor_tensor(out=acc, in0=w_cols[:, k], scalar=silu_c[:, k:k + 1], in1=acc,
                                              op0=ALU.mult, op1=ALU.add)
        op.then_inc(step_done, 1)


def head_block(nc, con, slots, A, x_src, hi, lo):
    with Alloc(nc, "head") as al:
        rows_a = al.sb("rows_a", [NROWS_A, P])
        rows_b = al.sb("rows_b", [NROWS_B, P])
        sq = al.sb("sq", [P, 2])
        esum = al.sb("esum", [P, 2])
        groups = 2 * D // GC
        raw = al.sb("raw", [P, groups, KD, GC])
        acc = [al.sb(f"acc{i}", [P, GC]) for i in range(2)]
        x = al.sb("x", [P, NT, D])
        junk = al.sb("junk", [P, D])
        ss, ms, rstd = al.sb("ss", [P, NT]), al.sb("ms", [P, NT]), al.sb("rstd", [P, NT])
        h = al.sb("h", [P, HBUF, T])
        ps_t = al.ps("ps_t", [P, 512])
        ps_u = al.ps("ps_u", [P, 512])
        ps_ada = al.ps("ps_ada", [P, 512])
        ps_l = al.ps("ps_l", [P, 512])
        ps = [al.ps(f"ps{i}", [P, T]) for i in range(4)]
        rows_in, rows_b_in, consts, cols_ready, silu_ready = map(
            al.sem, ("rows_in", "rows_b_in", "consts", "cols_ready", "silu_ready"))
        a_turned, b_turned = al.sem("a_turned"), al.sem("b_turned")
        landed = [al.sem(f"landed{i}") for i in range(groups)]
        x_in = [al.sem(f"x_in{i}") for i in range(NT)]
        acc_step, summed_up, ada_done, scale_done, lam_in, lam_prod, lam_sum, lam_exp, lam_done = map(
            al.sem, ("acc_step", "summed_up", "ada_done", "scale_done", "lam_in", "lam_prod", "lam_sum", "lam_exp",
                     "lam_done"))
        summed, meaned, powed, normed, turned, modded, hi_done, even_lo, odd_lo = map(
            al.sem, ("summed", "meaned", "powed", "normed", "turned", "modded", "hi_done", "even_lo", "odd_lo"))
        w = columns(A["w_ada"][0])
        block = al.block()

        @block.sync
        def _(sp):
            def rows(dst, r, src, n, sem):
                sp.dma_start(dst[r:r + n, :], src.rearrange("(r p) -> r p", p=P)).then_inc(sem, 16)

            rows(rows_a, R_BADA, A["b_ada"][0], 48, rows_in)
            rows(rows_a, R_GPREMIX, A["g_pre_mix"][0], 8, rows_in)
            rows(rows_a, R_GPOSTMIX, A["g_post_mix"][0], 8, rows_in)
            rows(rows_a, R_GPREFFN, A["g_pre_ffn"][0], 8, rows_in)
            rows(rows_a, R_GPOSTFFN, A["g_post_ffn"][0], 8, rows_in)
            rows(rows_a, R_CONVB, A["conv_b"][0], 16, rows_in)
            rows(rows_a, R_C, A["c"][0], 8, rows_in)
            for g in range(groups):
                sp.dma_start(raw[:, g], w[:, :, g * GC:(g + 1) * GC]).then_inc(landed[g], 16)
                if g < NT:
                    sp.dma_start(x[:, g], x_src[g * P:(g + 1) * P, :]).then_inc(x_in[g], 16)
            rows(rows_b, R_CONVW, A["conv_w"][0].rearrange("w c -> (w c)"), 64, rows_b_in)
            rows(rows_b, R_MGAIN, A["m_head_gain"][0], 8, rows_b_in)
            rows(rows_b, R_DGAIN, A["d_head_gain"][0], 8, rows_b_in)
            for n, name in enumerate(("lam_q1", "lam_q2", "lam_k1", "lam_k2")):
                sp.dma_start(con.lam_cols[:, n:n + 1], A[name].rearrange("a p -> p a")).then_inc(lam_in, 16)
            for n in range(2):
                sp.dma_start(con.gate_bias[:, n:n + 1],
                             A["b_if"][:, n * HEADS:(n + 1) * HEADS].rearrange("a h -> h a")).then_inc(lam_in, 16)
            slots.load_ahead(sp, w_group(A["w_in"][0], C_QK))

        @block.gpsimd
        def _(pool):
            pool.memset(con.ident[:], 0.0).then_inc(consts, 1)
            pool.memset(con.ones[:], 1.0).then_inc(consts, 1)
            pool.memset(con.pow_half[:], -0.5).then_inc(consts, 1)
            pool.memset(con.sel[:], 1.0).then_inc(consts, 1)
            pool.iota(con.iota[:], pattern=[[1, P]], base=0, channel_multiplier=0,
                      allow_small_or_imprecise_dtypes=True).then_inc(consts, 1)
            pool.wait_ge(consts, 5)
            pool.affine_select(out=con.ident[:], in_=con.ident[:], compare_op=ALU.not_equal, fill=1.0, base=0,
                               pattern=[[-1, P]], channel_multiplier=1).then_inc(consts, 1)
            pool.affine_select(out=con.sel[:], in_=con.sel[:], compare_op=ALU.is_equal, fill=0.0, base=0,
                               pattern=[[-1, HEADS], [0, P]], channel_multiplier=1).then_inc(consts, 1)
            pool.wait_ge(meaned, 1)
            pool.tensor_tensor(rstd[:], ms[:], con.pow_half[:, 0:NT], ALU.pow).then_inc(powed, 1)
            for k in range(1, KD, 2):
                pool.wait_ge(hi_done, k + 1)
                pool.tensor_tensor(lo[:, k], h[:, k % HBUF], as_f32(hi[:, k]), ALU.subtract).then_inc(odd_lo, 1)

        @block.tensor
        def _(pe):
            pe.wait_ge(consts, 7)
            pe.wait_ge(rows_in, 112)
            pe.transpose(ps_t[:, 0:NROWS_A], rows_a[:], con.ident[0:NROWS_A, 0:NROWS_A]).then_inc(a_turned, 1)

            def sum_columns(g):
                pe.wait_ge(acc_step, KD * (g + 1))
                for m in range(GC // P):
                    c = g * GC // P + m
                    mm = pe.matmul(ps_ada[:, c:c + 1], acc[g % 2][:, m * P:(m + 1) * P], con.ones[:, 0:1],
                                   start=True, stop=True)
                mm.then_inc(summed_up, 1)

            def turn(k):
                for t in range(NT):
                    mm = pe.transpose(ps[k % 4][:, t * P:(t + 1) * P], x[:, t, k * P:(k + 1) * P], con.ident[:])
                mm.then_inc(turned, 1)

            for g in range(groups - 1):
                sum_columns(g)
            pe.wait_ge(normed, NT)
            for k in range(4):
                turn(k)
            sum_columns(groups - 1)
            for k in range(4, KD):
                pe.wait_ge(modded, k - 3)
                turn(k)
            pe.wait_ge(rows_b_in, 48)
            pe.transpose(ps_u[:, 0:NROWS_B], rows_b[:], con.ident[0:NROWS_B, 0:NROWS_B]).then_inc(b_turned, 1)
            pe.wait_ge(lam_prod, 1)
            pe.matmul(ps_l[:, 0:2], con.ones[:], sq[:], start=True, stop=True).then_inc(lam_sum, 1)

        @block.scalar
        def _(act):
            act.wait_ge(cols_ready, 1)
            act.activation(con.silu_c[:], con.cols_a[:, R_C:R_C + KD], ACT.Silu).then_inc(silu_ready, 1)
            for t in range(NT):
                act.wait_ge(x_in[t], 16)
                if t:
                    act.wait_ge(summed, t)
                act.activation(junk[:], x[:, t], ACT.Square, accum_out=ss[:, t:t + 1]).then_inc(summed, 1)
            act.wait_ge(scale_done, 1)
            for k in range(KD):
                act.wait_ge(turned, k + 1)
                if k >= HBUF:
                    act.wait_ge(odd_lo if k % 2 else even_lo, (k - HBUF) // 2 + 1)
                act.activation(h[:, k % HBUF], ps[k % 4][:], ACT.Identity, bias=con.ada[:, k:k + 1],
                               scale=con.scale_a[:, k:k + 1]).then_inc(modded, 1)
            act.wait_ge(lam_sum, 1)
            act.activation(esum[:], ps_l[:, 0:2], ACT.Exp).then_inc(lam_exp, 1)

        @block.vector
        def _(dve):
            dve.wait_ge(a_turned, 1)
            dve.tensor_copy(con.cols_a[:], ps_t[:, 0:NROWS_A]).then_inc(cols_ready, 1)
            dve.wait_ge(silu_ready, 1)
            for g in range(groups):
                dve.wait_ge(landed[g], 16)
                wait(dve, summed_up, g - 1)
                ada_columns(dve, raw[:, g], con.silu_c, acc[g % 2][:], acc_step, KD * g)
                if g == NT:
                    dve.wait_ge(summed, NT)
                    dve.tensor_scalar(ms[:], ss[:], 1.0 / D, EPS, ALU.mult, ALU.add).then_inc(meaned, 1)
                if g == NT + 1:
                    dve.wait_ge(powed, 1)
                    for t in range(NT):
                        dve.tensor_scalar(x[:, t], x[:, t], rstd[:, t:t + 1], None, ALU.mult).then_inc(normed, 1)
            dve.wait_ge(summed_up, groups)
            dve.tensor_tensor(con.ada[:, 0:16], ps_ada[:, 0:16], con.cols_a[:, 0:16], ALU.add).then_inc(ada_done, 1)
            dve.wait_ge(ada_done, 1)
            dve.scalar_tensor_tensor(out=con.scale_a[:], in0=con.ada[:, 8:16], scalar=1.0,
                                     in1=con.cols_a[:, R_GPREMIX:R_GPREMIX + 8], op0=ALU.add,
                                     op1=ALU.mult).then_inc(scale_done, 1)
            for k in range(KD):
                dve.wait_ge(modded, k + 1)
                dve.tensor_copy(hi[:, k], h[:, k % HBUF]).then_inc(hi_done, 1)
                if k % 2 == 0:
                    dve.wait_ge(hi_done, k + 1)
                    dve.tensor_tensor(lo[:, k], h[:, k % HBUF], as_f32(hi[:, k]), ALU.subtract).then_inc(even_lo, 1)
            dve.wait_ge(b_turned, 1)
            dve.tensor_copy(con.cols_b[:], ps_u[:, 0:NROWS_B]).then_inc(cols_ready, 1)
            dve.wait_ge(lam_in, 96)
            dve.tensor_tensor(sq[:], con.lam_cols[:, 0:2], con.lam_cols[:, 2:4], ALU.mult).then_inc(lam_prod, 1)
            dve.wait_ge(cols_ready, 2)
            dve.tensor_scalar(con.cols_b[:, R_DGAIN:R_DGAIN + KD], con.cols_b[:, R_DGAIN:R_DGAIN + KD],
                              1.0 - LAM_INIT, None, ALU.mult).then_inc(lam_done, 1)
            dve.wait_ge(lam_exp, 1)
            dve.scalar_tensor_tensor(out=con.lam[:], in0=esum[:, 0:1], scalar=LAM_INIT, in1=esum[:, 1:2],
                                     op0=ALU.add, op1=ALU.subtract).then_inc(lam_done, 1)


class Slots:

    def __init__(self, al):
        self.raw = [al.sb(f"raw{i}", [P, KD, GC]) for i in range(2)]
        self.landed = [al.sem(f"landed{i}") for i in range(2)]
        self.loads = 0

    def load_ahead(self, sp, load):
        for s in range(2):
            sp.dma_start(self.raw[s][:], load(sp, 0, s)).then_inc(self.landed[s], 16)


def project_block(nc, tag, slots, sections, make, ada=None, following=None, ahead=None):
    with Alloc(nc, tag) as al:
        raw, landed, base = slots.raw, slots.landed, 16 * slots.loads
        whi = [al.sb(f"whi{i}", [P, KD, GC], F32R) for i in range(2)]
        wlo = [al.sb(f"wlo{i}", [P, KD, GC], F32R) for i in range(2)]
        bank = [al.ps(f"bank{i}", [P, 512]) for i in range(4)]
        part_hi, part_lo = al.sem("part_hi"), al.sem("part_lo")
        w_hi, w_lo, units = al.sem("w_hi"), al.sem("w_lo"), al.sem("units")
        freed = [al.sem(f"freed{i}") for i in range(4)]
        al.freed = freed
        empty_vector, empty_scalar = make(al)
        if ada:
            con, A, ada0 = ada
            w_ada = columns(A["w_ada"][0])
            ada_w, acc = al.sb("ada_w", [P, KD, GC]), [al.sb(f"acc{i}", [P, GC]) for i in range(2)]
            ps_ada = al.ps("ps_ada", [P, 512])
            ada_in, acc_step, summed_up, ada_done = map(al.sem, ("ada_in", "acc_step", "summed_up", "ada_done"))
        plan, g0, u0 = [], 0, 0
        for kind, groups, load, operand in sections:
            per = {"T": 2, "T1": 1, "N": 4}[kind]
            plan.append((kind, groups, load, operand, g0, u0, per))
            g0, u0 = g0 + groups, u0 + groups * per
        slots.loads += g0 // 2
        parts = [slice(k, k + 2) for k in range(0, KD, 2)]

        block = al.block()

        @block.sync
        def _(sp):
            for kind, groups, load, operand, gb, ub, per in plan:
                for it in range(groups // 2):
                    for s in range(2):
                        if not (isinstance(it, int) and gb + it == 0):
                            src = load(sp, it, s)
                            wait(sp, w_lo, gb + 2 * it + s - 1)
                            sp.dma_start(raw[s][:], src).then_inc(landed[s], 16)
                        n = gb + 2 * it + s - 1
                        if ada and 0 <= n < plan[0][1]:
                            wait(sp, acc_step, KD * n)
                            col = ada0 * P + n * GC
                            sp.dma_start(ada_w[:], w_ada[:, :, col:col + GC]).then_inc(ada_in, 16)
            if ada and g0 == plan[0][1]:
                sp.wait_ge(acc_step, KD * (g0 - 1))
                col = ada0 * P + (g0 - 1) * GC
                sp.dma_start(ada_w[:], w_ada[:, :, col:col + GC]).then_inc(ada_in, 16)
            if following or ahead:
                sp.wait_ge(w_lo, g0)
            if following:
                slots.load_ahead(sp, following)
            if ahead:
                ahead(sp)

        @block.gpsimd
        def _(pool):
            for kind, groups, load, operand, gb, ub, per in plan:
                for it in pairs(pool, groups // 2, gb == 0):
                    for s in range(2):
                        if isinstance(it, int) and gb + 2 * it + s == 0:
                            continue
                        pool.wait_ge(w_hi, gb + 2 * it + s + 1)
                        pool.tensor_tensor(wlo[s][:], raw[s][:], as_f32(whi[s][:]), ALU.subtract).then_inc(w_lo, 1)

        @block.tensor
        def _(pe):
            for kind, groups, load, operand, gb, ub, per in plan:
                for it in pairs(pe, groups // 2, gb == 0):
                    for s in range(2):
                        very_first = isinstance(it, int) and gb + 2 * it + s == 0
                        if not very_first:
                            pe.wait_ge(w_lo, gb + 2 * it + s + 1)
                        xh, xl = operand(s)
                        for c in range(per):
                            b = (s * per + c) % 4
                            use = (ub + s * per + c) // 4 + it * (2 * per // 4)
                            wait(pe, freed[b], use)
                            for k in range(KD):
                                if very_first and c == 0 and k % 2 == 0:
                                    if k < KD - 2:
                                        pe.wait_ge(part_lo, k // 2 + 1)
                                    else:
                                        pe.wait_ge(w_lo, 1)
                                if kind != "N":
                                    cs = slice(c * P, (c + 1) * P)
                                    ops = ((whi[s][:, k, cs], xh[:, k, :]), (whi[s][:, k, cs], xl[:, k, :]),
                                           (wlo[s][:, k, cs], xh[:, k, :]))
                                    out = bank[b][:]
                                else:
                                    ts = slice(c * P, (c + 1) * P)
                                    ops = ((xh[:, k, ts], whi[s][:, k, :]), (xh[:, k, ts], wlo[s][:, k, :]),
                                           (xl[:, k, ts], whi[s][:, k, :]))
                                    out = bank[b][:, 0:GC]
                                for n, (a, m) in enumerate(ops):
                                    mm = pe.matmul(out, a, m, start=(k == 0 and n == 0), stop=(k == KD - 1 and n == 2))
                            mm.then_inc(units, 1)
                        if ada and gb == 0:
                            pe.wait_ge(acc_step, KD * (2 * it + s + 1))
                            for m in range(2):
                                mm = pe.matmul(ps_ada[:, bass.ds(4 * it + 2 * s + m, 1)],
                                               acc[s][:, m * P:(m + 1) * P], con.ones[:, 0:1], start=True, stop=True)
                            mm.then_inc(summed_up, 1)

        def view(eng):
            for sec, (kind, groups, load, operand, gb, ub, per) in enumerate(plan):
                for it in pairs(eng, groups // 2, True, sec == len(plan) - 1):
                    for s in range(2):
                        first = ub + (2 * it + s) * per
                        last_group = isinstance(it, int) and gb + 2 * it + s + 1 == g0
                        if eng is nc.vector and not last_group:
                            o = 1 - s
                            eng.wait_ge(landed[o], base + 16 * (gb // 2 + it + s + 1))
                            wait(eng, units, first)
                            eng.tensor_copy(whi[o][:], raw[o][:]).then_inc(w_hi, 1)
                        if ada and gb == 0 and eng is nc.vector:
                            n = 2 * it + s
                            eng.wait_ge(ada_in, 16 * (n + 1))
                            wait(eng, summed_up, n - 1)
                            ada_columns(eng, ada_w, con.silu_c, acc[s][:], acc_step, KD * n)
                        for c in range(per):
                            b = (s * per + c) % 4
                            yield sec, it, s, c, first + c, bank[b], freed[b]

        @block.vector
        def _(dve):
            dve.wait_ge(landed[0], base + 16)
            for n, part in enumerate(parts):
                hi_sem, lo_sem = (part_hi, part_lo) if n < len(parts) - 1 else (w_hi, w_lo)
                dve.tensor_copy(whi[0][:, part], raw[0][:, part]).then_inc(hi_sem, 1)
                dve.wait_ge(hi_sem, n + 1 if hi_sem is part_hi else 1)
                dve.tensor_tensor(wlo[0][:, part], raw[0][:, part], as_f32(whi[0][:, part]),
                                  ALU.subtract).then_inc(lo_sem, 1)
            empty_vector(dve, view(dve), units)
            if ada:
                n = 2 * plan[0][1]
                dve.wait_ge(summed_up, plan[0][1])
                dve.tensor_tensor(con.ada[:, ada0:ada0 + n], ps_ada[:, 0:n], con.cols_a[:, ada0:ada0 + n],
                                  ALU.add).then_inc(ada_done, 1)
                if ada0 + n == 6 * KD:
                    dve.wait_ge(ada_done, 1)
                    dve.scalar_tensor_tensor(out=con.scale_b[:], in0=con.ada[:, 32:40], scalar=1.0,
                                             in1=con.cols_a[:, R_GPREFFN:R_GPREFFN + 8], op0=ALU.add, op1=ALU.mult)
                    for dst, gain, gate in ((con.gate_a, R_GPOSTMIX, 16), (con.gate_b, R_GPOSTFFN, 40)):
                        dve.tensor_tensor(dst[:], con.ada[:, gate:gate + 8], con.cols_a[:, gain:gain + 8], ALU.mult)

        @block.scalar
        def _(act):
            empty_scalar(act, view(act), units)


def w_group(w, col0, step=GC):
    v = columns(w)

    def load(sp, it, s):
        return v[:, :, bass.ds(settled(sp, col0 + it * 2 * GC + s * step), GC)]
    return load


def mlstm_inputs_block(nc, con, slots, A, hT, qk, v, out_gate, gates):
    w = A["w_in"][0]

    def make(al):
        acc = [al.sb(f"acc{i}", [P, T]) for i in range(2)]
        conv, silu_done = al.sem("conv"), al.sem("silu_done")

        def vector(dve, units_of, units):
            for sec, it, s, c, u, bank, freed in units_of:
                if sec == 2:
                    continue
                dve.wait_ge(units, u + 1)
                if sec == 0:
                    ch = 4 * it + 2 * s + c
                    wait(dve, silu_done, ch - 1)
                    dve.tensor_scalar(acc[c][:], bank[:], con.cols_b[:, bass.ds(R_CONVW + 48 + ch, 1)],
                                      con.cols_a[:, bass.ds(R_CONVB + ch, 1)], ALU.mult, ALU.add).then_inc(conv, 1)
                    for j in range(1, CONV):
                        dve.wait_ge(conv, 3 * ch + j)
                        op = dve.scalar_tensor_tensor(
                            out=acc[c][:, j:], in0=bank[:, 0:T - j],
                            scalar=con.cols_b[:, bass.ds(R_CONVW + 16 * (3 - j) + ch, 1)],
                            in1=acc[c][:, j:], op0=ALU.mult, op1=ALU.add)
                        op.then_inc(conv if j < 3 else freed, 1)
                elif sec == 1:
                    dve.tensor_copy(v[:, c, bass.ds(2 * it + s, 1), 0:DH],
                                    bank[:, 0:DH].rearrange("p (a d) -> p a d", a=1)).then_inc(freed, 1)
                else:
                    dve.tensor_scalar(gates[:, s], bank[0:HEADS, :], con.gate_bias[:, s:s + 1], None,
                                      ALU.add).then_inc(freed, 1)

        def scalar(act, units_of, units):
            for sec, it, s, c, u, bank, freed in units_of:
                if sec == 0:
                    act.wait_ge(freed, it + 1)
                    act.activation(qk[:, bass.ds(4 * it + 2 * s + c, 1), :], acc[c][:].rearrange("p (a t) -> p a t", a=1),
                                   ACT.Silu).then_inc(silu_done, 1)
                elif sec == 2:
                    act.wait_ge(units, u + 1)
                    act.activation(out_gate[:, bass.ds(4 * it + 2 * s + c, 1), :],
                                   bank[:].rearrange("p (a t) -> p a t", a=1), ACT.Sigmoid).then_inc(freed, 1)
        return vector, scalar

    op = lambda s: hT
    project_block(nc, "proj_m", slots, [("T", 8, w_group(w, C_QK), op), ("N", 4, w_group(w, C_MV), op),
                                 ("T", 4, w_group(w, C_MO), op), ("T1", 2, w_group(w, C_IF, HEADS), op)], make,
                  following=branch_load(A, C_GM, "w_br_m"))


def mlstm_block(nc, con, qk, v, out_gate, gates, y_hi, y_lo):
    H = HEADS
    steps = [(h, i) for h in range(H) for i in range(NT)]
    N, LATE = len(steps), 5

    def behind(n, delay):
        n -= delay
        return [steps[n][0]] if 0 <= n < N and steps[n][1] == NT - 1 else []

    with Alloc(nc, "mlstm") as al:
        lf, fsum, a, g, ones4 = [al.sb(n, [H, T]) for n in ("lf", "fsum", "a", "g", "ones4")]
        absf = expf = logf = lf
        nm = fsum
        a_col, floor = al.sb("a_col", [P, NT, H]), al.sb("floor", [P, NT, H])
        ex = [al.sb(f"ex{i}", [P, T]) for i in range(2)]
        ee = [al.sb(f"ee{i}", [P, T]) for i in range(2)]
        pt = [al.sb(f"pt{i}", [P, T]) for i in range(2)]
        pos, den, rden = al.sb("pos", [P, NT]), al.sb("den", [P, NT]), al.sb("rden", [P, NT])
        cell, y, junk = al.sb("cell", [P, NT, DH]), al.sb("y", [P, NT, DH]), al.sb("junk", [P, DH])
        ss, ms, rstd = al.sb("ss", [P, NT]), al.sb("ms", [P, NT]), al.sb("rstd", [P, NT])
        tmp = al.sb("tmp", [P, 2, T])
        ps_g, ps_t = al.ps("ps_g", [P, T]), al.ps("ps_t", [P, T])
        ps_s = [al.ps(f"ps_s{i}", [P, T]) for i in range(2)]
        ps_n = [al.ps(f"ps_n{i}", [P, T]) for i in range(NT)]
        (act_pre, dve_pre, ones_done, cols_t, col_done, floor_done, gb_done, ex_done, ee_done, mask_done, s_done,
         pt_done, pv_done, den_done, cell_done, ss_done, ms_done, pow_done, y_done, tr_done, tmp_done, hi_done,
         lo_done) = map(al.sem, (
             "act_pre", "dve_pre", "ones_done", "cols_t", "col_done", "floor_done", "gb_done", "ex_done", "ee_done",
             "mask_done", "s_done", "pt_done", "pv_done", "den_done", "cell_done", "ss_done", "ms_done", "pow_done",
             "y_done", "tr_done", "tmp_done", "hi_done", "lo_done"))
        block = al.block()

        @block.scalar
        def _(act):
            act.activation(absf[:], gates[:, 1], ACT.Abs).then_inc(act_pre, 1)
            act.wait_ge(act_pre, 1)
            act.activation(expf[:], absf[:], ACT.Exp, scale=-1.0).then_inc(act_pre, 1)
            act.wait_ge(act_pre, 2)
            act.activation(logf[:], expf[:], ACT.Ln, bias=1.0).then_inc(act_pre, 1)
            act.wait_ge(col_done, 1)
            act.activation(floor[:], ps_t[:, NT * H:2 * NT * H].rearrange("p (t h) -> p t h", h=H),
                           ACT.Exp).then_inc(floor_done, 1)
            for n in range(N + LATE):
                if n < N:
                    w = T - steps[n][1] * P
                    act.wait_ge(ex_done, n + 1)
                    wait(act, pt_done, n - 1)
                    act.activation(ee[n % 2][:, 0:w], ex[n % 2][:, 0:w], ACT.Exp, scale=-1.0).then_inc(ee_done, 1)
                for h in behind(n, 1):
                    for j in range(NT):
                        act.wait_ge(cell_done, NT * h + j + 1)
                        wait(act, ss_done, NT * h + j)
                        act.activation(junk[:], cell[:, j], ACT.Square, accum_out=ss[:, j:j + 1]).then_inc(ss_done, 1)
                for c in range(2):
                    for h in behind(n, 4 + c):
                        act.wait_ge(tmp_done, 2 * h + c + 1)
                        act.activation(y_hi[:, 2 * h + c], tmp[:, c], ACT.Copy).then_inc(hi_done, 1)

        @block.gpsimd
        def _(pool):
            pool.memset(ones4[:], 1.0).then_inc(ones_done, 1)
            pool.memset(v[:, :, :, DH:DH + 1], 1.0).then_inc(ones_done, 1)
            for n in range(N + LATE):
                if n < N:
                    pool.wait_ge(ee_done, n + 1)
                    pool.affine_select(out=ee[n % 2][:, 0:P], in_=ee[n % 2][:, 0:P], compare_op=ALU.is_ge, fill=0.0,
                                       base=0, pattern=[[1, P]], channel_multiplier=-1).then_inc(mask_done, 1)
                for h in behind(n, 1):
                    pool.wait_ge(ms_done, h + 1)
                    pool.tensor_tensor(rstd[:], ms[:], con.pow_half[:, 0:NT], ALU.pow).then_inc(pow_done, 1)

        @block.tensor
        def _(pe):
            pe.wait_ge(dve_pre, 5)
            for t in range(NT):
                pe.transpose(ps_t[:, t * H:(t + 1) * H], a[:, t * P:(t + 1) * P], con.ident[0:H, 0:H])
            for t in range(NT):
                mm = pe.transpose(ps_t[:, (NT + t) * H:(NT + t + 1) * H], nm[:, t * P:(t + 1) * P],
                                  con.ident[0:H, 0:H])
            mm.then_inc(cols_t, 1)

            def scores(n):
                h, i = steps[n]
                if i == 0:
                    wait(pe, ex_done, n)
                    pe.matmul(ps_g[:], con.sel[:, h, :], g[:], start=True, stop=True).then_inc(gb_done, 1)
                wait(pe, pt_done, n - 1)
                for k in range(2):
                    mm = pe.matmul(ps_s[n % 2][:, 0:T - i * P], qk[:, 8 + 2 * h + k, i * P:(i + 1) * P],
                                   qk[:, 2 * h + k, i * P:T], start=(k == 0), stop=(k == 1))
                mm.then_inc(s_done, 1)

            scores(0)
            pe.wait_ge(ones_done, 2)
            for n in range(N + LATE):
                if n + 1 < N:
                    scores(n + 1)
                if n < N:
                    h, i = steps[n]
                    pe.wait_ge(pt_done, n + 1)
                    if i == 0:
                        wait(pe, cell_done, NT * h)
                    for j in range(i, NT):
                        mm = pe.matmul(ps_n[j][:, 0:DH + 1], pt[n % 2][:, (j - i) * P:(j - i + 1) * P], v[:, i, h, :],
                                       start=(i == 0), stop=(i == j))
                    mm.then_inc(pv_done, 1)
                for c in range(2):
                    for h in behind(n, 2 + c):
                        pe.wait_ge(y_done, NT * (h + 1))
                        wait(pe, tmp_done, 2 * h + c)
                        if h == 0 and c == 0:
                            pe.wait_ge(col_done, 1)
                            pe.wait_ge(floor_done, 1)
                        for j in range(NT):
                            mm = pe.transpose(ps_t[:, j * P:(j + 1) * P], y[:, j, c * P:(c + 1) * P], con.ident[:])
                        mm.then_inc(tr_done, 1)

        @block.vector
        def _(dve):
            dve.wait_ge(act_pre, 3)
            dve.scalar_tensor_tensor(out=lf[:], in0=gates[:, 1], scalar=0.0, in1=logf[:], op0=ALU.min,
                                     op1=ALU.subtract).then_inc(dve_pre, 1)
            dve.wait_ge(ones_done, 1)
            dve.wait_ge(dve_pre, 1)
            dve.tensor_tensor_scan(fsum[:], ones4[:], lf[:], 0.0, ALU.mult, ALU.add).then_inc(dve_pre, 1)
            dve.wait_ge(dve_pre, 2)
            dve.tensor_tensor(a[:], gates[:, 0], fsum[:], ALU.subtract).then_inc(dve_pre, 1)
            dve.wait_ge(dve_pre, 3)
            dve.tensor_tensor_scan(g[:], a[:], a[:], 0.0, ALU.max, ALU.max).then_inc(dve_pre, 1)
            dve.wait_ge(dve_pre, 4)
            dve.scalar_tensor_tensor(out=nm[:], in0=fsum[:], scalar=-1.0, in1=g[:], op0=ALU.mult,
                                     op1=ALU.subtract).then_inc(dve_pre, 1)
            dve.wait_ge(cols_t, 1)
            dve.tensor_copy(a_col[:], ps_t[:, 0:NT * H].rearrange("p (t h) -> p t h", h=H)).then_inc(col_done, 1)
            dve.wait_ge(col_done, 1)

            def exponents(n):
                h, i = steps[n]
                w = T - i * P
                dve.wait_ge(gb_done, h + 1)
                wait(dve, ee_done, n - 1)
                dve.tensor_scalar(ex[n % 2][:, 0:w], ps_g[:, i * P:T], a_col[:, i, h:h + 1], 0.0, ALU.subtract,
                                  ALU.max).then_inc(ex_done, 1)

            def weights(n):
                w = T - steps[n][1] * P
                dve.wait_ge(s_done, n + 1)
                dve.wait_ge(mask_done, n + 1)
                wait(dve, pv_done, n - 1)
                dve.scalar_tensor_tensor(out=pt[n % 2][:, 0:w], in0=ps_s[n % 2][:, 0:w], scalar=DH ** -0.5,
                                         in1=ee[n % 2][:, 0:w], op0=ALU.mult, op1=ALU.mult).then_inc(pt_done, 1)

            def cells(h):
                dve.wait_ge(floor_done, 1)
                dve.wait_ge(pv_done, NT * (h + 1))
                for j in range(NT):
                    dve.tensor_tensor(pos[:, j:j + 1], ps_n[j][:, DH:DH + 1], floor[:, j, h:h + 1],
                                      ALU.max).then_inc(den_done, 1)
                dve.wait_ge(den_done, 9 * h + 4)
                for j in range(NT):
                    dve.scalar_tensor_tensor(out=den[:, j:j + 1], in0=ps_n[j][:, DH:DH + 1], scalar=-1.0,
                                             in1=pos[:, j:j + 1], op0=ALU.mult, op1=ALU.max).then_inc(den_done, 1)
                dve.wait_ge(den_done, 9 * h + 8)
                dve.reciprocal(rden[:], den[:]).then_inc(den_done, 1)
                dve.wait_ge(den_done, 9 * h + 9)
                wait(dve, y_done, NT * h)
                for j in range(NT):
                    dve.tensor_scalar(cell[:, j], ps_n[j][:, 0:DH], rden[:, j:j + 1], None,
                                      ALU.mult).then_inc(cell_done, 1)

            exponents(0)
            for n in range(N + LATE):
                if n + 1 < N:
                    exponents(n + 1)
                if n < N:
                    weights(n)
                for h in behind(n, 1):
                    dve.wait_ge(ss_done, NT * (h + 1))
                    dve.tensor_scalar(ms[:], ss[:], 1.0 / DH, EPS, ALU.mult, ALU.add).then_inc(ms_done, 1)
                    dve.wait_ge(pow_done, h + 1)
                    wait(dve, tr_done, 2 * h)
                    for j in range(NT):
                        dve.tensor_scalar(y[:, j], cell[:, j], rstd[:, j:j + 1], None, ALU.mult).then_inc(y_done, 1)
                for c in range(2):
                    for h in behind(n, 3 + c):
                        dve.wait_ge(tr_done, 2 * h + c + 1)
                        wait(dve, lo_done, 2 * (h - 1) + c + 1)
                        dve.scalar_tensor_tensor(out=tmp[:, c], in0=ps_t[:],
                                                 scalar=con.cols_b[:, R_MGAIN + 2 * h + c:R_MGAIN + 2 * h + c + 1],
                                                 in1=out_gate[:, 2 * h + c], op0=ALU.mult,
                                                 op1=ALU.mult).then_inc(tmp_done, 1)
                for h in behind(n, LATE):
                    for c in range(2):
                        dve.wait_ge(hi_done, 2 * h + c + 1)
                        dve.tensor_tensor(y_lo[:, 2 * h + c], tmp[:, c], as_f32(y_hi[:, 2 * h + c]),
                                          ALU.subtract).then_inc(lo_done, 1)
                for h in behind(n, 0):
                    cells(h)


def branch_load(A, gate_col, name):
    branch, gates = columns(A[name][0]), columns(A["w_in"][0])

    def load(sp, it, s):
        return branch[:, :, bass.ds(it * GC, GC)] if s else gates[:, :, bass.ds(gate_col + it * GC, GC)]
    return load


def gated_branch_block(nc, tag, slots, load, hT, y, merged, following, m_hl=None, ada=None):
    def make(al):
        freed_bank = lambda b: al.freed[b]
        sg = [al.sb(f"sg{i}", [P, T]) for i in range(2)]
        prod = [al.sb(f"prod{i}", [P, T]) for i in range(2)]
        added, m_hi_done = al.sem("added"), al.sem("m_hi_done")
        m_lo_done = al.sem("m_lo_done")
        freed_by = {}

        def vector(dve, units_of, units):
            for sec, it, s, c, u, bank, freed in units_of:
                freed_by[s, c] = freed
                if s == 0:
                    continue
                ch = 2 * it + c
                dve.wait_ge(units, u + 1)
                dve.wait_ge(freed_by[0, c], it + 1)
                out = merged[:, bass.ds(ch, 1), :]
                sg3 = sg[c][:].rearrange("p (a t) -> p a t", a=1)
                bank3 = bank[:].rearrange("p (a t) -> p a t", a=1)
                if m_hl is None:
                    dve.tensor_tensor(out, bank3, sg3, ALU.mult).then_inc(freed, 1)
                else:
                    p3 = prod[c][:].rearrange("p (a t) -> p a t", a=1)
                    wait(dve, m_lo_done, ch - 1)
                    dve.tensor_tensor(p3, bank3, sg3, ALU.mult).then_inc(freed, 1)
                    dve.wait_ge(freed, it + 1)
                    dve.tensor_tensor(p3, p3, out, ALU.add).then_inc(added, 1)
                    dve.wait_ge(added, ch + 1)
                    hi3, lo3 = m_hl[0][:, bass.ds(ch, 1), :], m_hl[1][:, bass.ds(ch, 1), :]
                    dve.tensor_copy(hi3, p3).then_inc(m_hi_done, 1)
                    dve.wait_ge(m_hi_done, ch + 1)
                    dve.tensor_tensor(lo3, p3, as_f32(hi3), ALU.subtract).then_inc(m_lo_done, 1)

        def scalar(act, units_of, units):
            seen = {}
            for sec, it, s, c, u, bank, freed in units_of:
                if s:
                    continue
                act.wait_ge(units, u + 1)
                wait(act, freed_bank(2 + c), it)
                act.activation(sg[c][:], bank[:], ACT.Sigmoid).then_inc(freed, 1)
        return vector, scalar

    project_block(nc, tag, slots, [("T", 8, load, lambda s: y if s else hT)], make, ada, following)


def attention_inputs_block(nc, con, slots, A, hT, qk, v):
    w = A["w_in"][0]

    def make(al):
        def vector(dve, units_of, units):
            for sec, it, s, c, u, bank, freed in units_of:
                if sec == 1:
                    dve.wait_ge(units, u + 1)
                    dve.tensor_copy(v[:, c, bass.ds(2 * it + s, 1), 0:DH],
                                    bank[:, 0:DH].rearrange("p (a d) -> p a d", a=1)).then_inc(freed, 1)

        def scalar(act, units_of, units):
            for sec, it, s, c, u, bank, freed in units_of:
                if sec == 0:
                    act.wait_ge(units, u + 1)
                    act.activation(qk[:, bass.ds(4 * it + 2 * s + c, 1), :],
                                   bank[:].rearrange("p (a t) -> p a t", a=1), ACT.Copy).then_inc(freed, 1)
        return vector, scalar

    op = lambda s: hT
    project_block(nc, "proj_d", slots, [("T", 8, w_group(w, C_DQ), op), ("N", 4, w_group(w, C_DV), op)], make,
                  (con, A, 32), branch_load(A, C_GD, "w_br_d"))


def attention_block(nc, con, qk, v, y_hi, y_lo):
    scale = DQK ** -0.5
    steps = [(h, j) for h in range(HEADS) for j in range(NT)]
    N = len(steps)

    def ended(n):
        return [(steps[n - 1 - c][0], c) for c in range(2) if 0 <= n - 1 - c < N and steps[n - 1 - c][1] == NT - 1]

    with Alloc(nc, "attn") as al:
        p = [[al.sb(f"p{i}{c}", [P, T]) for c in range(2)] for i in range(2)]
        mx, nb, sm, rs = [[al.sb(f"{n}{i}", [P, 2]) for i in range(2)] for n in ("mx", "nb", "sm", "rs")]
        p1w, aw, awt = al.sb("p1w", [P, T]), al.sb("aw", [P, T]), al.sb("awt", [P, T])
        y = [al.sb(f"y{i}", [P, NT, DH]) for i in range(2)]
        junk = al.sb("junk", [P, DH])
        ss, ms, rstd = [[al.sb(f"{n}{i}", [P, 1]) for i in range(2)] for n in ("ss", "ms", "rstd")]
        ps_s = [[al.ps(f"ps_s{i}{c}", [P, T]) for c in range(2)] for i in range(2)]
        ps_t, ps_y = al.ps("ps_t", [P, T]), al.ps("ps_y", [P, T])
        ps_o = [al.ps(f"ps_o{i}", [P, T]) for i in range(2)]
        (s_done, masked, max_done, nb_done, p_done, rs_done, w_done, p1_done, a_done, at_done, awt_done, o_done,
         ss_done, ms_done, pow_done, y_done, tr_done, hi_done, lo_done) = map(al.sem, (
             "s_done", "masked", "max_done", "nb_done", "p_done", "rs_done", "w_done", "p1_done", "a_done", "at_done",
             "awt_done", "o_done", "ss_done", "ms_done", "pow_done", "y_done", "tr_done", "hi_done", "lo_done"))
        block = al.block()

        @block.tensor
        def _(pe):
            def scores(n):
                h, j = steps[n]
                wait(pe, p_done, 2 * (n - 1))
                for c in range(2):
                    pe.matmul(ps_s[n % 2][c][:, 0:(j + 1) * P], qk[:, 2 * h + c, j * P:(j + 1) * P],
                              qk[:, 8 + 2 * h + c, 0:(j + 1) * P], start=True, stop=True).then_inc(s_done, 1)

            def output(n):
                h, j = steps[n]
                pe.wait_ge(a_done, n + 1)
                wait(pe, awt_done, n)
                for i in range(j + 1):
                    mm = pe.transpose(ps_t[:, i * P:(i + 1) * P], aw[:, i * P:(i + 1) * P], con.ident[:])
                mm.then_inc(at_done, 1)
                wait(pe, y_done, n - 1)
                pe.wait_ge(awt_done, n + 1)
                for i in range(j + 1):
                    mm = pe.matmul(ps_o[n % 2][:, 0:DH], awt[:, i * P:(i + 1) * P], v[:, i, h, 0:DH],
                                   start=(i == 0), stop=(i == j))
                mm.then_inc(o_done, 1)

            scores(0)
            for n in range(N + 3):
                if n + 1 < N:
                    scores(n + 1)
                if 1 <= n <= N:
                    output(n - 1)
                for h, c in ended(n - 1):
                    pe.wait_ge(y_done, NT * (h + 1))
                    wait(pe, lo_done, 2 * h + c)
                    for t in range(NT):
                        mm = pe.transpose(ps_y[:, t * P:(t + 1) * P], y[h % 2][:, t, c * P:(c + 1) * P], con.ident[:])
                    mm.then_inc(tr_done, 1)

        @block.scalar
        def _(act):
            def norm(n):
                w = (steps[n][1] + 1) * P
                act.wait_ge(at_done, n + 1)
                wait(act, o_done, n)
                act.activation(awt[:, 0:w], ps_t[:, 0:w], ACT.Copy).then_inc(awt_done, 1)
                act.wait_ge(o_done, n + 1)
                wait(act, ss_done, n)
                wait(act, ms_done, n - 1)
                act.activation(junk[:], ps_o[n % 2][:, 0:DH], ACT.Square, accum_out=ss[n % 2][:]).then_inc(ss_done, 1)

            for n in range(N + 3):
                if n < N:
                    w = (steps[n][1] + 1) * P
                    act.wait_ge(nb_done, n + 1)
                    wait(act, a_done, n - 1)
                    for c in range(2):
                        act.activation(p[n % 2][c][:, 0:w], ps_s[n % 2][c][:, 0:w], ACT.Exp,
                                       bias=nb[n % 2][:, c:c + 1], scale=scale,
                                       accum_out=sm[n % 2][:, c:c + 1]).then_inc(p_done, 1)
                if 1 <= n <= N:
                    norm(n - 1)
                for h, c in ended(n - 1):
                    act.wait_ge(tr_done, 2 * h + c + 1)
                    gain = con.cols_b[:, R_DGAIN + 2 * h + c:R_DGAIN + 2 * h + c + 1]
                    act.activation(y_hi[:, 2 * h + c], ps_y[:], ACT.Copy, scale=gain).then_inc(hi_done, 1)

        @block.gpsimd
        def _(pool):
            for n in range(N):
                pool.wait_ge(ms_done, n + 1)
                wait(pool, y_done, n - 1)
                pool.tensor_tensor(rstd[n % 2][:], ms[n % 2][:], con.pow_half[:, 0:1], ALU.pow).then_inc(pow_done, 1)

        @block.vector
        def _(dve):
            def maxima(n):
                w = (steps[n][1] + 1) * P
                dve.wait_ge(s_done, 2 * n + 2)
                for c in range(2):
                    dve.memset(ps_s[n % 2][c][0:CHUNK, w - CHUNK:w], NEG).then_inc(masked, 1)
                dve.wait_ge(masked, 2 * n + 2)
                for c in range(2):
                    dve.tensor_reduce(mx[n % 2][:, c:c + 1], ps_s[n % 2][c][:, 0:w], AX_X, ALU.max).then_inc(max_done, 1)
                dve.wait_ge(max_done, 2 * n + 2)
                wait(dve, p_done, 2 * (n - 1))
                dve.tensor_scalar(nb[n % 2][:], mx[n % 2][:], -scale, None, ALU.mult).then_inc(nb_done, 1)

            def weights(n):
                w = (steps[n][1] + 1) * P
                dve.wait_ge(p_done, 2 * n + 2)
                dve.reciprocal(rs[n % 2][:], sm[n % 2][:]).then_inc(rs_done, 1)
                dve.wait_ge(rs_done, n + 1)
                dve.tensor_tensor(rs[n % 2][:, 1:2], rs[n % 2][:, 1:2], con.lam[:], ALU.mult).then_inc(w_done, 1)
                dve.wait_ge(w_done, n + 1)
                dve.tensor_scalar(p1w[:, 0:w], p[n % 2][1][:, 0:w], rs[n % 2][:, 1:2], None, ALU.mult).then_inc(p1_done, 1)
                dve.wait_ge(p1_done, n + 1)
                wait(dve, at_done, n)
                dve.scalar_tensor_tensor(out=aw[:, 0:w], in0=p[n % 2][0][:, 0:w], scalar=rs[n % 2][:, 0:1],
                                         in1=p1w[:, 0:w], op0=ALU.mult, op1=ALU.subtract).then_inc(a_done, 1)

            def mean(n):
                dve.wait_ge(ss_done, n + 1)
                wait(dve, pow_done, n - 1)
                dve.tensor_scalar(ms[n % 2][:], ss[n % 2][:], 1.0 / DH, EPS, ALU.mult, ALU.add).then_inc(ms_done, 1)

            def norm(n):
                h, j = steps[n]
                dve.wait_ge(pow_done, n + 1)
                wait(dve, tr_done, 2 * (h - 1))
                dve.tensor_scalar(y[h % 2][:, j], ps_o[n % 2][:, 0:DH], rstd[n % 2][:], None,
                                  ALU.mult).then_inc(y_done, 1)

            maxima(0)
            for n in range(N + 3):
                if 2 <= n <= N + 1:
                    mean(n - 2)
                if n + 1 < N:
                    maxima(n + 1)
                if 2 <= n <= N + 1:
                    norm(n - 2)
                if n < N:
                    weights(n)
                for h, c in ended(n - 1):
                    dve.wait_ge(hi_done, 2 * h + c + 1)
                    gain = con.cols_b[:, R_DGAIN + 2 * h + c:R_DGAIN + 2 * h + c + 1]
                    dve.scalar_tensor_tensor(out=y_lo[:, 2 * h + c], in0=ps_y[:], scalar=gain,
                                             in1=as_f32(y_hi[:, 2 * h + c]), op0=ALU.mult,
                                             op1=ALU.subtract).then_inc(lo_done, 1)


def out_block(nc, slots, A, m_hl, y):
    def make(al):
        def vector(dve, units_of, units):
            for sec, it, s, c, u, bank, freed in units_of:
                if c % 2 == 0:
                    dve.wait_ge(units, u + 1)
                    dve.tensor_copy(y[:, c, bass.ds((2 * it + s) * GC, GC)], bank[:, 0:GC]).then_inc(freed, 1)

        def scalar(act, units_of, units):
            for sec, it, s, c, u, bank, freed in units_of:
                if c % 2:
                    act.wait_ge(units, u + 1)
                    act.activation(y[:, c, bass.ds((2 * it + s) * GC, GC)], bank[:, 0:GC], ACT.Copy).then_inc(freed, 1)
        return vector, scalar

    project_block(nc, "proj_o", slots, [("N", 4, w_group(A["w_out"][0], 0), lambda s: m_hl)], make)


def middle_block(nc, con, x_src, y, x1, hi, lo, slots, following):
    with Alloc(nc, "mid") as al:
        x = al.sb("x", [P, NT, D])
        row_a = al.sb("row_a", [P, D])
        diag = [al.sb(f"diag{i}", [P, P]) for i in range(2)]
        junk = al.sb("junk", [P, D])
        ss, ms, rstd = [[al.sb(f"{n}{i}", [P, NT]) for i in range(2)] for n in ("ss", "ms", "rstd")]
        yg = [al.sb(f"yg{i}", [P, D]) for i in range(2)]
        xn = y
        h = al.sb("h", [P, HBUF, T])
        ps = [al.ps(f"ps{i}", [P, P]) for i in range(2)]
        ps_h = [al.ps(f"ps_h{i}", [P, T]) for i in range(4)]
        x_in = [al.sem(f"x_in{i}") for i in range(NT)]
        (diag_done, spread, row_done, ss_done, ms_done, pow_done, yg_done, sum_done, stored, normed, turned, modded,
         hi_done, even_lo, odd_lo) = map(al.sem, (
             "diag_done", "spread", "row_done", "ss_done", "ms_done", "pow_done", "yg_done", "sum_done", "stored",
             "normed", "turned", "modded", "hi_done", "even_lo", "odd_lo"))
        block = al.block()

        @block.sync
        def _(sp):
            for t in range(NT):
                sp.dma_start(x[:, t], x_src[t * P:(t + 1) * P, :]).then_inc(x_in[t], 16)
            slots.load_ahead(sp, following)
            for t in range(NT):
                sp.wait_ge(sum_done, t + 1)
                sp.dma_start(x1[t * P:(t + 1) * P, :], x[:, t]).then_inc(stored, 16)
            sp.wait_ge(stored, 16 * NT)

        @block.scalar
        def _(act):
            def square(src, n, t):
                wait(act, ss_done, NT * n + t)
                act.activation(junk[:], src[:, t], ACT.Square, accum_out=ss[n][:, t:t + 1]).then_inc(ss_done, 1)

            def keep_row(row, k):
                act.wait_ge(spread, k + 1)
                act.activation(row[:, k % KD * P:(k % KD + 1) * P], ps[k % 2][:], ACT.Copy).then_inc(row_done, 1)

            for t in range(NT):
                square(y, 0, t)
                keep_row(row_a, 2 * t)
                keep_row(row_a, 2 * t + 1)
            for t in range(NT):
                act.wait_ge(sum_done, t + 1)
                square(x, 1, t)
            for k in range(KD):
                keep_row(con.row_b, KD + k)
            for k in range(KD):
                act.wait_ge(turned, k + 1)
                if k >= HBUF:
                    act.wait_ge(odd_lo if k % 2 else even_lo, (k - HBUF) // 2 + 1)
                act.activation(h[:, k % HBUF], ps_h[k % 4][:], ACT.Identity, bias=con.ada[:, 24 + k:25 + k],
                               scale=con.scale_b[:, k:k + 1]).then_inc(modded, 1)

        @block.gpsimd
        def _(pool):
            for n in range(2):
                pool.wait_ge(ms_done, n + 1)
                pool.tensor_tensor(rstd[n][:], ms[n][:], con.pow_half[:, 0:NT], ALU.pow).then_inc(pow_done, 1)
            for k in range(1, KD, 2):
                pool.wait_ge(hi_done, k + 1)
                pool.tensor_tensor(lo[:, k], h[:, k % HBUF], as_f32(hi[:, k]), ALU.subtract).then_inc(odd_lo, 1)

        @block.tensor
        def _(pe):
            for k in range(2 * KD):
                pe.wait_ge(diag_done, k + 1)
                wait(pe, row_done, k - 1)
                pe.matmul(ps[k % 2][:], con.ones[:], diag[k % 2][:], start=True, stop=True).then_inc(spread, 1)
            pe.wait_ge(normed, NT)
            for k in range(KD):
                wait(pe, modded, k - 3)
                for t in range(NT):
                    mm = pe.transpose(ps_h[k % 4][:, t * P:(t + 1) * P], xn[:, t, k * P:(k + 1) * P], con.ident[:])
                mm.then_inc(turned, 1)

        @block.vector
        def _(dve):
            def diagonal(col, k):
                wait(dve, spread, k - 1)
                dve.tensor_scalar(diag[k % 2][:], con.ident[:], col[:, k % KD:k % KD + 1], None,
                                  ALU.mult).then_inc(diag_done, 1)

            for k in range(KD):
                diagonal(con.gate_a, k)
            dve.wait_ge(ss_done, NT)
            dve.tensor_scalar(ms[0][:], ss[0][:], 1.0 / D, EPS, ALU.mult, ALU.add).then_inc(ms_done, 1)
            dve.wait_ge(pow_done, 1)
            dve.wait_ge(row_done, KD)
            for t in range(NT):
                dve.wait_ge(x_in[t], 16)
                wait(dve, sum_done, t - 1)
                dve.scalar_tensor_tensor(out=yg[t % 2][:], in0=y[:, t], scalar=rstd[0][:, t:t + 1], in1=row_a[:],
                                         op0=ALU.mult, op1=ALU.mult).then_inc(yg_done, 1)
                dve.wait_ge(yg_done, t + 1)
                dve.tensor_tensor(x[:, t], x[:, t], yg[t % 2][:], ALU.add).then_inc(sum_done, 1)
            for k in range(2):
                diagonal(con.gate_b, KD + k)
            dve.wait_ge(ss_done, 2 * NT)
            dve.tensor_scalar(ms[1][:], ss[1][:], 1.0 / D, EPS, ALU.mult, ALU.add).then_inc(ms_done, 1)
            for k in range(2, KD):
                diagonal(con.gate_b, KD + k)
            dve.wait_ge(pow_done, 2)
            for t in range(NT):
                dve.tensor_scalar(xn[:, t], x[:, t], rstd[1][:, t:t + 1], None, ALU.mult).then_inc(normed, 1)
            for k in range(KD):
                dve.wait_ge(modded, k + 1)
                dve.tensor_copy(hi[:, k], h[:, k % HBUF]).then_inc(hi_done, 1)
                if k % 2 == 0:
                    dve.wait_ge(hi_done, k + 1)
                    dve.tensor_tensor(lo[:, k], h[:, k % HBUF], as_f32(hi[:, k]), ALU.subtract).then_inc(even_lo, 1)


class Consts:

    def __init__(self, al):
        self.ident, self.ones = al.sb("ident", [P, P]), al.sb("ones", [P, P])
        self.iota, self.pow_half = al.sb("iota", [P, P]), al.sb("pow_half", [P, 8])
        self.sel = al.sb("sel", [HEADS, HEADS, P])
        self.cols_a, self.cols_b = al.sb("cols_a", [P, NROWS_A]), al.sb("cols_b", [P, NROWS_B])
        self.silu_c, self.ada = al.sb("silu_c", [P, KD]), al.sb("ada", [P, 48])
        self.lam_cols, self.lam = al.sb("lam_cols", [P, 4]), al.sb("lam", [P, 1])
        self.gate_bias = al.sb("gate_bias", [HEADS, 2])
        self.scale_a, self.scale_b = al.sb("scale_a", [P, KD]), al.sb("scale_b", [P, KD])
        self.row_b = al.sb("row_b", [P, D])
        self.gate_a, self.gate_b = al.sb("gate_a", [P, KD]), al.sb("gate_b", [P, KD])


def mixer(nc, con, slots, A, hT, x1):
    x = A["x"].rearrange("b s d -> (b s) d")
    with Alloc(nc, "mix") as al:
        merged = al.sb("merged", [P, KD, T])
        y_hl = al.sb("y_hi", [P, KD, T], F32R), al.sb("y_lo", [P, KD, T], F32R)
        with Alloc(nc, "in") as ai:
            qk, v = ai.sb("qk", [P, 2 * KD, T]), ai.sb("v", [P, NT, HEADS, DH + 1])
            with Alloc(nc, "gate") as ag:
                out_gate, gates = merged, ag.sb("gates", [HEADS, 2, T])
                mlstm_inputs_block(nc, con, slots, A, hT, qk, v, out_gate, gates)
                mlstm_block(nc, con, qk, v, out_gate, gates, *y_hl)
            gated_branch_block(nc, "branch_m", slots, branch_load(A, C_GM, "w_br_m"), hT, y_hl, merged,
                               w_group(A["w_in"][0], C_DQ), ada=(con, A, 16))
            attention_inputs_block(nc, con, slots, A, hT, qk, v)
            attention_block(nc, con, qk, v, *y_hl)
        with Alloc(nc, "mhl") as am:
            m_hl = am.sb("m_hi", [P, KD, T], F32R), am.sb("m_lo", [P, KD, T], F32R)
            gated_branch_block(nc, "branch_d", slots, branch_load(A, C_GD, "w_br_d"), hT, y_hl, merged,
                               w_group(A["w_out"][0], 0), m_hl)
            y = am.sb("y", [P, NT, D])
            out_block(nc, slots, A, m_hl, y)
            recycle_semaphores(nc, slots.landed)
            middle_block(nc, con, x, y, x1, *hT, slots, w_group(A["w_query"][0], 0))


class Ring:

    def __init__(self, al, slots):
        self.tile = [slots.raw[i // 2][:, (i % 2) * KD // 2:(i % 2 + 1) * KD // 2, :].rearrange("p k n -> p (k n)")
                     for i in range(U_RING)]
        self.u_in, self.v_in, self.ag_in = [[al.sem(f"{n}{i}") for i in range(U_RING)] for n in ("u_in", "v_in", "ag_in")]

    def load_u(self, sp, A, s, n):
        sp.dma_start(self.tile[s], A["expert_u"][0][bass.ds(n * P, P), :]).then_inc(self.u_in[s], 16)


U_RING, R_STEPS, G_STEPS, G_TOK = 4, 12, 16, 8
NEXP = NK


def query_block(nc, slots, ring, A, hT, qry, keys, keys_in):
    def ahead(sp):
        for i in range(2):
            half = A["sub_keys"][0][i * PH // 2:(i + 1) * PH // 2]
            sp.dma_start(keys[i][:], half.rearrange("h c n d -> n (h c) d")).then_inc(keys_in, 16)
        for s in range(U_RING):
            ring.load_u(sp, A, s, s)

    def make(al):
        def vector(dve, units_of, units):
            for sec, it, s, c, u, bank, freed in units_of:
                pass

        def scalar(act, units_of, units):
            for sec, it, s, c, u, bank, freed in units_of:
                act.wait_ge(units, u + 1)
                act.activation(qry[:, bass.ds(4 * it + 2 * s + c, 1), :],
                               bank[:].rearrange("p (a t) -> p a t", a=1), ACT.Copy).then_inc(freed, 1)
        return vector, scalar

    project_block(nc, "query", slots, [("T", 8, w_group(A["w_query"][0], 0), lambda s: hT)], make, ahead=ahead)


def scores_block(nc, con, qry, keys, keys_in, sc, stored, scores):
    HC = PH * HALVES
    with Alloc(nc, "scores") as al:
        keys_t = al.sb("keys_t", [P, HC, NK])
        ps = [al.ps(f"ps{i}", [P, 4, P]) for i in range(4)]
        turned, kept, scored, copied = map(al.sem, ("turned", "kept", "scored", "copied"))
        block = al.block()

        @block.sync
        def _(sp):
            for t in range(NT):
                sp.wait_ge(copied, 4 * (t + 1))
                sp.dma_start(scores[t * P:(t + 1) * P, :], sc[t].rearrange("p a n -> p (a n)")).then_inc(stored, 16)

        @block.tensor
        def _(pe):
            pe.wait_ge(keys_in, 32)
            for q in range(4):
                for m in range(4):
                    mm = pe.transpose(ps[q][:, m, :], keys[q // 2][:, 4 * (q % 2) + m, :], con.ident[:])
                mm.then_inc(turned, 1)
            for t in range(NT):
                for q in range(4):
                    pe.wait_ge(kept, 4)
                    wait(pe, copied, 4 * (t - 1) + q + 1)
                    for m in range(4):
                        mm = pe.matmul(ps[q][:, m, :], qry[:, 4 * q + m, t * P:(t + 1) * P], keys_t[:, 4 * q + m, :],
                                       start=True, stop=True)
                    mm.then_inc(scored, 1)

        @block.vector
        def _(dve):
            for q in range(4):
                dve.wait_ge(turned, q + 1)
                dve.tensor_copy(keys_t[:, 4 * q:4 * q + 4, :], ps[q][:]).then_inc(kept, 1)

        @block.scalar
        def _(act):
            for t in range(NT):
                for q in range(4):
                    act.wait_ge(scored, 4 * t + q + 1)
                    act.activation(sc[t][:, 4 * q:4 * q + 4, :], ps[q][:], ACT.Copy).then_inc(copied, 1)


def experts_in_block(nc, con, ring, hot, stage, scores_stored, A, hT, scores, acts, gmat):
    HC = PH * HALVES
    u = A["expert_u"][0]
    with Alloc(nc, "xin") as al:
        raw, landed = ring.tile, ring.u_in
        uhi = [al.sb(f"uhi{i}", [P, KD, P], F32R) for i in range(2)]
        ulo = [al.sb(f"ulo{i}", [P, KD, P], F32R) for i in range(2)]
        act_t = [al.sb(f"act{i}", [P, T]) for i in range(4)]
        sc, sc2 = al.sb("sc", [P, HC, NK]), al.sb("sc2", [P, HC, NK])
        top, ix, ixf = al.sb("top", [P, HC, TOPK]), al.sb("ix", [P, HC, TOPK], U32), al.sb("ixf", [P, HC, TOPK])
        best, bpos = al.sb("best", [P, PH, TOPK]), al.sb("bpos", [P, PH, TOPK], U32)
        au, bu = al.sb("au", [P, PH, TOPK], U32), al.sb("bu", [P, PH, TOPK], U32)
        rank = [al.sb(f"rank{c}", [P, PH, TOPK]) for c in range(2)]
        pick = [al.sb(f"pick{c}", [P, PH * TOPK, TOPK]) for c in range(2)]
        key = [al.sb(f"key{c}", [P, PH * TOPK]) for c in range(2)]
        eg, ge, gate = [al.sb(n, [P, PH, TOPK]) for n in ("eg", "ge", "gate")]
        gsum, ginv = al.sb("gsum", [P, PH]), al.sb("ginv", [P, PH])
        slot = [al.sb(f"slot{n}", [P, T]) for n in range(3)]
        hot_j, hot_i = hot[0:2], hot[2:4]
        ps_t = [al.ps(f"ps_t{i}", [P, KD, P]) for i in range(2)]
        ps_u = [al.ps(f"ps_u{i}", [P, T]) for i in range(2)]
        ps_g = [al.ps(f"ps_g{i}", [P, 4, NK]) for i in range(2)]
        kept = [al.sem(f"kept{i}") for i in range(4)]
        flushed = [al.sem(f"flushed{i}") for i in range(2)]
        (t_done, hi_done, lo_done, u_done, gelu_done, sc_in, chosen, exp_done, sub_done, pool_step, keys_done,
         slots_t, slots_done, hot_done, g_done, staged, sum_inv, is_rank) = map(al.sem, (
             "t_done", "hi_done", "lo_done", "u_done", "gelu_done", "sc_in", "chosen", "exp_done", "sub_done",
             "pool_step", "keys_done", "slots_t", "slots_done", "hot_done", "g_done", "staged", "sum_inv", "is_rank"))
        block = al.block()
        n_r = NT * R_STEPS
        n_m = 4
        n_g = T // G_TOK
        n_g0 = n_r + n_m
        n_tail = NEXP - n_g0 - n_g
        assert n_tail > 0 and n_tail % 4 == 0
        cand = sc[:].rearrange("p (h c) k -> p h (c k)", c=2)
        cand2 = sc2[:].rearrange("p (h c) k -> p h (c k)", c=2)
        STAGES = 16

        @block.sync
        def _(sp):
            def every(n, s, more, args):
                early = isinstance(n, int) and n < 4
                row = settled(sp, n * P)
                arow = settled(sp, (n - 4) * P) if not early else 0
                if not early:
                    sp.wait_ge(t_done, n - 3)
                    sp.dma_start(raw[s % U_RING], u[bass.ds(row, P), :]).then_inc(landed[s % U_RING], 16)
                    sp.wait_ge(gelu_done, n - 3)
                    sp.dma_start(acts[bass.ds(arow, P), :], act_t[s % 4][:]).then_inc(kept[s % 4], 16)
                if more:
                    more(*args)

            def route(tt, s):
                if s == 0:
                    trow = settled(sp, tt * P)
                    if isinstance(tt, int) and tt == 0:
                        sp.wait_ge(scores_stored, 16 * NT)
                    wait(sp, chosen, STAGES * (tt - 1) + 13)
                    sp.dma_start(sc[:].rearrange("p a k -> p (a k)"), scores[bass.ds(trow, P), :]).then_inc(sc_in, 16)

            def gates(gi, q):
                if q >= 12:
                    flush(gi, 0, q - 12)
                if 4 <= q < 8 and not (isinstance(gi, int) and gi == 0):
                    flush(gi - 1, 1, q - 4)

            def flush(gi, h, part):
                tok = settled(sp, gi * (G_STEPS * G_TOK) + h * 8 * G_TOK)
                rows = slice(part * NK // 4, (part + 1) * NK // 4)
                sp.wait_ge(staged, 2 * (G_STEPS * gi + 8 * h + 8))
                sp.dma_start(gmat.rearrange("(i j) t -> j i t", j=NK)[:, rows, bass.ds(tok, 8 * G_TOK)],
                             stage[h][:, rows, :]).then_inc(flushed[h], 16)

            for tt in pairs(sp, NT, True):
                for s in range(R_STEPS):
                    every(R_STEPS * tt + s, s, route, (tt, s))
            for s in range(n_m):
                every(n_r + s, s, None, None)
            for gi in pairs(sp, n_g // G_STEPS, True):
                for q in range(G_STEPS):
                    every(n_g0 + G_STEPS * gi + q, q, gates, (gi, q))
            for it in range(n_tail // 4):
                for s in range(4):
                    every(n_g0 + n_g + 4 * it + s, s, None, None)
                    if it == 1:
                        flush(n_g // G_STEPS - 1, 1, s)
            sp.wait_ge(g_done, 2 * n_g)
            for h in range(2):
                sp.wait_ge(flushed[h], 64 * (n_g // G_STEPS))
            for n in range(NEXP, NEXP + 4):
                m, rows = n - NEXP, slice((n - NEXP) * P, (n - NEXP + 1) * P)
                sp.wait_ge(t_done, n - 3)
                sp.dma_start(raw[m], A["expert_v"][0][rows, :]).then_inc(ring.v_in[m], 16)
                sp.wait_ge(kept[m], 16)
                sp.dma_start(act_of(hot[m]), acts[rows, :]).then_inc(ring.ag_in[m], 16)
                sp.dma_start(g_of(hot[m]), gmat[rows, :]).then_inc(ring.ag_in[m], 16)
                sp.wait_ge(gelu_done, n - 3)
                sp.dma_start(acts[(n - 4) * P:(n - 3) * P, :], act_t[n % 4][:]).then_inc(kept[n % 4], 16)
            for i in range(4):
                sp.wait_ge(kept[i], 16 * NEXP // 4)

        @block.tensor
        def _(pe):
            def turn(n, s):
                pe.wait_ge(landed[s % U_RING], 16 * (n // U_RING + 1) if isinstance(n, int) else lap(n, s))
                wait(pe, lo_done, n - 1)
                for k in range(KD):
                    mm = pe.transpose(ps_t[s % 2][:, k, :], raw[s % U_RING][:, k * P:(k + 1) * P], con.ident[:])
                mm.then_inc(t_done, 1)

            laps = {}

            def lap(n, s):
                return laps["value"]

            def every(n, s, more, args, last=False, base=None, it=None, per=None):
                if not last:
                    if base is not None:
                        laps["value"] = 16 * ((base + s + 1) // U_RING + 1) + 16 * (per // U_RING) * it
                    turn(n + 1, s + 1)
                pe.wait_ge(lo_done, n + 1)
                wait(pe, gelu_done, n - 1)
                i = 0
                for k in range(KD):
                    for a, m in ((uhi, hT[0]), (uhi, hT[1]), (ulo, hT[0])):
                        mm = pe.matmul(ps_u[s % 2][:], a[s % 2][:, k, :], m[:, k, :], start=(i == 0),
                                       stop=(i == 3 * KD - 1))
                        i += 1
                mm.then_inc(u_done, 1)
                if more:
                    more(*args)

            def turn_slots(tt):
                pe.wait_ge(keys_done, 2 * tt + 2)
                pe.wait_ge(chosen, STAGES * (tt + 1))
                wait(pe, slots_done, tt)
                for i, src in enumerate((key[0][:], key[1][:], gate[:].rearrange("p h k -> p (h k)"))):
                    mm = pe.transpose(ps_g[0][:, i, :], src, con.ident[:])
                mm.then_inc(slots_t, 1)

            def route(tt, s):
                if s == 6 and not (isinstance(tt, int) and tt == 0):
                    turn_slots(tt - 1)

            def gates(gi, q):
                m = G_STEPS * gi + q
                pe.wait_ge(hot_done, m + 1)
                for b in range(2):
                    wait(pe, staged, 2 * m + b - 1)
                    for k in range(4):
                        mm = pe.matmul(ps_g[b][:, k, :], hot_j[q % 2][:, 4 * b + k, :], hot_i[q % 2][:, 4 * b + k, :],
                                       start=True, stop=True)
                    mm.then_inc(g_done, 1)

            pe.wait_ge(landed[0], 16)
            turn(0, 0)
            for tt in pairs(pe, NT, True):
                for s in range(R_STEPS):
                    every(R_STEPS * tt + s, s, route, (tt, s), base=0, it=tt, per=R_STEPS)
            for s in range(n_m):
                every(n_r + s, s, None, None)
            turn_slots(NT - 1)
            pe.wait_ge(slots_done, NT)
            for gi in pairs(pe, n_g // G_STEPS, True):
                for q in range(G_STEPS):
                    every(n_g0 + G_STEPS * gi + q, q, gates, (gi, q), base=n_g0, it=gi, per=G_STEPS)
            for it in pairs(pe, n_tail // 4, False, True):
                for s in range(4):
                    n = n_g0 + n_g + 4 * it + s
                    every(n, s, None, None, last=isinstance(n, int) and n == NEXP - 1, base=n_g0 + n_g, it=it, per=4)

        @block.scalar
        def _(act):
            def cut(n, s):
                act.wait_ge(t_done, n + 1)
                wait(act, u_done, n - 1)
                act.activation(uhi[s % 2][:], ps_t[s % 2][:], ACT.Copy).then_inc(hi_done, 1)

            def every(n, s, more, args, last=False, laps=None):
                if not last:
                    cut(n + 1, s + 1)
                act.wait_ge(u_done, n + 1)
                if laps is None or not (isinstance(laps, int) and laps <= 0):
                    wait(act, kept[s % 4], laps)
                act.activation(act_t[s % 4][:], ps_u[s % 2][:], ACT.Gelu).then_inc(gelu_done, 1)
                if more:
                    more(*args)

            def route(tt, s):
                if s == R_STEPS - 1:
                    act.wait_ge(sub_done, tt + 1)
                    act.activation(ge[:], eg[:], ACT.Exp).then_inc(exp_done, 1)

            def gates(gi, q):
                m = G_STEPS * gi + q
                for b in range(2):
                    act.wait_ge(g_done, 2 * m + b + 1)
                    if q % 8 == 0 and b == 0 and not (isinstance(gi, int) and gi == 0):
                        act.wait_ge(flushed[q // 8], 64 * gi)
                    t0 = (q % 8) * G_TOK + 4 * b
                    act.activation(stage[q // 8][:, :, t0:t0 + 4], ps_g[b][:].rearrange("p t i -> p i t"),
                                   ACT.Copy).then_inc(staged, 1)

            cut(0, 0)
            for tt in pairs(act, NT, True):
                for s in range(R_STEPS):
                    every(R_STEPS * tt + s, s, route, (tt, s), laps=16 * (s // 4) + 16 * (R_STEPS // 4) * tt)
            for s in range(n_m):
                every(n_r + s, s, None, None, laps=16 * ((n_r + s) // 4))
            for gi in pairs(act, n_g // G_STEPS, True):
                for q in range(G_STEPS):
                    every(n_g0 + G_STEPS * gi + q, q, gates, (gi, q), laps=16 * ((n_g0 + q) // 4) + 16 * (G_STEPS // 4) * gi)
            for it in pairs(act, n_tail // 4, False, True):
                for s in range(4):
                    n = n_g0 + n_g + 4 * it + s
                    every(n, s, None, None, last=isinstance(n, int) and n == NEXP - 1,
                          laps=16 * ((n_g0 + n_g) // 4) + 16 * it)

        @block.gpsimd
        def _(pool):
            step = [0]

            def chain(op):
                op.then_inc(pool_step, 1)
                step[0] += 1
                return step[0]

            per_tile = 2 * 4
            for tt in pairs(pool, NT, True):
                step[0] = 0
                wait(pool, slots_t, tt)
                for c in range(HALVES):
                    base = per_tile * tt
                    pool.wait_ge(is_rank, 2 * tt + c + 1)
                    p4 = pick[c][:].rearrange("p (h k) a -> p h k a", h=PH)
                    nums = ixf[:].rearrange("p (h c) k -> p h c k", c=2)[:, :, c, :].unsqueeze(2).to_broadcast(
                        [P, PH, TOPK, TOPK])
                    chain(pool.tensor_tensor(p4, p4, nums, ALU.mult))
                    for w in (8, 4, 2):
                        pool.wait_ge(pool_step, base + step[0])
                        chain(pool.tensor_tensor(pick[c][:, :, 0:w], pick[c][:, :, 0:w], pick[c][:, :, w:2 * w],
                                                 ALU.add))
                    pool.wait_ge(pool_step, base + step[0])
                    pool.tensor_tensor(key[c][:].unsqueeze(2), pick[c][:, :, 0:1], pick[c][:, :, 1:2],
                                       ALU.add).then_inc(keys_done, 1)

        @block.vector
        def _(dve):
            def cut(n, s):
                dve.wait_ge(hi_done, n + 1)
                dve.tensor_tensor(ulo[s % 2][:], ps_t[s % 2][:], as_f32(uhi[s % 2][:]), ALU.subtract).then_inc(lo_done, 1)

            def every(n, s, more, args, last=False):
                if more is gates:
                    more(*args)
                if not last:
                    cut(n + 1, s + 1)
                if more is route:
                    more(*args)

            def at(tt, k):
                dve.wait_ge(chosen, STAGES * tt + k)

            def top8(out, src, tt, k, count):
                for x in range(count):
                    op = dve.max(out=out(x), in_=src(x))
                op.then_inc(chosen, 1)
                at(tt, k)

            def where(out, vals, src, tt, k, count):
                for x in range(count):
                    op = dve.max_index(out=out(x), in_max=vals(x), in_values=src(x))
                op.then_inc(chosen, 1)
                at(tt, k)

            def strike(out, vals, src, tt, k, count):
                for x in range(count):
                    op = dve.match_replace(out=out(x), in_to_replace=vals(x), in_values=src(x), imm_value=NEG)
                op.then_inc(chosen, 1)
                at(tt, k)

            lo8, hi8 = slice(0, 8), slice(8, 16)
            s_of, s2_of = (lambda x: sc[:, x, :]), (lambda x: sc2[:, x, :])
            c_of, c2_of = (lambda x: cand[:, x, :]), (lambda x: cand2[:, x, :])

            def route(tt, s):
                first = isinstance(tt, int) and tt == 0
                if s == 0:
                    if not first:
                        dve.wait_ge(exp_done, tt)
                    dve.wait_ge(sc_in, 16 * (tt + 1))
                    dve.memset(gsum[:], 0.0)
                    top8(lambda x: top[:, x, lo8], s_of, tt, 1, HC)
                elif s == 1:
                    where(lambda x: ix[:, x, lo8], lambda x: top[:, x, lo8], s_of, tt, 2, HC)
                elif s == 2:
                    strike(s2_of, lambda x: top[:, x, lo8], s_of, tt, 3, HC)
                elif s == 3:
                    top8(lambda x: top[:, x, hi8], s2_of, tt, 4, HC)
                elif s == 4:
                    where(lambda x: ix[:, x, hi8], lambda x: top[:, x, hi8], s2_of, tt, 5, HC)
                elif s == 5:
                    if not first:
                        dve.wait_ge(keys_done, 2 * tt)
                    dve.tensor_copy(ixf[:], ix[:]).then_inc(chosen, 1)
                    at(tt, 6)
                    t4 = top[:].rearrange("p (h c) k -> p h c k", c=2)
                    shape = [P, PH, TOPK, TOPK]
                    dve.tensor_tensor(cand.rearrange("p h (a b) -> p h a b", b=TOPK),
                                      t4[:, :, 0, :].unsqueeze(3).to_broadcast(shape),
                                      t4[:, :, 1, :].unsqueeze(2).to_broadcast(shape), ALU.add).then_inc(chosen, 1)
                    at(tt, 7)
                elif s == 6:
                    if not first:
                        copy_slots(tt - 1)
                    top8(lambda x: best[:, x, lo8], c_of, tt, 8, PH)
                elif s == 7:
                    where(lambda x: bpos[:, x, lo8], lambda x: best[:, x, lo8], c_of, tt, 9, PH)
                elif s == 8:
                    strike(c2_of, lambda x: best[:, x, lo8], c_of, tt, 10, PH)
                elif s == 9:
                    top8(lambda x: best[:, x, hi8], c2_of, tt, 11, PH)
                elif s == 10:
                    where(lambda x: bpos[:, x, hi8], lambda x: best[:, x, hi8], c2_of, tt, 12, PH)
                    dve.tensor_single_scalar(au[:], bpos[:], 4, ALU.logical_shift_right)
                    dve.tensor_single_scalar(bu[:], bpos[:], 15, ALU.bitwise_and).then_inc(chosen, 1)
                    at(tt, 13)
                    dve.tensor_copy(rank[0][:], au[:])
                    dve.tensor_copy(rank[1][:], bu[:]).then_inc(chosen, 1)
                else:
                    opts = con.iota[:, 0:TOPK].unsqueeze(1).to_broadcast([P, PH * TOPK, TOPK])
                    dve.tensor_tensor(eg[:], best[:], best[:, :, 0:1].to_broadcast([P, PH, TOPK]),
                                      ALU.subtract).then_inc(sub_done, 1)
                    at(tt, 14)
                    for c in range(HALVES):
                        mine = rank[c][:].rearrange("p h k -> p (h k)").unsqueeze(2).to_broadcast(
                            [P, PH * TOPK, TOPK])
                        dve.tensor_tensor(pick[c][:], mine, opts, ALU.is_equal).then_inc(is_rank, 1)
                    dve.wait_ge(exp_done, tt + 1)
                    dve.tensor_reduce(gsum[:], ge[:], AX_X, ALU.add).then_inc(chosen, 1)
                    at(tt, 15)
                    dve.reciprocal(ginv[:], gsum[:]).then_inc(sum_inv, 1)
                    dve.wait_ge(sum_inv, tt + 1)
                    dve.tensor_tensor(gate[:], ge[:], ginv[:].unsqueeze(2).to_broadcast([P, PH, TOPK]),
                                      ALU.mult).then_inc(chosen, 1)

            def copy_slots(tt):
                dve.wait_ge(slots_t, tt + 1)
                for i in range(3):
                    op = dve.tensor_copy(slot[i][:, bass.ds(tt * P, P)], ps_g[0][:, i, :])
                op.then_inc(slots_done, 1)

            def gates(gi, q):
                m = G_STEPS * gi + q
                wait(dve, g_done, 2 * (m - 1))
                for k in range(G_TOK):
                    tok = gi * (G_STEPS * G_TOK) + q * G_TOK + k
                    i_s, j_s, g_s = [slot[x][:, bass.ds(tok, 1)] for x in range(3)]
                    dve.tensor_scalar(hot_j[q % 2][:, k, :], con.iota[:], j_s, None, ALU.is_equal)
                    op = dve.tensor_scalar(hot_i[q % 2][:, k, :], con.iota[:], i_s, g_s, ALU.is_equal, ALU.mult)
                op.then_inc(hot_done, 1)

            cut(0, 0)
            for tt in pairs(dve, NT, True):
                for s in range(R_STEPS):
                    every(R_STEPS * tt + s, s, route, (tt, s))
            for s in range(n_m):
                every(n_r + s, s, None, None)
            copy_slots(NT - 1)
            dve.wait_ge(slots_done, NT)
            for gi in pairs(dve, n_g // G_STEPS, True):
                for q in range(G_STEPS):
                    every(n_g0 + G_STEPS * gi + q, q, gates, (gi, q))
            for it in pairs(dve, n_tail // 4, False, True):
                for s in range(4):
                    n = n_g0 + n_g + 4 * it + s
                    every(n, s, None, None, last=isinstance(n, int) and n == NEXP - 1)


def act_of(slot):
    return slot[:, 0:T // NK, :].rearrange("p a n -> p (a n)")


def g_of(slot):
    return slot[:, T // NK:2 * T // NK, :].rearrange("p a n -> p (a n)")


def experts_out_block(nc, con, ring, hot, A, acts, gmat, x1, dst):
    vexp = A["expert_v"][0]
    RING = U_RING
    with Alloc(nc, "xout") as al:
        v, a, g = ring.tile, [act_of(x) for x in hot], [g_of(x) for x in hot]
        vhi, vlo = [[al.sb(f"{n}{i}", [P, D], F32R) for i in range(2)] for n in ("vhi", "vlo")]
        wt = [al.sb(f"wt{i}", [P, T]) for i in range(2)]
        whi, wlo = [[al.sb(f"{n}{i}", [P, T], F32R) for i in range(2)] for n in ("whi", "wlo")]
        out = [[al.ps(f"out{t}{h}", [P, T]) for h in range(2)] for t in range(NT)]
        v_in, ag_in = ring.v_in, ring.ag_in
        x, junk = al.sb("x", [P, NT, D]), al.sb("junk", [P, T])
        yg = [al.sb(f"yg{i}", [P, T]) for i in range(4)]
        ss, ssum, ms, rstd = [al.sb(n, [P, 2 * NT if n == "ss" else NT]) for n in ("ss", "ssum", "ms", "rstd")]
        (vhi_done, vlo_done, wt_done, whi_done, wlo_done, used, x_in, ss_done, chain, pow_done, yg_done, dve_sum,
         pool_sum, stored) = map(al.sem, (
             "vhi_done", "vlo_done", "wt_done", "whi_done", "wlo_done", "used", "x_in", "ss_done", "chain",
             "pow_done", "yg_done", "dve_sum", "pool_sum", "stored"))
        block = al.block()

        def steps(eng):
            for it in pairs(eng, NEXP // RING, True, True):
                for s in range(RING):
                    yield RING * it + s, s, it

        @block.sync
        def _(sp):
            for n, s, it in steps(sp):
                if isinstance(it, int) and it == 0:
                    continue
                row = settled(sp, n * P)
                wait(sp, vlo_done, n - 3)
                sp.dma_start(v[s], vexp[bass.ds(row, P), :]).then_inc(v_in[s], 16)
                wait(sp, wt_done, n - 3)
                sp.dma_start(a[s], acts[bass.ds(row, P), :]).then_inc(ag_in[s], 16)
                sp.dma_start(g[s], gmat[bass.ds(row, P), :]).then_inc(ag_in[s], 16)
            for t in range(NT):
                sp.dma_start(x[:, t], x1[t * P:(t + 1) * P, :]).then_inc(x_in, 16)
            for t in range(NT):
                sp.wait_ge(dve_sum, t + 1)
                sp.wait_ge(pool_sum, t + 1)
                sp.dma_start(dst[t * P:(t + 1) * P, :], x[:, t]).then_inc(stored, 16)
            sp.wait_ge(stored, 16 * NT)

        @block.scalar
        def _(act):
            for n, s, it in steps(act):
                act.wait_ge(v_in[s], 16 * (it + 1))
                wait(act, used, n - 1)
                act.activation(vhi[s % 2][:], v[s], ACT.Copy).then_inc(vhi_done, 1)
                act.wait_ge(wt_done, n + 1)
                act.activation(whi[s % 2][:], wt[s % 2][:], ACT.Copy).then_inc(whi_done, 1)
            act.wait_ge(used, NEXP)
            for m in range(2 * NT):
                wait(act, ss_done, m)
                act.activation(junk[:], out[m // 2][m % 2][:], ACT.Square, accum_out=ss[:, m:m + 1]).then_inc(ss_done, 1)

        @block.gpsimd
        def _(pool):
            for n, s, it in steps(pool):
                pool.wait_ge(vhi_done, n + 1)
                pool.tensor_tensor(vlo[s % 2][:], v[s], as_f32(vhi[s % 2][:]), ALU.subtract).then_inc(vlo_done, 1)
            pool.wait_ge(chain, 2)
            pool.tensor_tensor(rstd[:], ms[:], con.pow_half[:, 0:NT], ALU.pow).then_inc(pow_done, 1)
            pool.wait_ge(x_in, 16 * NT)
            for t in range(NT):
                m = 2 * t + 1
                pool.wait_ge(yg_done, m + 1)
                pool.tensor_tensor(x[:, t, T:D], x[:, t, T:D], yg[m % 4][:], ALU.add).then_inc(pool_sum, 1)

        @block.vector
        def _(dve):
            for n, s, it in steps(dve):
                dve.wait_ge(ag_in[s], 32 * (it + 1))
                wait(dve, wlo_done, n - 1)
                dve.tensor_tensor(wt[s % 2][:], a[s], g[s], ALU.mult).then_inc(wt_done, 1)
                dve.wait_ge(whi_done, n + 1)
                dve.tensor_tensor(wlo[s % 2][:], wt[s % 2][:], as_f32(whi[s % 2][:]), ALU.subtract).then_inc(wlo_done, 1)
            dve.wait_ge(ss_done, 2 * NT)
            ss3 = ss[:].rearrange("p (t h) -> p t h", h=2)
            dve.tensor_tensor(ssum[:].unsqueeze(2), ss3[:, :, 0:1], ss3[:, :, 1:2], ALU.add).then_inc(chain, 1)
            dve.wait_ge(chain, 1)
            dve.tensor_scalar(ms[:], ssum[:], 1.0 / D, EPS, ALU.mult, ALU.add).then_inc(chain, 1)
            dve.wait_ge(pow_done, 1)
            dve.wait_ge(x_in, 16 * NT)
            for m in range(2 * NT):
                t, half = m // 2, slice(m % 2 * T, (m % 2 + 1) * T)
                if m % 2:
                    wait(dve, pool_sum, t - 1)
                dve.scalar_tensor_tensor(out=yg[m % 4][:], in0=out[t][m % 2][:], scalar=rstd[:, t:t + 1],
                                         in1=con.row_b[:, half], op0=ALU.mult, op1=ALU.mult).then_inc(yg_done, 1)
                if m % 2 == 0:
                    dve.wait_ge(yg_done, m + 1)
                    dve.tensor_tensor(x[:, t, half], x[:, t, half], yg[m % 4][:], ALU.add).then_inc(dve_sum, 1)

        @block.tensor
        def _(pe):
            for n, s, it in steps(pe):
                first, last = isinstance(n, int) and n == 0, isinstance(n, int) and n == NEXP - 1
                pe.wait_ge(vlo_done, n + 1)
                pe.wait_ge(wlo_done, n + 1)
                for t in range(NT):
                    ts = slice(t * P, (t + 1) * P)
                    for i, (w, m) in enumerate(((whi, vhi), (whi, vlo), (wlo, vhi))):
                        for h in range(2):
                            mm = pe.matmul(out[t][h][:], w[s % 2][:, ts], m[s % 2][:, h * T:(h + 1) * T],
                                           start=(first and i == 0), stop=(last and i == 2))
                mm.then_inc(used, 1)


def experts(nc, con, slots, ring, A, hT, x1, scores, acts, gmat, out):
    with Alloc(nc, "experts") as al:
        hot = [al.sb(f"hot{i}", [P, G_TOK, NK]) for i in range(4)]
        with Alloc(nc, "in") as ai:
            stage = [ai.sb(f"stage{i}", [P, NK, 8 * G_TOK]) for i in range(2)]
            HC = PH * HALVES
            sc = [stage[t // 2][:].rearrange("p a b -> p (a b)")[:, t % 2 * HC * NK:(t % 2 + 1) * HC * NK].rearrange(
                "p (a n) -> p a n", n=NK) for t in range(NT)]
            scores_stored = ai.sem("scores_stored")
            with Alloc(nc, "qry") as aq:
                qry, keys, keys_in = aq.sb("qry", [P, HC, T]), hot[0:2], aq.sem("keys_in")
                query_block(nc, slots, ring, A, hT, qry, keys, keys_in)
                scores_block(nc, con, qry, keys, keys_in, sc, scores_stored, scores)
            experts_in_block(nc, con, ring, hot, stage, scores_stored, A, hT, scores, acts, gmat)
        experts_out_block(nc, con, ring, hot, A, acts, gmat, x1, out)


def build_program(nc, A, out):
    Alloc.sems = []
    x1 = nc.dram_tensor("x1_scratch", (T, D), F32, kind="Internal").ap()
    scores = nc.dram_tensor("scores_scratch", (T, PH * HALVES * NK), F32, kind="Internal").ap()
    acts = nc.dram_tensor("act_scratch", (NK * NK, T), F32, kind="Internal").ap()
    gmat = nc.dram_tensor("gate_scratch", (NK * NK, T), F32, kind="Internal").ap()
    with Alloc(nc, "con") as al:
        con = Consts(al)
        hT = al.sb("h_hi", [P, KD, T], F32R), al.sb("h_lo", [P, KD, T], F32R)
        slots = Slots(al)
        head_block(nc, con, slots, A, A["x"].rearrange("b s d -> (b s) d"), *hT)
        mixer(nc, con, slots, A, hT, x1)
        ring = Ring(al, slots)
        experts(nc, con, slots, ring, A, hT, x1, scores, acts, gmat, out.rearrange("b s d -> (b s) d"))


NAMES = ["x", "c", "w_ada", "b_ada", "g_pre_mix", "g_post_mix", "g_pre_ffn", "g_post_ffn", "w_in", "b_if", "conv_w",
         "conv_b", "m_head_gain", "lam_q1", "lam_k1", "lam_q2", "lam_k2", "d_head_gain", "w_br_m", "w_br_d", "w_out",
         "w_query", "sub_keys", "expert_u", "expert_v"]


def kernel(**inputs):
    import concourse.bacc as bacc
    from concourse.bass_utils import run_bass_kernel_spmd

    nc = bacc.Bacc("TRN2", target_bir_lowering=False, num_devices=1)
    arrays, views = {}, {}
    for name in NAMES:
        a = np.ascontiguousarray(inputs[name])
        arrays[f"in_{name}"] = a
        views[name] = nc.dram_tensor(f"in_{name}", a.shape, mybir.dt.from_np(a.dtype), kind="ExternalInput").ap()
    out = nc.dram_tensor("out", inputs["x"].shape, F32, kind="ExternalOutput").ap()
    build_program(nc, views, out)
    result = run_bass_kernel_spmd(nc, [arrays], core_ids=[0])
    return result.results[0]["out"]
```
